# Optimizing a Trainium2 kernel written in Bass

```python
import jax, jax.numpy as jnp
from jax import lax
import numpy as np

D_MODEL = 2048
BATCH = 1
SEQ = 256
DEPTH = 2

N_MIXERS = 2
HEAD_DIM = 128
MIX_WIDTH = D_MODEL
N_MEM_HEADS = 4
N_MIX_HEADS = (MIX_WIDTH - N_MEM_HEADS * HEAD_DIM) // HEAD_DIM
N_KV_GROUPS = 2
HEADS_PER_GROUP = N_MIX_HEADS // N_KV_GROUPS
N_MEM = 256
Q_BLOCK = 128
CMP_LEN = 32
CMP_STRIDE = 16
CMP_HIDDEN = 2 * HEAD_DIM
SEL_BLOCK = 64
N_SEL = 16
WINDOW = 512
N_BRANCH = 3
D_FF = 5632
CONV_WIDTH = 3
ROPE_THETA = 10000.0
NORM_EPS = 1e-6
SB_COLS = 3 * N_MIX_HEADS * HEAD_DIM + N_MEM_HEADS * HEAD_DIM
NSA_COLS = (N_MIX_HEADS * HEAD_DIM + 6 * N_KV_GROUPS * HEAD_DIM
            + N_BRANCH * N_MIX_HEADS + N_MEM_HEADS * HEAD_DIM)

kernel_name = "hybrid_stickbreak_nsa_memory_convffn"

def rmsnorm(x, g):
    xf = x.astype(jnp.float32)
    y = xf * lax.rsqrt(jnp.mean(xf * xf, axis=-1, keepdims=True) + NORM_EPS)
    return (y * g.astype(jnp.float32)).astype(x.dtype)

def rope_tables(positions):
    inv_freq = jnp.power(ROPE_THETA, -jnp.arange(0, HEAD_DIM, 2, dtype=jnp.float32) / HEAD_DIM)
    ang = positions.astype(jnp.float32)[..., None] * inv_freq
    return jnp.cos(ang)[:, :, None, :], jnp.sin(ang)[:, :, None, :]

def apply_rope(u, cos, sin):
    uf = u.astype(jnp.float32)
    u1, u2 = uf[..., :HEAD_DIM // 2], uf[..., HEAD_DIM // 2:]
    return jnp.concatenate([u1 * cos - u2 * sin, u2 * cos + u1 * sin], axis=-1).astype(u.dtype)

def masked_softmax(s, mask):
    s = jnp.where(mask, s, -jnp.inf)
    m = jnp.max(s, axis=-1, keepdims=True)
    m = jnp.where(jnp.isfinite(m), m, 0.0)
    e = jnp.exp(s - m)
    return e / jnp.maximum(jnp.sum(e, axis=-1, keepdims=True), 1e-30)

def split_cols(a, sizes):
    outs, start = [], 0
    for n in sizes:
        outs.append(a[..., start:start + n])
        start += n
    return outs

def stick_breaking_attention(q, k, v):
    B, S, H, Dh = q.shape
    scale = Dh ** -0.5
    outs = []
    for blk in range(S // Q_BLOCK):
        end = (blk + 1) * Q_BLOCK
        qb = q[:, blk * Q_BLOCK:end]
        kp, vp = k[:, :end], v[:, :end]
        z = jnp.einsum('bthd,bshd->bhts', qb, kp).astype(jnp.float32) * scale
        t_pos = blk * Q_BLOCK + jnp.arange(Q_BLOCK)
        mask = jnp.arange(end)[None, :] < t_pos[:, None]
        log_keep = jnp.where(mask, jax.nn.log_sigmoid(-z), 0.0)
        log_keep_between = lax.cumsum(log_keep, axis=3, reverse=True) - log_keep
        a = jnp.where(mask, jnp.exp(jax.nn.log_sigmoid(z) + log_keep_between), 0.0)
        outs.append(jnp.einsum('bhts,bshd->bthd', a.astype(v.dtype), vp))
    return jnp.concatenate(outs, axis=1)

def stick_breaking_mixer(h, w_in):
    B, S, _ = h.shape
    q, k, v, q_mem = split_cols(h @ w_in, [N_MIX_HEADS * HEAD_DIM] * 3 + [N_MEM_HEADS * HEAD_DIM])
    shp = (B, S, N_MIX_HEADS, HEAD_DIM)
    o = stick_breaking_attention(q.reshape(shp), k.reshape(shp), v.reshape(shp))
    return o.reshape(B, S, N_MIX_HEADS * HEAD_DIM), q_mem

def compress(u, pe, w1, w2):
    B, S, G, Dh = u.shape
    ch = u.reshape(B, S // CMP_STRIDE, CMP_STRIDE, G, Dh)
    blk = jnp.concatenate([ch[:, :-1], ch[:, 1:]], axis=2) + pe[:, None, :]
    nc = blk.shape[1]
    flat = blk.transpose(0, 1, 3, 2, 4).reshape(B, nc, G, CMP_LEN * Dh)
    return jax.nn.silu(flat @ w1) @ w2

def overlap_matrix(nc, ns):
    c0 = jnp.arange(nc)[:, None] * CMP_STRIDE
    s0 = jnp.arange(ns)[None, :] * SEL_BLOCK
    ov = jnp.minimum(c0 + CMP_LEN, s0 + SEL_BLOCK) - jnp.maximum(c0, s0)
    return jnp.maximum(ov, 0).astype(jnp.float32) / CMP_STRIDE

def nsa_mixer(h, w_in, pe, w1, w2, cos, sin):
    B, S, _ = h.shape
    G, HPG, Dh = N_KV_GROUPS, HEADS_PER_GROUP, HEAD_DIM
    kvw = G * Dh
    q, kc, vc, ks, vs, kw, vw, g_logit, q_mem = split_cols(
        h @ w_in, [N_MIX_HEADS * Dh] + [kvw] * 6 + [N_BRANCH * N_MIX_HEADS, N_MEM_HEADS * Dh])
    q = apply_rope(q.reshape(B, S, N_MIX_HEADS, Dh), cos, sin)
    kc = apply_rope(kc.reshape(B, S, G, Dh), cos, sin)
    ks = apply_rope(ks.reshape(B, S, G, Dh), cos, sin)
    kw = apply_rope(kw.reshape(B, S, G, Dh), cos, sin)
    vc, vs, vw = (u.reshape(B, S, G, Dh) for u in (vc, vs, vw))
    gates = jax.nn.sigmoid(g_logit.astype(jnp.float32)).reshape(B, S, N_MIX_HEADS, N_BRANCH)
    scale = Dh ** -0.5
    t = jnp.arange(S)
    qg = q.reshape(B, S, G, HPG, Dh)

    k_cmp = compress(kc, pe[0], w1[0], w2[0])
    v_cmp = compress(vc, pe[1], w1[1], w2[1])
    nc = k_cmp.shape[1]
    s_c = jnp.einsum('btghd,bcgd->bghtc', qg, k_cmp).astype(jnp.float32) * scale
    c_end = jnp.arange(nc) * CMP_STRIDE + CMP_LEN - 1
    p_c = masked_softmax(s_c, c_end[None, :] <= t[:, None])
    o_cmp = jnp.einsum('bghtc,bcgd->btghd', p_c.astype(v_cmp.dtype), v_cmp)

    ns = S // SEL_BLOCK
    imp = jnp.einsum('bghtc,cj->bgtj', p_c, overlap_matrix(nc, ns))
    cur = t // SEL_BLOCK
    jb = jnp.arange(ns)[None, :]
    valid = jb <= cur[:, None]
    forced = (jb == 0) | (jb == cur[:, None]) | (jb == cur[:, None] - 1)
    score = jnp.where(forced, jnp.inf, jnp.where(valid, imp, -jnp.inf))
    n_sel = min(N_SEL, ns)
    _, idx = lax.top_k(score, n_sel)
    sel_ok = idx <= cur[None, None, :, None]

    ks_blocks = ks.reshape(B, ns, SEL_BLOCK, G, Dh).transpose(0, 3, 1, 2, 4)
    vs_blocks = vs.reshape(B, ns, SEL_BLOCK, G, Dh).transpose(0, 3, 1, 2, 4)
    pad = ((0, 0), (WINDOW, 0), (0, 0), (0, 0))
    kw_pad, vw_pad = jnp.pad(kw, pad), jnp.pad(vw, pad)
    gather_blocks = jax.vmap(jax.vmap(lambda kb, ib: kb[ib]))

    nqb = S // Q_BLOCK
    q_blocks = jnp.moveaxis(qg.reshape(B, nqb, Q_BLOCK, G, HPG, Dh), 1, 0)
    idx_blocks = jnp.moveaxis(idx.reshape(B, G, nqb, Q_BLOCK, n_sel), 2, 0)
    ok_blocks = jnp.moveaxis(sel_ok.reshape(B, G, nqb, Q_BLOCK, n_sel), 2, 0)

    def query_block(args):
        qb, idxb, okb, bi = args
        tq = bi * Q_BLOCK + jnp.arange(Q_BLOCK)
        kg = gather_blocks(ks_blocks, idxb)
        vg = gather_blocks(vs_blocks, idxb).reshape(B, G, Q_BLOCK, n_sel * SEL_BLOCK, Dh)
        s_s = jnp.einsum('btghd,bgtnkd->bghtnk', qb, kg).astype(jnp.float32) * scale
        s_s = s_s.reshape(B, G, HPG, Q_BLOCK, n_sel * SEL_BLOCK)
        tok = idxb[..., None] * SEL_BLOCK + jnp.arange(SEL_BLOCK)
        m_s = okb[..., None] & (tok <= tq[None, None, :, None, None])
        p_s = masked_softmax(s_s, m_s.reshape(B, G, 1, Q_BLOCK, n_sel * SEL_BLOCK))
        o_s = jnp.einsum('bghtm,bgtmd->btghd', p_s.astype(vg.dtype), vg)
        kwin = lax.dynamic_slice_in_dim(kw_pad, bi * Q_BLOCK, Q_BLOCK + WINDOW, axis=1)
        vwin = lax.dynamic_slice_in_dim(vw_pad, bi * Q_BLOCK, Q_BLOCK + WINDOW, axis=1)
        kp = bi * Q_BLOCK - WINDOW + jnp.arange(Q_BLOCK + WINDOW)
        m_w = (kp[None, :] <= tq[:, None]) & (kp[None, :] > tq[:, None] - WINDOW) & (kp[None, :] >= 0)
        s_w = jnp.einsum('btghd,bsgd->bghts', qb, kwin).astype(jnp.float32) * scale
        p_w = masked_softmax(s_w, m_w)
        o_w = jnp.einsum('bghts,bsgd->btghd', p_w.astype(vwin.dtype), vwin)
        return o_s, o_w

    o_sel, o_win = lax.map(query_block, (q_blocks, idx_blocks, ok_blocks, jnp.arange(nqb)))
    shp = (B, S, N_MIX_HEADS, Dh)
    o_sel = jnp.moveaxis(o_sel, 0, 1).reshape(shp)
    o_win = jnp.moveaxis(o_win, 0, 1).reshape(shp)
    o = (gates[..., 0:1] * o_cmp.reshape(shp) + gates[..., 1:2] * o_sel
         + gates[..., 2:3] * o_win).astype(h.dtype)
    return o.reshape(B, S, N_MIX_HEADS * Dh), q_mem

def memory_attention(q_mem, mem_n, w_kv):
    B, S, _ = q_mem.shape
    km, vm = split_cols(mem_n @ w_kv, [N_MEM_HEADS * HEAD_DIM] * 2)
    q = q_mem.reshape(B, S, N_MEM_HEADS, HEAD_DIM)
    km = km.reshape(B, -1, N_MEM_HEADS, HEAD_DIM)
    vm = vm.reshape(B, -1, N_MEM_HEADS, HEAD_DIM)
    s = jnp.einsum('bthd,bmhd->bhtm', q, km).astype(jnp.float32) * HEAD_DIM ** -0.5
    p = jax.nn.softmax(s, axis=-1)
    return jnp.einsum('bhtm,bmhd->bthd', p.astype(vm.dtype), vm).reshape(B, S, N_MEM_HEADS * HEAD_DIM)

def conv_ffn(h, w_gate, w_up, conv_w, conv_b, w_down):
    S = h.shape[1]
    g_pre = h @ w_gate
    gp = jnp.pad(g_pre, ((0, 0), (CONV_WIDTH - 1, 0), (0, 0)))
    gc = conv_b
    for k in range(CONV_WIDTH):
        gc = gc + gp[:, k:k + S] * conv_w[k]
    return (jax.nn.silu(gc) * (h @ w_up)) @ w_down

def setup_inputs(seed: int = 0) -> dict:
    key = jax.random.key(seed)
    ks = jax.random.split(key, 16)
    f32 = jnp.float32
    n_sb = len(range(0, DEPTH, N_MIXERS))
    n_nsa = len(range(1, DEPTH, N_MIXERS))

    def normal(k, shape, scale):
        return jax.random.normal(k, shape, f32) * scale

    positions = (jax.random.randint(ks[2], (BATCH, 1), 0, 4096, dtype=jnp.int32)
                 + jnp.arange(SEQ, dtype=jnp.int32)[None, :])
    return {
        "x": normal(ks[0], (BATCH, SEQ, D_MODEL), 1.0),
        "mem": normal(ks[1], (BATCH, N_MEM, D_MODEL), 1.0),
        "positions": positions,
        "norm_g": 1.0 + normal(ks[3], (DEPTH, 5, D_MODEL), 0.05),
        "w_in_sb": normal(ks[4], (n_sb, D_MODEL, SB_COLS), D_MODEL ** -0.5),
        "w_in_nsa": normal(ks[5], (n_nsa, D_MODEL, NSA_COLS), D_MODEL ** -0.5),
        "cmp_pe": normal(ks[6], (n_nsa, 2, CMP_LEN, HEAD_DIM), 0.1),
        "cmp_w1": normal(ks[7], (n_nsa, 2, CMP_LEN * HEAD_DIM, CMP_HIDDEN), (CMP_LEN * HEAD_DIM) ** -0.5),
        "cmp_w2": normal(ks[8], (n_nsa, 2, CMP_HIDDEN, HEAD_DIM), CMP_HIDDEN ** -0.5),
        "w_mem_kv": normal(ks[9], (DEPTH, D_MODEL, 2 * N_MEM_HEADS * HEAD_DIM), D_MODEL ** -0.5),
        "w_o": normal(ks[10], (DEPTH, MIX_WIDTH, D_MODEL), MIX_WIDTH ** -0.5),
        "w_ffn_gate": normal(ks[11], (DEPTH, D_MODEL, D_FF), D_MODEL ** -0.5),
        "w_ffn_up": normal(ks[12], (DEPTH, D_MODEL, D_FF), D_MODEL ** -0.5),
        "ffn_conv_w": normal(ks[13], (DEPTH, CONV_WIDTH, D_FF), CONV_WIDTH ** -0.5),
        "ffn_conv_b": normal(ks[14], (DEPTH, D_FF), 0.01),
        "w_ffn_down": normal(ks[15], (DEPTH, D_FF, D_MODEL), D_FF ** -0.5),
    }

def reference(x, mem, positions, norm_g, w_in_sb, w_in_nsa, cmp_pe, cmp_w1, cmp_w2,
              w_mem_kv, w_o, w_ffn_gate, w_ffn_up, ffn_conv_w, ffn_conv_b, w_ffn_down):
    cos, sin = rope_tables(positions)
    for i in range(DEPTH):
        j = i // N_MIXERS
        h = rmsnorm(x, norm_g[i, 0])
        if i % N_MIXERS == 0:
            o_mix, q_mem = stick_breaking_mixer(h, w_in_sb[j])
        else:
            o_mix, q_mem = nsa_mixer(h, w_in_nsa[j], cmp_pe[j], cmp_w1[j], cmp_w2[j], cos, sin)
        o_mem = memory_attention(q_mem, rmsnorm(mem, norm_g[i, 4]), w_mem_kv[i])
        attn = jnp.concatenate([o_mix, o_mem], axis=-1) @ w_o[i]
        x = x + rmsnorm(attn, norm_g[i, 1])
        h = rmsnorm(x, norm_g[i, 2])
        f = conv_ffn(h, w_ffn_gate[i], w_ffn_up[i], ffn_conv_w[i], ffn_conv_b[i], w_ffn_down[i])
        x = x + rmsnorm(f, norm_g[i, 3])
    return x


_drawn_inputs = setup_inputs


def setup_inputs(seed=0):
    import zlib

    import numpy as np

    out = dict(_drawn_inputs(seed))
    spreads = {}
    factors = {'ffn_conv_b': 7.036}
    for name, (base, spread) in spreads.items():
        noise = np.random.default_rng([zlib.crc32(name.encode()), seed]).standard_normal(out[name].shape)
        drawn = base * np.exp(spread * noise) if base else spread * noise
        out[name] = __import__('jax').numpy.asarray(drawn.astype(out[name].dtype))
    for name, factor in factors.items():
        out[name] = (out[name] * factor).astype(out[name].dtype)
    return out
```

```python
from contextlib import ExitStack, contextmanager

import numpy as np

import concourse.bass as bass
from concourse import mybir

F32 = mybir.dt.float32
F32R = mybir.dt.float32r
BF16 = mybir.dt.bfloat16
I32 = mybir.dt.int32
ACT = mybir.ActivationFunctionType
ALU = mybir.AluOpType
AX_X = mybir.AxisListType.X

P = 128
T = 256
D = 2048
DT = D // P
DFF = 5632
FT = DFF // P
HEADS, MEM_HEADS, GROUPS = 12, 4, 2
HPG = HEADS // GROUPS
CMP_STRIDE, CMP_LEN = 16, 32
NC = T // CMP_STRIDE - 1
SCALE = P ** -0.5
EPS = 1e-6
NEG = -1e30
GUARD = -1e29
RING = 4
PIECE = 8
K16 = (8, 8)
K32 = (8, 8, 8, 8)
K44 = (8, 8, 7, 7, 7, 7)
MAGIC = 1.5 * 2.0 ** 23
TWO_PI_PARTS = (6.28125, 1.93500518798828125e-3, 3.01991598e-7)

C_ONES, C_IDENT, C_NEGL, C_NEGONES = 0, P, 2 * P, 3 * P
C_FREQ, C_SIGN, C_EPS, C_HALFPI = (4 * P + k for k in range(4))
C_COLS = 4 * P + 4
M_IDENT, M_STICK, M_CAUSAL, M_CMP = 0, P, 2 * P, 3 * P
M_COLS = 3 * P + 2 * CMP_STRIDE


class At:

    def __init__(self, base, step=0):
        self.base, self.step = base, step

    def __call__(self, i, k=0):
        return self.base + k if i is None or not self.step else i * self.step + (self.base + k)

    def slot(self, k=0):
        return (self.base + k) % RING

    def landings(self, i, k=0):
        first = 16 * ((self.base + k) // RING + 1)
        return first if i is None or not self.step else i * (16 * self.step // RING) + first


class Slot:

    def __init__(self, prev=None, w=None, chunk=None, pieces=None, operand=None, gate=None, order=None,
                 before=(), after=(), react=(), hooks=None):
        self.w, self.chunk, self.pieces = w, chunk, pieces
        self.c = self.n = None
        self.operand = operand
        self.prev = prev
        self.gate = gate
        self.order = order
        self.before, self.after, self.react = before, after, react
        self.hooks = hooks or {}


def schedule():
    plan = []
    state = {"c": 0, "n": 0}

    def add(rounds, slots):
        chunks, pieces = len(slots), sum(len(s.pieces) for s in slots)
        if rounds:
            assert chunks % 2 == 0 and pieces % RING == 0
        for s in slots:
            s.c = At(state["c"], chunks if rounds else 0)
            s.n = At(state["n"], pieces if rounds else 0)
            state["c"] += 1
            state["n"] += len(s.pieces)
        if rounds:
            state["c"] += chunks * (rounds - 1)
            state["n"] += pieces * (rounds - 1)
        plan.append((rounds, slots))

    for l in range(2):
        last = None if l == 0 else ("memv", (0, At(3)))
        k0 = Slot(w=f"mem{l}", chunk=At(0), pieces=K16, operand=f"amem{l}", prev=last)
        v0 = Slot(w=f"mem{l}", chunk=At(1), pieces=K16, operand=f"amem{l}", prev=("memk", (l, At(0))))
        if l == 0:
            k0.before, k0.react, k0.gate = [("stats", 0)], [("stats", 0), ("apply", 0)], ("h", 0)
            v0.react = [("apply", 1)]
        else:
            k0.after, k0.react = [("vT", At(3)), ("stats", 1)], [("stats", 1)]
            v0.react, v0.gate = [("vcopy", (0, 3, At(3))), ("apply", 2)], None
            k0.gate = ("h", 1)
        add(None, [k0, v0])
        add(3, [
            Slot(w=f"mem{l}", chunk=At(2, 2), pieces=K16, operand=f"amem{l}", prev=("memv", (l, At(0, 1))),
                 after=[("vT", At(4 * l, 1))]),
            Slot(w=f"mem{l}", chunk=At(3, 2), pieces=K16, operand=f"amem{l}", prev=("memk", (l, At(1, 1))),
                 react=[("vcopy", (l, At(0, 1), At(4 * l, 1)))]),
        ])

    extra = {}
    for g in range(MEM_HEADS):
        extra.setdefault(g + 1, ([], []))[0].append(("memA", g))
        extra.setdefault(g + 2, ([], []))[0].append(("memB", g))
        extra.setdefault(g + 2, ([], []))[1].append(("memA", g))
        extra.setdefault(g + 3, ([], []))[0].append(("memC", g))
        extra.setdefault(g + 3, ([], []))[1].append(("memB", g))
        extra.setdefault(g + 4, ([], []))[1].append(("memC", g))
    rank = {"memC": 0, "memB": 1, "memA": 2}

    def ordered(steps):
        return sorted(steps, key=lambda s: rank[s[0]])

    def memory_steps(k):
        after, react = extra.get(k, ([], []))
        return ordered(after), ordered(react)[::-1]

    slots = []
    for g in range(MEM_HEADS):
        after, react = memory_steps(g)
        slots.append(Slot(w="in0", chunk=At(g), pieces=K16, operand="h", after=after, react=react,
                          prev=("memv", (1, At(3))) if g == 0 else ("qm", g - 1)))
    slots[0].after = [("vT", At(7))] + slots[0].after
    slots[0].gate = ("h", 2)
    slots[1].react = [("vcopy", (1, 3, At(7)))] + slots[1].react
    for h in range(2):
        for j, kind in enumerate("qkv"):
            after, react = memory_steps(4 + 3 * h + j)
            prev = ("qm", 3) if (h, j) == (0, 0) else ("qkv", ("vqk"[j], (h if j else h - 1) % 2))
            slots.append(Slot(w="in0", chunk=At(4 + 3 * h + j), pieces=K16, operand="h", prev=prev,
                              after=after, react=react))
    for j, s in enumerate(slots[7:]):
        s.after = s.after + [("stick" + "ABC"[j], (At(0), 0))]
        if j:
            s.react = s.react + [("stick" + "AB"[j - 1], (At(0), 0))]
    add(None, slots)
    slots = []
    for h in range(2):
        p, q = h % 2, (h + 1) % 2
        before, this = (At(2 + h - 1, 2), q), None
        slots += [
            Slot(prev=("qkv", ("v", q)), after=[("stickA", before)], react=[("stickC", (At(h, 2), p))]),
            Slot(prev=("qkv", ("q", p)), after=[("stickB", before)], react=[("stickA", before)]),
            Slot(prev=("qkv", ("k", p)), after=[("stickC", before)], react=[("stickB", before)]),
        ]
    for j, s in enumerate(slots):
        s.w, s.chunk, s.pieces, s.operand = "in0", At(10 + j, 6), K16, "h"
    add(5, slots)

    def out_projection(l, first, second):
        first.w = second.w = f"out{l}"
        first.order = {0: [0, 1, 2, 3, 4, 5, 6, 7, 8, 9, 12, 13, 14, 15, 10, 11]}[0]
        first.gate = ("o", l)
        for k, s in enumerate((first, second)):
            s.chunk, s.pieces, s.operand = At(k), K16, "o"
        add(None, [first, second])
        add(7, [Slot(w=f"out{l}", chunk=At(2 + k, 2), pieces=K16, operand="o", prev=("y", (l, 1, At(1 + k, 2))))
                for k in range(2)])

    def ffn(l):
        s = l + 2 if l == 0 else 4
        gate0 = Slot(w=f"ffn{l}", chunk=At(0), pieces=K16, operand="h", prev=("y", (l, 1, At(DT - 1))),
                     before=[("post", 2 * l), ("stats", s)], gate=("h", 3 + 2 * l),
                     react=[("post", 2 * l), ("stats", s), ("apply", 3 + 2 * l)])
        up0 = Slot(w=f"ffn{l}", chunk=At(1), pieces=K16, operand="h", prev=("gate", (l, At(0))))
        add(None, [gate0, up0])
        add(FT - 1, [
            Slot(w=f"ffn{l}", chunk=At(2, 2), pieces=K16, operand="h", prev=("up", (l, At(0, 1)))),
            Slot(w=f"ffn{l}", chunk=At(3, 2), pieces=K16, operand="h", prev=("gate", (l, At(1, 1)))),
        ])
        add(None, [
            Slot(w=f"down{l}", chunk=At(0), pieces=K44, operand="mid", prev=("up", (l, At(FT - 1))),
                 gate=("mid", l)),
            Slot(w=f"down{l}", chunk=At(1), pieces=K44, operand="mid", prev=("y", (l, 3, At(0)))),
        ])
        add(7, [Slot(w=f"down{l}", chunk=At(2 + k, 2), pieces=K44, operand="mid", prev=("y", (l, 3, At(1 + k, 2))))
                for k in range(2)])

    h11 = (At(11), 1)
    out_projection(
        0,
        Slot(prev=("qkv", ("v", 1)), react=[("stickC", (At(10), 0)), ("stickA", h11), ("stickB", h11), ("stickC", h11)],
             hooks={8: [("stickA", h11)], 10: [("stickB", h11)], 11: [("stickC", h11)]}),
        Slot(prev=("y", (0, 1, At(0)))))
    ffn(0)

    kinds = [("rope", "kc0"), ("rope", "kc1"), ("vc", 0), ("vc", 1), ("v", (0, 0)), ("v", (0, 1)), ("v", (1, 0)),
             ("v", (1, 1)), ("rope", "ks0"), ("rope", "ks1"), ("rope", "kw0"), ("rope", "kw1"), ("gates", 0)]
    kinds += [("qm", g) for g in range(MEM_HEADS)] + [("hid", k) for k in range(4)]
    kinds += [("rope", f"q{h % 2}") for h in range(HEADS)]
    slots = []
    cmp0, q0 = 17, 21
    for k in range(q0 + HEADS):
        s = Slot(prev=kinds[k - 1] if k else ("y", (0, 3, At(DT - 1))))
        if cmp0 <= k < q0:
            s.w, s.chunk, s.pieces, s.operand = "cmp", At(k - cmp0), K32, f"blk{(k - cmp0) // 2}"
        else:
            s.w, s.chunk, s.pieces, s.operand = "in1", At(k if k < cmp0 else k - 4), K16, "h"
        s.after, s.react = [], []
        slots.append(s)
    slots[0].before, slots[0].gate = [("post", 1), ("stats", 3)], ("h", 4)
    slots[0].react = [("post", 1), ("stats", 3), ("apply", 4), ("tables", 0)]
    for j, (w, g) in enumerate([(0, 0), (0, 1), (1, 0), (1, 1)]):
        slots[5 + j].after.append(("vT", At(20 + j)))
        slots[6 + j].react.append(("vcopy1", (w, g, 20 + j)))
    slots[4].react.append(("blocks", 0))
    slots[5].react.append(("blocks", 1))
    slots[13].after.append(("gatesT", 24))
    slots[14].react.append(("gates", 24))
    for g in range(MEM_HEADS):
        slots[14 + g].after.append(("memA", 4 + g))
        slots[15 + g].after.append(("memB", 4 + g))
        slots[15 + g].react.append(("memA", 4 + g))
        slots[16 + g].after.append(("memC", 4 + g))
        slots[16 + g].react.append(("memB", 4 + g))
        slots[17 + g].react.append(("memC", 4 + g))
    for s in slots:
        mem = [x for x in s.after if x[0] in rank]
        s.after = [x for x in s.after if x[0] not in rank] + ordered(mem)
        mem = [x for x in s.react if x[0] in rank]
        s.react = [x for x in s.react if x[0] not in rank] + ordered(mem)[::-1]
    slots[19].after.append(("kcmp", 25))
    slots[20].react.append(("kcmp", 25))
    slots[21].after.append(("vcmp", 26))
    slots[22].react.append(("vcmp", 26))
    for k in range(HEADS):
        s = slots[q0 + k]
        s.after += [("nsa" + x, k - d) for x, d in (("C", 3), ("B", 2), ("A", 1)) if k >= d]
        s.react += [("nsa" + x, k - d) for x, d in (("A", 2), ("B", 3), ("C", 4)) if k >= d]
    add(None, slots)
    out_projection(
        1,
        Slot(prev=kinds[-1], before=[("nsaC", 9), ("nsaB", 10)],
             react=[("nsaA", 10), ("nsaB", 9), ("nsaC", 8), ("nsaB", 10), ("nsaC", 9), ("nsaA", 11), ("nsaC", 10),
                    ("nsaB", 11), ("nsaC", 11)],
             hooks={8: [("nsaC", 10), ("nsaA", 11)], 10: [("nsaB", 11), ("nsaC", 11)]}),
        Slot(prev=("y", (1, 1, At(0)))))
    ffn(1)
    return plan, state["c"], state["n"]


PLAN, CHUNKS, PIECES_ALL = schedule()


class Steps:

    def __init__(self, eng, sem):
        self.eng, self.sem, self.n, self.i, self.per = eng, sem, 0, None, 0

    def value(self):
        return self.n if self.i is None else self.i * self.per + self.n

    def done(self, ins):
        ins.then_inc(self.sem, 1)
        self.n += 1
        self.eng.wait_ge(self.sem, self.value())

    @contextmanager
    def rounds(self, n, i, per):
        start, self.i, self.per = self.n, i, per
        yield
        assert self.n - start == per, (self.n - start, per)
        self.n, self.i = start + per * n, None


def build(nc, A):
    with ExitStack() as ctx:
        def sb(name, shape, dt=F32, stack=ctx):
            return stack.enter_context(nc.sbuf_tensor(name, shape, dt))

        def sem(name):
            return ctx.enter_context(nc.semaphore(name))

        x = sb("x", [P, DT, T])
        with ExitStack() as over:
            y = sb("y", [P, DT, T], F32, over)
        h = sb("h", [P, DT, 2, T], F32R)
        raw = [sb(f"raw{k}", [P, PIECE * P]) for k in range(RING)]
        hi = [sb(f"hi{k}", [P, PIECE * P], F32R) for k in range(RING)]
        lo = [sb(f"lo{k}", [P, PIECE * P], F32R) for k in range(RING)]
        cross = sb("cross", [P, 2, T])
        cst = sb("cst", [P, C_COLS])
        msk = sb("msk", [P, M_COLS], BF16)
        gains = sb("gains", [P, 2, 5, DT])
        conv = sb("conv", [P, 2, FT, 4])
        acc = sb("acc", [P, T])
        sq1 = sb("sq1", [P, T])
        vtmp = sb("vtmp", [P, T])
        yt = sb("yt", [P, 2, T])
        root = sb("root", [P, T])
        rstd = sb("rstd", [P, T])
        with ExitStack() as over:
            sq = sb("sq", [P, 4, T], F32, over)
            hf = sb("hf", [P, 4, T], F32, over)
        with ExitStack() as over:
            gp = sb("gp", [P, T + 8], F32, over)
            cv = sb("cv", [P, 3, T], F32, over)
            sg = sb("sg", [P, T], F32, over)
            up = sb("up", [P, T], F32, over)
            mf = sb("mf", [P, T], F32, over)
        sb("shared", [P, 8 * T])
        def region(tensors):
            with ExitStack() as over:
                return [sb(n, s, dt, over) for n, s, dt in tensors]

        mid, = region([("mid", [P, FT, 2, T], F32R)])
        o, memT, km0, vm0, amem1 = region([
            ("o", [P, DT, 2, T], F32R), ("memT", [P, DT, T], F32), ("km0", [P, MEM_HEADS, T], F32),
            ("vm0", [P, 2, MEM_HEADS, P], F32), ("amem1", [P, DT, 2, T], F32R)])
        _, km1, vm1 = region([("o_a", [P, DT, 2, T], F32R), ("km1", [P, MEM_HEADS, T], F32),
                              ("vm1", [P, 2, MEM_HEADS, P], F32)])
        (_, _, _, _, qm_0, pm_0, ptm_0, q2, k2, vT2, vtok, ab, ex, ln, rl, sp, aw) = region([
            ("o_b", [P, DT, 2, T], F32R), ("memT_b", [P, DT, T], F32), ("km0_b", [P, MEM_HEADS, T], F32),
            ("vm0_b", [P, 2, MEM_HEADS, P], F32), ("qm_0", [P, MEM_HEADS, T], F32), ("pm_0", [P, 2, T], F32),
            ("ptm_0", [P, 2, T], F32), ("q2", [P, 2, T], F32), ("k2", [P, 2, T], F32), ("vT2", [P, 2, T], F32),
            ("vtok", [P, 2, P], F32), ("ab", [P, 384], F32), ("ex", [P, 384], F32), ("ln", [P, 384], F32),
            ("rl", [P, 384], F32), ("sp", [P, 384], F32), ("aw", [P, 384], F32)])
        with ExitStack() as over:
            (_, km1b, vm1b, cosT, sinT, ub, us, ra, rb, kT, vT, kc, vc, w2, pe, hid, ehid, hs, kcmp, vcmp,
             gt, eg, G, qr, qm_1, pm_1, ptm_1, vtmp1) = [sb(n, shape, F32R if n == "o_c" else F32, over) for n, shape in [
                 ("o_c", [P, DT, 2, T]), ("km1b", [P, MEM_HEADS, T]), ("vm1b", [P, 2, MEM_HEADS, P]),
                 ("cosT", [P, T]), ("sinT", [P, T]), ("ub", [P, T]), ("us", [P, T]), ("ra", [P, T]), ("rb", [P, T]),
                 ("kT", [P, 2, GROUPS, T]), ("vT", [P, 2, GROUPS, 2, P]), ("kc", [P, GROUPS, T]),
                 ("vc", [P, GROUPS, T]), ("w2", [P, 2, 2, P]), ("pe", [P, 2, CMP_LEN]), ("hid", [P, 2, 2 * NC]),
                 ("ehid", [P, 3, 2 * NC]), ("hs", [P, 2, 2, 2 * NC]), ("kcmp", [P, GROUPS, NC]),
                 ("vcmp", [P, GROUPS, P]), ("gt", [P, T]), ("eg", [P, 2, 36]), ("G", [P, HEADS, 3, 2]),
                 ("qr", [P, 2, T]), ("qm_1", [P, MEM_HEADS, T]), ("pm_1", [P, 2, T]), ("ptm_1", [P, 2, T]),
                 ("vtmp1", [P, T])]]
            blkf0, blkf1 = region([("blkf0", [P, CMP_LEN, 2 * NC], F32), ("blkf1", [P, CMP_LEN, 2 * NC], F32)])
            ps_s, ps_w, ps_c, pt_s, pt_w, pt_c = region([
                ("ps_s", [P, 384], F32), ("ps_w", [P, 384], F32), ("ps_c", [P, 2, 16], F32),
                ("pt_s", [P, 384], F32), ("pt_w", [P, 384], F32), ("pt_c", [P, 2, P], F32)])
        blk = region([("blk0", [P, CMP_LEN, 2, 2 * NC], F32R), ("blk1", [P, CMP_LEN, 2, 2 * NC], F32R)])
        sb("region", [P, FT, 2, T], F32R)
        mxs = sb("mxs", [P, 8])
        nb = sb("nb", [P, 8])
        sums = sb("sums", [P, 8])
        guard = sb("guard", [P, 8])
        rs = sb("rs", [P, 8])
        wgt = sb("wgt", [P, 8])
        km, vm = [km0, km1], [vm0, vm1]
        kmem, vmem = [km0, km1b], [vm0, vm1b]
        qms, pms, ptms = [qm_0, qm_1], [pm_0, pm_1], [ptm_0, ptm_1]
        amem = [o, amem1]

        def bank(name):
            return ctx.enter_context(nc.psum_tensor(name, [P, 512], F32))

        gb = [bank("gemm0"), bank("gemm1")]
        SA, SB, TA, TB, OB, XB = (bank(n) for n in ("SA", "SB", "TA", "TB", "OB", "XB"))

        landed = [sem(f"landed{k}") for k in range(RING)]
        hi_done, lo_done, piece_done = sem("hi_done"), sem("lo_done"), sem("piece_done")
        cross_done, evac_done = sem("cross_done"), sem("evac_done")
        s_mem, s_x, s_small = sem("s_mem"), sem("s_x"), sem("s_small")
        s_l1, s_spill = sem("s_l1"), sem("s_spill")
        s_out = sem("s_out")
        dve_step, act_step, pool_step = sem("dve_step"), sem("act_step"), sem("pool_step")
        sq_ready, sq_read = sem("sq_ready"), sem("sq_read")
        post_stat, root_ready, xn_ready = sem("post_stat"), sem("root_ready"), sem("xn_ready")
        hf_ready, hh_ready, h_done = sem("hf_ready"), sem("hh_ready"), sem("h_done")
        yt_ready, yt_read, acc_done = sem("yt_ready"), sem("yt_read"), sem("acc_done")
        x_written, x_read = sem("x_written"), sem("x_read")
        z_ready, ln_ready, sp_ready, c_ready, a_ready = (sem(n) for n in (
            "z_ready", "ln_ready", "sp_ready", "c_ready", "a_ready"))
        pv_ready, o_done, vtok_ready = sem("pv_ready"), sem("o_done"), sem("vtok_ready")
        ms_ready, mb_ready, me_ready, mp_ready, mt_ready, mpt_ready, mo_ready = (sem(n) for n in (
            "ms_ready", "mb_ready", "me_ready", "mp_ready", "mt_ready", "mpt_ready", "mo_ready"))
        conv_ready, silu_ready, mid_done = sem("conv_ready"), sem("silu_ready"), sem("mid_done")
        abs_ready, red_ready, trig_ready = sem("abs_ready"), sem("red_ready"), sem("trig_ready")
        rope_in, rope_done = sem("rope_in"), sem("rope_done")
        blkf_ready, blkh_ready, blk_done = sem("blkf_ready"), sem("blkh_ready"), sem("blk_done")
        hid_ready, hexp_ready, hs_ready = sem("hid_ready"), sem("hexp_ready"), sem("hs_ready")
        gt_ready, gexp_ready = sem("gt_ready"), sem("gexp_ready")
        cmp_ready = sem("cmp_ready")
        ns_ready, nb_ready, ne_ready, np_ready, nt_ready, npt_act, npt_dve = (sem(n) for n in (
            "ns_ready", "nb_ready", "ne_ready", "np_ready", "nt_ready", "npt_act", "npt_dve"))

        ones, ident = cst[:, C_ONES:C_ONES + P], cst[:, C_IDENT:C_IDENT + P]
        neg_l, neg_ones = cst[:, C_NEGL:C_NEGL + P], cst[:, C_NEGONES:C_NEGONES + P]

        def col(c):
            return cst[:, c:c + 1]

        identb, stick_mask = msk[:, M_IDENT:M_IDENT + P], msk[:, M_STICK:M_STICK + P]
        causal_mask = msk[:, M_CAUSAL:M_CAUSAL + P]

        def one(ap, k):
            return ap[:, k, :] if isinstance(k, int) else ap[:, bass.ds(k, 1), :].rearrange("p o t -> p (o t)")

        SMALL = 16 * 4
        ROOT_S, ROOT_P = (1, 2, 4, 6, 8), (3, 5, 7, 9)
        APPLY = [
            ("mem", 0, 4, "amem0"), ("mem", 1, 4, "amem1"), ("x", 0, 0, "h"), ("x", 0, 2, "h"),
            ("x", 1, 0, "h"), ("x", 1, 2, "h")]
        POST = [(0, 1), (0, 3), (1, 1), (1, 3)]
        dest = {"amem0": o, "amem1": amem1, "h": h, "o": o, "mid": mid, "blk0": blk[0], "blk1": blk[1]}
        ROPE_DEST = {"kc0": kc[:, 0, :], "kc1": kc[:, 1, :], "ks0": kT[:, 0, 0, :], "ks1": kT[:, 0, 1, :],
                     "kw0": kT[:, 1, 0, :], "kw1": kT[:, 1, 1, :], "q0": qr[:, 0, :], "q1": qr[:, 1, :]}
        L0_DOWN_END = None
        for rounds, slots in PLAN:
            for s in slots:
                if s.w == "down0" and rounds:
                    L0_DOWN_END = s.n.base + len(s.pieces) + s.n.step * (rounds - 1)
        NSLOT = sum((r or 1) * len(s) for r, s in PLAN)
        assert NSLOT == CHUNKS
        block = ctx.enter_context(nc.Block())

        @block.sync
        def _(sp):
            def load(s, i, j, off):
                k = s.n.slot(j)
                if s.n.base + j >= RING:
                    sp.wait_ge(lo_done, s.n(i, j - RING + 1))
                kt = s.pieces[j]
                c = s.chunk(i)
                w = A[s.w]
                src = (w[c] if isinstance(c, int) else w[bass.ds(c, 1)].rearrange("o p k n -> (o p) k n"))
                src = src[:, off:off + kt, :].rearrange("p k n -> p (k n)")
                sp.dma_start(raw[k][:, 0:kt * P], src).then_inc(landed[k], 16)

            def layer1_loads():
                sp.wait_ge(piece_done, L0_DOWN_END)
                sp.wait_ge(s_spill, 32)
                sp.dma_start(km1b[:], A["spill_k"]).then_inc(s_l1, 16)
                sp.dma_start(vm1b[:], A["spill_v"]).then_inc(s_l1, 16)
                sp.dma_start(w2[:], A["cmp_w2"]).then_inc(s_l1, 16)
                sp.dma_start(pe[:], A["cmp_pe"]).then_inc(s_l1, 16)
                sp.dma_start(ra[:].bitcast(I32), A["positions"]).then_inc(s_l1, 16)

            for rounds, slots in PLAN:
                def body(i):
                    for s in slots:
                        off = 0
                        for j in range(len(s.pieces)):
                            load(s, i, j, off)
                            off += s.pieces[j]
                        if s.w == "in1" and s.chunk(i) == 0:
                            layer1_loads()
                if rounds:
                    with sp.Fori(0, rounds) as i:
                        body(i)
                else:
                    body(None)
            for c in range(DT):
                sp.wait_ge(xn_ready, 3 * DT + c + 1)
                sp.dma_start(A["out"][:, c, :], x[:, c, :]).then_inc(s_out, 16)
            sp.wait_ge(s_out, 16 * DT)

        @block.tensor
        def _(pe_):
            mm, tr = nc.tensor.matmul, nc.tensor.transpose

            def add(out, lhsT, rhs, first, last=True):
                return mm(out, lhsT, rhs, start=first, stop=last, skip_group_check=True)

            def stats(k):
                for c in range(DT):
                    pe_.wait_ge(sq_ready, DT * k + c + 1)
                    if k == 0 and c == 0:
                        pe_.wait_ge(s_small, SMALL)
                    mm(SB[:, T:2 * T], ones, sq[:, c % 4, :], start=c == 0, stop=c == DT - 1).then_inc(sq_read, 1)

            def post(k):
                pe_.wait_ge(acc_done, DT * (k + 1))
                mm(SB[:, 0:T], ones, acc[:], start=True, stop=True).then_inc(post_stat, 1)

            def transposes_of_v(s, i, u, src):
                pe_.wait_ge(evac_done, s.c(i))
                if u.base >= 1:
                    pe_.wait_ge(x_read, u(i))
                tr(XB[:, 0:P], src[:, 0:P], ident)
                tr(XB[:, P:2 * P], src[:, P:2 * P], ident).then_inc(x_written, 1)

            def stickA(s, i, a):
                hd, p = a
                transposes_of_v(s, i, At(8 + hd.base, hd.step), vT2[:, p, :])
                add(SA[:, 0:T], k2[:, p, 0:P], q2[:, p, :], True, False)
                add(SA[:, T:T + P], k2[:, p, P:T], q2[:, p, P:T], False, False)
                add(SA[:, 0:P], identb, stick_mask, False, False)
                add(SA[:, T:T + P], identb, stick_mask, False).then_inc(z_ready, 1)

            def stickB(s, i, a):
                hd, p = a
                pe_.wait_ge(sp_ready, hd(i, 1))
                add(SA[:, 0:T], neg_l, sp[:, 0:T], False, False)
                add(SA[:, P:T], neg_ones, sp[:, T:T + P], False, False)
                add(SA[:, T:T + P], neg_l, sp[:, T:T + P], False).then_inc(c_ready, 1)

            def stickC(s, i, a):
                hd, p = a
                pe_.wait_ge(a_ready, hd(i, 1))
                pe_.wait_ge(vtok_ready, hd(i, 1))
                pe_.wait_ge(o_done, hd(i, 0 if hd.base == 0 else MEM_HEADS)) if hd.base else None
                add(OB[:, 0:T], vtok[:, 0, :], aw[:, 0:T], True, False)
                add(OB[:, P:T], vtok[:, 1, :], aw[:, T:T + P], False).then_inc(pv_ready, 1)

            def memA(s, i, g):
                l, k = divmod(g, MEM_HEADS)
                pe_.wait_ge(evac_done, s.c(i))
                if l and k == 0:
                    pe_.wait_ge(s_l1, 16 * 5)
                for t in range(2):
                    m = add(SB[:, t * T:(t + 1) * T], qms[l][:, k, t * P:(t + 1) * P], kmem[l][:, k, :], t == 0)
                m.then_inc(ms_ready, 1)

            def memB(s, i, g):
                l = g // MEM_HEADS
                pe_.wait_ge(mp_ready, g + 1)
                for m_ in range(2):
                    for t in range(2):
                        m = tr(TA[:, m_ * T + t * P:m_ * T + (t + 1) * P], pms[l][:, t, m_ * P:(m_ + 1) * P], ident)
                m.then_inc(mt_ready, 1)

            def memC(s, i, g):
                l, k = divmod(g, MEM_HEADS)
                pe_.wait_ge(mpt_ready, g + 1)
                if k:
                    pe_.wait_ge(o_done, 16 * l + k)
                add(TB[:, 0:T], vmem[l][:, 0, k, :], ptms[l][:, 0, :], True, False)
                add(TB[:, 0:T], vmem[l][:, 1, k, :], ptms[l][:, 1, :], False).then_inc(mo_ready, 1)

            def gatesT(s, i, u):
                pe_.wait_ge(evac_done, s.c(i))
                pe_.wait_ge(x_read, u)
                for t in range(2):
                    m = tr(XB[:, t * P:(t + 1) * P], gt[:, t * P:(t + 1) * P], ident)
                m.then_inc(x_written, 1)

            def kcmp_mm(s, i, u):
                pe_.wait_ge(hs_ready, 2)
                pe_.wait_ge(x_read, u)
                for c in range(2):
                    m = mm(XB[:, 0:2 * NC], w2[:, 0, c, :], hs[:, 0, c, :], start=c == 0, stop=c == 1)
                m.then_inc(x_written, 1)

            def vcmp_mm(s, i, u):
                pe_.wait_ge(hs_ready, 4)
                pe_.wait_ge(x_read, u)
                for g in range(GROUPS):
                    for c in range(2):
                        m = add(XB[0:NC, g * P:(g + 1) * P], hs[:, 1, c, g * NC:(g + 1) * NC], w2[:, 1, c, :],
                                g == 0 and c == 0)
                m.then_inc(x_written, 1)

            def nsaA(s, i, hd):
                p, g = hd % 2, hd // HPG
                pe_.wait_ge(rope_done, 6 + hd + 1)
                pe_.wait_ge(cmp_ready, 1)
                qt = [qr[:, p, t * P:(t + 1) * P] for t in range(2)]
                for b, s_ in ((0, SA), (1, SB)):
                    add(s_[:, 0:P], qt[0], kT[:, b, g, 0:P], True, False)
                    add(s_[:, P:3 * P], qt[1], kT[:, b, g, :], False, False)
                    add(s_[:, 0:P], identb, causal_mask, False, False)
                    m = add(s_[:, 2 * P:3 * P], identb, causal_mask, False, b == 1)
                    if b == 0:
                        for t in range(2):
                            at = 3 * P + 16 * t
                            add(SA[:, at:at + NC], qt[t], kcmp[:, g, :], False, False)
                            add(SA[:, at:at + NC], identb, msk[:, M_CMP + 16 * t:M_CMP + 16 * t + NC], False, t == 1)
                m.then_inc(ns_ready, 1)

            def nsaB(s, i, hd):
                pe_.wait_ge(np_ready, hd + 1)
                for b, (src, dst) in enumerate(((ps_s, TA), (ps_w, TB))):
                    for k in range(3):
                        tr(dst[:, k * P:(k + 1) * P], src[:, k * P:(k + 1) * P], ident)
                    m = tr(XB[0:NC, b * P:(b + 1) * P], ps_c[:, b, 0:NC], ident)
                m.then_inc(nt_ready, 1)

            def nsaC(s, i, hd):
                g = hd // HPG
                pe_.wait_ge(npt_act, hd + 1)
                pe_.wait_ge(npt_dve, hd + 1)
                if hd == 0:
                    pe_.wait_ge(cmp_ready, 2)
                pe_.wait_ge(o_done, 16 + MEM_HEADS + hd)
                add(OB[:, 0:T], vcmp[0:NC, g, :], pt_c[0:NC, :, :].rearrange("p a b -> p (a b)"), True, False)
                for b, pt in ((0, pt_s), (1, pt_w)):
                    add(OB[:, 0:T], vT[:, b, g, 0, :], pt[:, 0:T], False, False)
                    m = add(OB[:, P:T], vT[:, b, g, 1, :], pt[:, T:T + P], False, b == 1)
                m.then_inc(pv_ready, 1)

            steps = {
                "stats": lambda s, i, a: stats(a), "post": lambda s, i, a: post(a),
                "vT": lambda s, i, a: transposes_of_v(s, i, a, vtmp if a.base < 8 else vtmp1),
                "stickA": stickA, "stickB": stickB, "stickC": stickC, "memA": memA, "memB": memB, "memC": memC,
                "gatesT": gatesT, "kcmp": kcmp_mm, "vcmp": vcmp_mm, "nsaA": nsaA, "nsaB": nsaB, "nsaC": nsaC}

            def gemm(s, i):
                if s.c.base >= 2:
                    pe_.wait_ge(evac_done, s.c(i, -1))
                act = dest[s.operand]
                cols = 2 * NC if s.w == "cmp" else T
                out = gb[s.c.base % 2]
                order = s.order or range(sum(s.pieces))
                k = 0
                starts = [sum(s.pieces[:j]) for j in range(len(s.pieces))]
                if s.w == "cmp" and s.chunk(i) % 2 == 0:
                    pe_.wait_ge(blk_done, s.chunk(i) // 2 + 1)
                if s.gate and s.gate[0] == "mid":
                    pe_.wait_ge(mid_done, FT * s.gate[1] + FT - 1)
                for j, kts in enumerate(s.pieces):
                    pe_.wait_ge(lo_done, s.n(i, j + 1))
                    for _ in range(kts):
                        kt = order[k]
                        for step, a in s.hooks.get(kt, ()):
                            steps[step](s, i, a)
                        if s.gate:
                            if s.gate[0] == "h":
                                pe_.wait_ge(h_done, DT * s.gate[1] + kt + 1)
                            elif s.gate[0] == "o" and kt < HEADS:
                                pe_.wait_ge(o_done, 16 * s.gate[1] + MEM_HEADS + kt + 1)
                            elif s.gate[0] == "mid" and kt == FT - 1:
                                pe_.wait_ge(mid_done, FT * (s.gate[1] + 1))
                        slot = s.n.slot([m for m in range(len(starts)) if starts[m] <= kt][-1])
                        at = (kt - starts[[m for m in range(len(starts)) if starts[m] <= kt][-1]]) * P
                        mm(out[:, 0:2 * cols], hi[slot][:, at:at + P], act[:, kt, :, :].rearrange("p a t -> p (a t)"),
                           start=k == 0, stop=False, skip_group_check=True)
                        m = mm(out[:, cols:2 * cols], lo[slot][:, at:at + P], act[:, kt, 0, :],
                               start=False, stop=k == sum(s.pieces) - 1, skip_group_check=True)
                        k += 1
                    m.then_inc(piece_done, 1)

            pe_.wait_ge(s_small, SMALL)
            for rounds, slots in PLAN:
                def body(i):
                    for s in slots:
                        for step, a in s.before:
                            steps[step](s, i, a)
                        gemm(s, i)
                        for step, a in s.after:
                            steps[step](s, i, a)
                if rounds:
                    with pe_.Fori(0, rounds) as i:
                        body(i)
                else:
                    body(None)
            post(3)

        @block.scalar
        def _(act_):
            act = nc.scalar.activation
            me = Steps(act_, act_step)

            act_.dma_start(memT[:], A["memT"]).then_inc(s_mem, 16)
            act_.dma_start(cst[:], A["consts"]).then_inc(s_small, 16)
            act_.dma_start(msk[:], A["masks"]).then_inc(s_small, 16)
            act_.dma_start(gains[:], A["gains"]).then_inc(s_small, 16)
            act_.dma_start(conv[:], A["conv"]).then_inc(s_small, 16)
            act_.dma_start(x[:], A["xT"]).then_inc(s_x, 16)
            act_.wait_ge(s_small, SMALL)

            def round_piece(s, i, j):
                k, kt = s.n.slot(j), s.pieces[j]
                act_.wait_ge(landed[k], s.n.landings(i, j))
                if s.n.base + j >= RING:
                    act_.wait_ge(piece_done, s.n(i, j - RING + 1))
                act(hi[k][:, 0:kt * P], raw[k][:, 0:kt * P], ACT.Copy).then_inc(hi_done, 1)

            def take_cross(s, i, last_piece=None):
                act_.wait_ge(piece_done, s.n(i) if s is not None else PIECES_ALL)
                b = (s.c.base - 1) % 2 if s is not None else (CHUNKS - 1) % 2
                c = 2 * NC if s is not None and s.prev[0] == "hid" else T
                act(cross[:, b, 0:c], gb[b][:, c:2 * c], ACT.Copy).then_inc(cross_done, 1)

            def square_root(src):
                act(root[:], src, ACT.Sqrt, bias=col(C_EPS), scale=1.0 / D).then_inc(root_ready, 1)

            def stats(k):
                src = memT if k == 0 else x
                if k == 0:
                    act_.wait_ge(s_mem, 16)
                if k == 1:
                    act_.wait_ge(s_x, 16)
                for c in range(DT):
                    if k >= 2:
                        act_.wait_ge(xn_ready, DT * (k - 2) + c + 1)
                    if DT * k + c >= 4:
                        act_.wait_ge(sq_read, DT * k + c - 3)
                    act(sq[:, c % 4, :], src[:, c, :], ACT.Square).then_inc(sq_ready, 1)
                act_.wait_ge(sq_read, DT * (k + 1))
                square_root(SB[:, T:2 * T])

            def apply_norm(k):
                for c in range(DT):
                    act_.wait_ge(hf_ready, DT * k + c + 1)
                    act(dest[APPLY[k][3]][:, c, 0, :], hf[:, c % 4, :], ACT.Copy).then_inc(hh_ready, 1)

            def post(k):
                act_.wait_ge(post_stat, k + 1)
                square_root(SB[:, 0:T])

            def stickA(i, a):
                hd, p = a
                act_.wait_ge(z_ready, hd(i, 1))
                me.done(act(ab[:], SA[:, 0:384], ACT.Abs, scale=SCALE))
                nc.scalar.sem_inc(abs_ready, 1)
                me.done(act(ex[:], ab[:], ACT.Exp, scale=-1.0))
                act(ln[:], ex[:], ACT.Ln, bias=1.0).then_inc(ln_ready, 1)

            def stickB(i, a):
                hd, p = a
                act_.wait_ge(c_ready, hd(i, 1))
                act(aw[:], SA[:, 0:384], ACT.Exp, scale=SCALE).then_inc(a_ready, 1)

            def memA(i, g):
                act_.wait_ge(mb_ready, g + 1)
                for t in range(2):
                    m = act(pms[g // MEM_HEADS][:, t, :], SB[:, t * T:(t + 1) * T], ACT.Exp, bias=nb[:, t:t + 1],
                            scale=SCALE, accum_out=sums[:, t:t + 1])
                    m.then_inc(me_ready, 1)

            def memB(i, g):
                act_.wait_ge(mt_ready, g + 1)
                act(ptms[g // MEM_HEADS][:].rearrange("p a t -> p (a t)"), TA[:, :], ACT.Copy).then_inc(mpt_ready, 1)

            def tables(_):
                act_.wait_ge(red_ready, 1)
                act(sinT[:], ub[:], ACT.Sin).then_inc(trig_ready, 1)
                me.done(act(us[:], ub[:], ACT.Abs))
                act(cosT[:], us[:], ACT.Sin, scale=-1.0, bias=col(C_HALFPI)).then_inc(trig_ready, 1)

            def blocks(k):
                act_.wait_ge(blkf_ready, k + 1)
                act(blk[k][:, :, 0, :], (blkf0, blkf1)[k][:], ACT.Copy).then_inc(blkh_ready, 1)

            def hidden(k):
                act_.wait_ge(hid_ready, k + 1)
                act(ehid[:, 0, :], hid[:, k % 2, :], ACT.Exp, scale=-1.0).then_inc(hexp_ready, 1)

            def gates():
                act_.wait_ge(x_written, 25)
                act(eg[:], XB[:, 0:T].rearrange("p (t c) -> p t c", t=2)[:, :, 0:36], ACT.Exp, scale=-1.0)\
                    .then_inc(gexp_ready, 1)

            def nsaA(i, hd):
                act_.wait_ge(nb_ready, hd + 1)
                spans = [(ps_c[:, 0, 0:NC], SA[:, 384:384 + NC]), (ps_c[:, 1, 0:NC], SA[:, 400:400 + NC]),
                         (ps_s[:, 0:P], SA[:, 0:P]), (ps_s[:, P:384], SA[:, P:384]),
                         (ps_w[:, 0:P], SB[:, 0:P]), (ps_w[:, P:384], SB[:, P:384])]
                for k, (dst, src) in enumerate(spans):
                    act(dst, src, ACT.Exp, bias=nb[:, k:k + 1], scale=SCALE, accum_out=sums[:, k:k + 1])\
                        .then_inc(ne_ready, 1)

            def nsaB(i, hd):
                act_.wait_ge(nt_ready, hd + 1)
                act(pt_s[:], TA[:, 0:384], ACT.Copy).then_inc(npt_act, 1)

            def silu(l, f, i):
                act_.wait_ge(conv_ready, FT * l + 1 + f if isinstance(f, int) else f + (FT * l + 1))
                act(sg[:], cv[:, 2, :], ACT.Silu).then_inc(silu_ready, 1)

            steps = {
                "stats": lambda i, a: stats(a), "apply": lambda i, a: apply_norm(a), "post": lambda i, a: post(a),
                "stickA": stickA, "stickB": stickB, "memA": memA, "memB": memB, "tables": lambda i, a: tables(a),
                "blocks": lambda i, a: blocks(a), "gates": lambda i, a: gates(), "nsaA": nsaA, "nsaB": nsaB}

            for rounds, slots in PLAN:
                def body(i):
                    for s in slots:
                        first = min(len(s.pieces), RING)
                        for j in range(first):
                            round_piece(s, i, j)
                        if s.prev:
                            take_cross(s, i)
                            if s.prev[0] == "gate":
                                silu(s.prev[1][0], s.prev[1][1](i), i)
                            if s.prev[0] == "hid":
                                hidden(s.prev[1])
                        for step, a in s.react:
                            if step in steps:
                                steps[step](i, a)
                        for j in range(first, len(s.pieces)):
                            round_piece(s, i, j)
                if rounds:
                    per = 2 * sum(step == "stickA" for s in slots for step, _ in s.react)
                    with act_.Fori(0, rounds) as i, me.rounds(rounds, i, per):
                        body(i)
                else:
                    body(None)
            take_cross(None, None)
            post(3)

        @block.vector
        def _(dve):
            tt, ts, stt = nc.vector.tensor_tensor, nc.vector.tensor_scalar, nc.vector.scalar_tensor_tensor
            me = Steps(dve, dve_step)
            dve.wait_ge(s_small, SMALL)

            def split_piece(s, i, j):
                k, kt = s.n.slot(j), s.pieces[j]
                dve.wait_ge(hi_done, s.n(i, j + 1))
                tt(lo[k][:, 0:kt * P], raw[k][:, 0:kt * P], hi[k][:, 0:kt * P].bitcast(F32), ALU.subtract)\
                    .then_inc(lo_done, 1)

            def split_out(dst, k, src):
                def part(n):
                    return dst[:, k, n, :] if isinstance(k, int) else \
                        dst[:, bass.ds(k, 1), n, :].rearrange("p o t -> p (o t)")
                me.done(ts(part(0), src, 1.0, None, ALU.mult))
                return tt(part(1), src, part(0).bitcast(F32), ALU.subtract)

            def take(s, i):
                kind, a = s.prev if s is not None else ("y", (1, 3, At(DT - 1)))
                c = s.c(i) if s is not None else CHUNKS
                b = ((s.c.base if s is not None else CHUNKS) - 1) % 2
                dve.wait_ge(cross_done, c)
                main, cr = gb[b][:, 0:T], cross[:, b, :]
                if kind == "memk":
                    tt(one(km[a[0]], a[1](i)), main, cr, ALU.add).then_inc(evac_done, 1)
                elif kind == "memv":
                    tt(vtmp[:], main, cr, ALU.add).then_inc(evac_done, 1)
                elif kind == "qm":
                    tt(qms[0 if s.w == "in0" else 1][:, a, :], main, cr, ALU.add).then_inc(evac_done, 1)
                elif kind == "qkv":
                    tt({"q": q2, "k": k2, "v": vT2}[a[0]][:, a[1], :], main, cr, ALU.add).then_inc(evac_done, 1)
                elif kind == "v":
                    j = GROUPS * a[0] + a[1]
                    if j:
                        dve.wait_ge(x_written, 20 + j)
                    tt(vtmp1[:], main, cr, ALU.add).then_inc(evac_done, 1)
                elif kind == "vc":
                    tt(vc[:, a, :], main, cr, ALU.add).then_inc(evac_done, 1)
                elif kind == "gates":
                    tt(gt[:], main, cr, ALU.add).then_inc(evac_done, 1)
                elif kind == "rope":
                    n = rope_seen[0]
                    rope_seen[0] += 1
                    if n >= 1:
                        dve.wait_ge(rope_done, n)
                    tt(ub[:], main, cr, ALU.add).then_inc(rope_in, 1)
                    half = P // 2
                    tt(us[0:half], gb[b][half:P, 0:T], cross[half:P, b, :], ALU.add).then_inc(rope_in, 1)
                    tt(us[half:P], gb[b][0:half, 0:T], cross[0:half, b, :], ALU.add).then_inc(evac_done, 1)
                elif kind == "hid":
                    me.done(tt(hid[:, a % 2, :], gb[b][:, 0:2 * NC], cross[:, b, 0:2 * NC], ALU.add))
                    nc.vector.sem_inc(evac_done, 1)
                    nc.vector.sem_inc(hid_ready, 1)
                    dve.wait_ge(hexp_ready, a + 1)
                    me.done(ts(ehid[:, 1, :], ehid[:, 0, :], 1.0, None, ALU.add))
                    me.done(nc.vector.reciprocal(ehid[:, 2, :], ehid[:, 1, :]))
                    tt(hs[:, a // 2, a % 2, :], hid[:, a % 2, :], ehid[:, 2, :], ALU.mult).then_inc(hs_ready, 1)
                elif kind == "y":
                    l, gain, c = a
                    n = DT * (2 * l + (gain == 3))
                    cc = c(i)
                    p = c.base % 2
                    if n + c.base >= 1:
                        dve.wait_ge(yt_read, cc + n)
                    me.done(tt(yt[:, p, :], main, cr, ALU.add))
                    nc.vector.sem_inc(evac_done, 1)
                    nc.vector.sem_inc(yt_ready, 1)
                    me.done(ts(one(y, cc), yt[:, p, :], gains[:, l, gain, bass.ds(cc, 1)], None, ALU.mult))
                elif kind == "gate":
                    l, f = a[0], a[1](i)
                    if l == 0 and a[1].base == 0 and not a[1].step:
                        dve.wait_ge(s_spill, 32)
                    me.done(tt(gp[:, 2:T + 2], main, cr, ALU.add))
                    nc.vector.sem_inc(evac_done, 1)
                    def tap(k):
                        return conv[:, l, f, k:k + 1] if isinstance(f, int) else \
                            conv[:, l, bass.ds(f, 1), k:k + 1].rearrange("p o k -> p (o k)")
                    me.done(ts(cv[:, 0, :], gp[:, 0:T], tap(0), tap(3), ALU.mult, ALU.add))
                    me.done(stt(cv[:, 1, :], gp[:, 1:T + 1], tap(1), cv[:, 0, :], ALU.mult, ALU.add))
                    stt(cv[:, 2, :], gp[:, 2:T + 2], tap(2), cv[:, 1, :], ALU.mult, ALU.add).then_inc(conv_ready, 1)
                elif kind == "up":
                    l, f = a[0], a[1](i)
                    me.done(tt(up[:], main, cr, ALU.add))
                    nc.vector.sem_inc(evac_done, 1)
                    dve.wait_ge(silu_ready, f + (FT * l + 1))
                    me.done(tt(mf[:], up[:], sg[:], ALU.mult))
                    split_out(mid, f, mf[:]).then_inc(mid_done, 1)

            rope_seen = [0]

            def stats(k):
                dve.wait_ge(root_ready, ROOT_S[k])
                me.done(nc.vector.reciprocal(rstd[:], root[:]))

            def apply_norm(k):
                src, l, gain, dst = APPLY[k]
                if k == 2:
                    stats(1)
                src_t, r = (memT, rstd) if src == "mem" else (x, rstd)
                d = dest[dst]

                def low(c):
                    dve.wait_ge(hh_ready, DT * k + c + 1)
                    tt(d[:, c, 1, :], hf[:, c % 4, :], d[:, c, 0, :].bitcast(F32), ALU.subtract).then_inc(h_done, 1)
                for c in range(DT):
                    stt(hf[:, c % 4, :], src_t[:, c, :], gains[:, l, gain, c:c + 1], r[:], ALU.mult, ALU.mult)\
                        .then_inc(hf_ready, 1)
                    if c >= 1:
                        low(c - 1)
                low(DT - 1)

            def post(k):
                dve.wait_ge(root_ready, ROOT_P[k])
                me.done(nc.vector.reciprocal(rstd[:], root[:]))
                for c in range(DT):
                    me.done(tt(hf[:, c % 4, :], y[:, c, :], rstd[:], ALU.mult))
                    tt(x[:, c, :], x[:, c, :], hf[:, c % 4, :], ALU.add).then_inc(xn_ready, 1)
                if k < 3:
                    dve.wait_ge(xn_ready, DT * (k + 1))

            def vcopy(i, a):
                l, k, u = a
                k = k(i) if isinstance(k, At) else k
                dve.wait_ge(x_written, u(i, 1))
                dst = vm[l][:, :, k, :] if isinstance(k, int) else \
                    vm[l][:, :, bass.ds(k, 1), :].rearrange("p s o d -> p s (o d)")
                ts(dst, XB[:, 0:T].rearrange("p (s d) -> p s d", s=2), 1.0, None, ALU.mult).then_inc(x_read, 1)

            def vcopy1(i, a):
                w, g, u = a
                dve.wait_ge(x_written, u + 1)
                nc.vector.tensor_copy(vT[:, w, g, :, :], XB[:, 0:T].rearrange("p (s d) -> p s d", s=2))\
                    .then_inc(x_read, 1)

            def stickA(i, a):
                hd, p = a
                dve.wait_ge(x_written, hd(i, 9))
                me.done(nc.vector.tensor_copy(vtok[:], XB[:, 0:T].rearrange("p (s d) -> p s d", s=2)))
                nc.vector.sem_inc(x_read, 1)
                nc.vector.sem_inc(vtok_ready, 1)
                dve.wait_ge(abs_ready, hd(i, 1))
                me.done(ts(rl[:], SA[:, 0:384], 0.0, None, ALU.max))
                dve.wait_ge(ln_ready, hd(i, 1))
                stt(sp[:], ln[:], 1.0 / SCALE, rl[:], ALU.mult, ALU.add).then_inc(sp_ready, 1)

            def stickC(i, a):
                hd, p = a
                dve.wait_ge(pv_ready, hd(i, 1))
                split_out(o, hd(i), OB[:, 0:T]).then_inc(o_done, 1)

            def memA(i, g):
                l = g // MEM_HEADS
                dve.wait_ge(ms_ready, g + 1)
                me.done(nc.vector.reduce_max(mxs[:, 0:2], SB[:].rearrange("p (t m) -> p t m", t=2), AX_X))
                ts(nb[:, 0:2], mxs[:, 0:2], -SCALE, None, ALU.mult).then_inc(mb_ready, 1)
                dve.wait_ge(me_ready, 2 * g + 2)
                me.done(nc.vector.reciprocal(rs[:, 0:2], sums[:, 0:2]))
                for t in range(2):
                    m = ts(pms[l][:, t, :], pms[l][:, t, :], rs[:, t:t + 1], None, ALU.mult)
                    me.done(m)
                nc.vector.sem_inc(mp_ready, 1)

            def memC(i, g):
                dve.wait_ge(mo_ready, g + 1)
                split_out(o, HEADS + g % MEM_HEADS, TB[:, 0:T]).then_inc(o_done, 1)

            def tables(_):
                dve.wait_ge(s_l1, 16 * 5)
                me.done(nc.vector.tensor_copy(rb[:], ra[:].bitcast(I32)))
                me.done(ts(ub[:], rb[:], col(C_FREQ), None, ALU.mult))
                me.done(ts(us[:], ub[:], float(1 / (2 * np.pi)), None, ALU.mult))
                me.done(ts(ra[:], us[:], MAGIC, None, ALU.add))
                me.done(ts(us[:], ra[:], MAGIC, None, ALU.subtract))
                for part in TWO_PI_PARTS:
                    me.done(stt(rb[:], us[:], -part, ub[:], ALU.mult, ALU.add))
                    me.done(nc.vector.tensor_copy(ub[:], rb[:]))
                me.done(ts(ub[:], ub[:], 3.1415925, -3.1415925, ALU.min, ALU.max))
                nc.vector.sem_inc(red_ready, 1)
                dve.wait_ge(trig_ready, 2)
                me.done(ts(sinT[:], sinT[:], col(C_SIGN), None, ALU.mult))

            def blocks(k):
                u, bf = (kc, vc)[k], (blkf0, blkf1)[k]
                if k == 0:
                    dve.wait_ge(rope_done, 2)
                for g in range(GROUPS):
                    v = u[:, g, :].rearrange("p (c b) -> p b c", b=CMP_STRIDE)
                    for a in range(2):
                        js = slice(a * CMP_STRIDE, (a + 1) * CMP_STRIDE)
                        me.done(tt(bf[:, js, g * NC:(g + 1) * NC], v[:, :, a:a + NC],
                                   pe[:, k, js].rearrange("p (j o) -> p j o", o=1).broadcast_to((P, CMP_STRIDE, NC)),
                                   ALU.add))
                nc.vector.sem_inc(blkf_ready, 1)
                dve.wait_ge(blkh_ready, k + 1)
                tt(blk[k][:, :, 1, :], bf[:], blk[k][:, :, 0, :].bitcast(F32), ALU.subtract).then_inc(blk_done, 1)

            def gates():
                dve.wait_ge(gexp_ready, 1)
                nc.vector.sem_inc(x_read, 1)
                me.done(ts(eg[:], eg[:], 1.0, None, ALU.add))
                me.done(nc.vector.reciprocal(G[:].rearrange("p h b t -> p t (h b)"), eg[:]))

            def kcmp_copy():
                dve.wait_ge(x_written, 26)
                me.done(nc.vector.tensor_copy(kcmp[:].rearrange("p g c -> p (g c)"), XB[:, 0:2 * NC]))
                nc.vector.sem_inc(x_read, 1)
                nc.vector.sem_inc(cmp_ready, 1)

            def vcmp_copy():
                dve.wait_ge(x_written, 27)
                me.done(nc.vector.tensor_copy(vcmp[0:NC].rearrange("p g d -> p (g d)"), XB[0:NC, 0:T]))
                nc.vector.sem_inc(x_read, 1)
                nc.vector.sem_inc(cmp_ready, 1)

            def nsaA(i, hd):
                dve.wait_ge(ns_ready, hd + 1)
                rm = nc.vector.reduce_max
                rm(mxs[:, 0:2], SA[:, 384:416].rearrange("p (t c) -> p t c", t=2)[:, :, 0:NC], AX_X)
                rm(mxs[:, 2:3], SA[:, 0:P], AX_X)
                rm(mxs[:, 3:4], SA[:, P:384], AX_X)
                rm(mxs[:, 4:5], SB[:, 0:P], AX_X)
                me.done(rm(mxs[:, 5:6], SB[:, P:384], AX_X))
                ts(nb[:, 0:6], mxs[:, 0:6], GUARD, -SCALE, ALU.max, ALU.mult).then_inc(nb_ready, 1)
                dve.wait_ge(ne_ready, 6 * hd + 6)
                me.done(ts(guard[:, 0:6], sums[:, 0:6], 1e-30, None, ALU.max))
                me.done(nc.vector.reciprocal(rs[:, 0:6], guard[:, 0:6]))
                me.done(tt(wgt[:, 0:6], rs[:, 0:6], G[:, hd, :, :].rearrange("p b t -> p (b t)"), ALU.mult))
                parts = [ps_c[:, 0, 0:NC], ps_c[:, 1, 0:NC], ps_s[:, 0:P], ps_s[:, P:384], ps_w[:, 0:P], ps_w[:, P:384]]
                for k, part in enumerate(parts):
                    m = ts(part, part, wgt[:, k:k + 1], None, ALU.mult)
                m.then_inc(np_ready, 1)

            def nsaB(i, hd):
                dve.wait_ge(nt_ready, hd + 1)
                nc.vector.tensor_copy(pt_w[:], TB[:, 0:384])
                nc.vector.tensor_copy(pt_c[0:NC].rearrange("p a b -> p (a b)"), XB[0:NC, 0:T]).then_inc(npt_dve, 1)

            def nsaC(i, hd):
                dve.wait_ge(pv_ready, HEADS + hd + 1)
                split_out(o, hd, OB[:, 0:T]).then_inc(o_done, 1)

            steps = {
                "stats": lambda i, a: None if a == 1 else stats(a), "apply": lambda i, a: apply_norm(a),
                "post": lambda i, a: post(a), "vcopy": vcopy, "vcopy1": vcopy1, "stickA": stickA, "stickC": stickC,
                "memA": memA, "memC": memC, "tables": lambda i, a: tables(a), "blocks": lambda i, a: blocks(a),
                "gates": lambda i, a: gates(), "kcmp": lambda i, a: kcmp_copy(), "vcmp": lambda i, a: vcmp_copy(),
                "nsaA": nsaA, "nsaB": nsaB, "nsaC": nsaC}
            PER_TAKE = {"y": 2, "gate": 3, "up": 3}
            PER_STEP = {"stickA": 2, "stickC": 1}

            for rounds, slots in PLAN:
                def body(i):
                    for s in slots:
                        first = min(len(s.pieces), RING)
                        for j in range(first):
                            split_piece(s, i, j)
                        if s.prev:
                            take(s, i)
                        for step, a in s.react:
                            if step in steps:
                                steps[step](i, a)
                        for j in range(first, len(s.pieces)):
                            split_piece(s, i, j)
                if slots[0].w in ("ffn0", "ffn1") and not rounds:
                    pad_needed = True
                else:
                    pad_needed = False
                if rounds:
                    per = sum(PER_TAKE.get(s.prev[0], 0) + sum(PER_STEP.get(step, 0) for step, _ in s.react)
                              for s in slots)
                    with dve.Fori(0, rounds) as i, me.rounds(rounds, i, per):
                        body(i)
                elif pad_needed:
                    for s in slots:
                        for j in range(len(s.pieces)):
                            split_piece(s, None, j)
                        if s.prev[0] == "gate":
                            me.done(nc.vector.memset(gp[:, 0:2], 0.0))
                        take(s, None)
                        for step, a in s.react:
                            steps[step](None, a)
                else:
                    body(None)
            take(None, None)
            post(3)

        @block.gpsimd
        def _(pool):
            tt = nc.gpsimd.tensor_tensor
            me = Steps(pool, pool_step)

            def squares(n, i, c):
                p = c.base % 2
                pool.wait_ge(yt_ready, c(i, n + 1))
                if c.base == 0:
                    me.done(tt(acc[:], yt[:, p, :], yt[:, p, :], ALU.mult))
                    nc.gpsimd.sem_inc(yt_read, 1)
                else:
                    me.done(tt(sq1[:], yt[:, p, :], yt[:, p, :], ALU.mult))
                    nc.gpsimd.sem_inc(yt_read, 1)
                    me.done(tt(acc[:], acc[:], sq1[:], ALU.add))
                nc.gpsimd.sem_inc(acc_done, 1)

            def rotate(k, dst):
                pool.wait_ge(rope_in, 2 * k + 2)
                pool.wait_ge(trig_ready, 2)
                me.done(tt(ra[:], ub[:], cosT[:], ALU.mult))
                me.done(tt(rb[:], us[:], sinT[:], ALU.mult))
                tt(dst, ra[:], rb[:], ALU.add).then_inc(rope_done, 1)

            ropes = 0
            for rounds, slots in PLAN:
                if slots[0].w == "in0" and not rounds:
                    pool.wait_ge(evac_done, 16)
                    pool.wait_ge(x_read, 8)
                    pool.dma_start(A["spill_k"], km1[:]).then_inc(s_spill, 16)
                    pool.dma_start(A["spill_v"], vm1[:]).then_inc(s_spill, 16)
                todo = [s for s in slots if s.prev and s.prev[0] in ("y", "rope")]
                if not todo:
                    continue

                def body(i):
                    nonlocal ropes
                    for s in todo:
                        if s.prev[0] == "y":
                            l, gain, c = s.prev[1]
                            squares(DT * (2 * l + (gain == 3)), i, c)
                        else:
                            pool.wait_ge(evac_done, s.c(i))
                            rotate(ropes, ROPE_DEST[s.prev[1]])
                            ropes += 1
                if rounds:
                    with pool.Fori(0, rounds) as i, me.rounds(rounds, i, 2 * len(todo)):
                        body(i)
                else:
                    body(None)
            squares(3 * DT, None, At(DT - 1))


def kernel(x, mem, positions, norm_g, w_in_sb, w_in_nsa, cmp_pe, cmp_w1, cmp_w2, w_mem_kv, w_o,
           w_ffn_gate, w_ffn_up, ffn_conv_w, ffn_conv_b, w_ffn_down):
    import ml_dtypes
    import concourse.bacc as bacc
    from concourse.bass_utils import run_bass_kernel_spmd as run

    def tiles(w):
        k, n = w.shape
        return w.reshape(k // P, P, n // P, P).transpose(2, 1, 0, 3)

    def feature_major(a):
        return np.ascontiguousarray(np.asarray(a)[0].T.reshape(DT, P, T).transpose(1, 0, 2))

    consts = np.zeros((P, C_COLS), np.float32)
    consts[:, C_ONES:C_ONES + P] = 1
    consts[:, C_IDENT:C_IDENT + P] = np.eye(P)
    consts[:, C_NEGL:C_NEGL + P] = -np.tril(np.ones((P, P)))
    consts[:, C_NEGONES:C_NEGONES + P] = -1
    freq = (10000.0 ** (-np.arange(0, P, 2) / P)).astype(np.float32)
    consts[:, C_FREQ] = np.concatenate([freq, freq])
    consts[:, C_SIGN] = np.repeat([-1.0, 1.0], P // 2)
    consts[:, C_EPS] = EPS
    consts[:, C_HALFPI] = np.pi / 2
    masks = np.zeros((P, M_COLS), np.float32)
    masks[:, M_IDENT:M_IDENT + P] = np.eye(P)
    masks[:, M_STICK:M_STICK + P] = NEG * np.tril(np.ones((P, P)))
    masks[:, M_CAUSAL:M_CAUSAL + P] = NEG * np.triu(np.ones((P, P)), 1)
    end = np.arange(NC) * CMP_STRIDE + CMP_LEN - 1
    for t in range(2):
        masks[:, M_CMP + 16 * t:M_CMP + 16 * t + NC] = NEG * (end[None, :] > (t * P + np.arange(P))[:, None])

    w_in_sb, w_in_nsa, w_mem_kv, w_o = (np.asarray(a) for a in (w_in_sb, w_in_nsa, w_mem_kv, w_o))
    w_ffn_gate, w_ffn_up, w_ffn_down = (np.asarray(a) for a in (w_ffn_gate, w_ffn_up, w_ffn_down))
    cmp_w1, cmp_w2, cmp_pe = (np.asarray(a) for a in (cmp_w1, cmp_w2, cmp_pe))
    sb = tiles(w_in_sb[0])
    order = [3 * HEADS + g for g in range(MEM_HEADS)] + [j * HEADS + hd for hd in range(HEADS) for j in range(3)]
    arrays = {"in0": sb[order]}
    q_cols, kv_cols = HEADS * P, GROUPS * P
    nsa = w_in_nsa[0]
    parts = {n: nsa[:, q_cols + j * kv_cols:q_cols + (j + 1) * kv_cols]
             for j, n in enumerate(("kc", "vc", "ks", "vs", "kw", "vw"))}
    g0 = q_cols + 6 * kv_cols
    gates = np.concatenate([nsa[:, g0:g0 + 3 * HEADS], np.zeros((D, P - 3 * HEADS), np.float32)], 1)
    arrays["in1"] = tiles(np.concatenate(
        [parts[n] for n in ("kc", "vc", "vs", "vw", "ks", "kw")] + [gates, nsa[:, g0 + 3 * HEADS:], nsa[:, :q_cols]], 1))
    for l in range(2):
        m = tiles(w_mem_kv[l])
        arrays[f"mem{l}"] = m[[j * MEM_HEADS + g for g in range(MEM_HEADS) for j in range(2)]]
        arrays[f"out{l}"] = tiles(w_o[l])
        arrays[f"ffn{l}"] = np.stack([tiles(w_ffn_gate[l]), tiles(w_ffn_up[l])], 1).reshape(2 * FT, P, DT, P)
        arrays[f"down{l}"] = tiles(w_ffn_down[l])
    arrays["cmp"] = np.concatenate([tiles(cmp_w1[0, k]) for k in range(2)])
    arrays["cmp_w2"] = cmp_w2[0].reshape(2, 2, P, P).transpose(2, 0, 1, 3)
    arrays["cmp_pe"] = cmp_pe[0].transpose(2, 0, 1)
    arrays["gains"] = np.asarray(norm_g).reshape(2, 5, DT, P).transpose(3, 0, 1, 2)
    arrays["conv"] = np.concatenate([np.asarray(ffn_conv_w), np.asarray(ffn_conv_b)[:, None]], 1)\
        .reshape(2, 4, FT, P).transpose(3, 0, 2, 1)
    arrays["positions"] = np.broadcast_to(np.asarray(positions), (P, T))
    arrays["consts"] = consts
    arrays["masks"] = masks.astype(ml_dtypes.bfloat16)
    arrays["xT"], arrays["memT"] = feature_major(x), feature_major(mem)

    nc = bacc.Bacc("TRN2", target_bir_lowering=False, num_devices=1)
    arrays = {n: np.ascontiguousarray(a) for n, a in arrays.items()}
    A = {n: nc.dram_tensor("in_" + n, a.shape, mybir.dt.from_np(a.dtype), kind="ExternalInput").ap()
         for n, a in arrays.items()}
    A["spill_k"] = nc.dram_tensor("spill_k", (P, MEM_HEADS, T), F32, kind="Internal").ap()
    A["spill_v"] = nc.dram_tensor("spill_v", (P, 2, MEM_HEADS, P), F32, kind="Internal").ap()
    A["out"] = nc.dram_tensor("out", (P, DT, T), F32, kind="ExternalOutput").ap()
    build(nc, A)
    got = run(nc, [{"in_" + n: a for n, a in arrays.items()}], core_ids=[0]).results[0]["out"]
    return np.ascontiguousarray(got.transpose(2, 1, 0)).reshape(1, T, D)
```

```python
from contextlib import ExitStack, contextmanager

import numpy as np

import concourse.bass as bass
from concourse import mybir

F32 = mybir.dt.float32
F32R = mybir.dt.float32r
BF16 = mybir.dt.bfloat16
I32 = mybir.dt.int32
ACT = mybir.ActivationFunctionType
ALU = mybir.AluOpType
AX_X = mybir.AxisListType.X

P = 128
T = 256
D = 2048
DT = D // P
DFF = 5632
FT = DFF // P
HEADS, MEM_HEADS, GROUPS = 12, 4, 2
HPG = HEADS // GROUPS
CMP_STRIDE, CMP_LEN = 16, 32
NC = T // CMP_STRIDE - 1
SCALE = P ** -0.5
EPS = 1e-6
NEG = -1e30
GUARD = -1e29
RING = 4
PIECE = 8
LEAD = 2
K16 = (8, 8)
K32 = (8, 8, 8, 8)
K44 = (8, 8, 7, 7, 7, 7)
MAGIC = 1.5 * 2.0 ** 23
TWO_PI_PARTS = (6.28125, 1.93500518798828125e-3, 3.01991598e-7)

C_ONES, C_IDENT, C_NEGL, C_NEGONES = 0, P, 2 * P, 3 * P
C_FREQ, C_SIGN, C_EPS, C_HALFPI = (4 * P + k for k in range(4))
C_COLS = 4 * P + 4
M_IDENT, M_STICK, M_CAUSAL, M_CMP = 0, P, 2 * P, 3 * P
M_COLS = 3 * P + 2 * CMP_STRIDE


class At:

    def __init__(self, base, step=0):
        self.base, self.step = base, step

    def __call__(self, i, k=0):
        return self.base + k if i is None or not self.step else i * self.step + (self.base + k)

    def slot(self, k=0):
        return (self.base + k) % RING

    def landings(self, i, k=0):
        first = 16 * ((self.base + k) // RING + 1)
        return first if i is None or not self.step else i * (16 * self.step // RING) + first


class Slot:

    def __init__(self, prev=None, w=None, chunk=None, pieces=None, operand=None, gate=None, order=None,
                 before=(), after=(), react=(), hooks=None):
        self.w, self.chunk, self.pieces = w, chunk, pieces
        self.c = self.n = None
        self.operand = operand
        self.prev = prev
        self.gate = gate
        self.order = order
        self.before, self.after, self.react = before, after, react
        self.hooks = hooks or {}
        self.ahead = self.rest = None


def schedule():
    plan = []
    state = {"c": 0, "n": 0}

    def add(rounds, slots):
        chunks, pieces = len(slots), sum(len(s.pieces) for s in slots)
        if rounds:
            assert chunks % 2 == 0 and pieces % RING == 0
        for s in slots:
            s.c = At(state["c"], chunks if rounds else 0)
            s.n = At(state["n"], pieces if rounds else 0)
            state["c"] += 1
            state["n"] += len(s.pieces)
            s.ahead = range(LEAD if state["n"] > len(s.pieces) else 0, RING)
            s.rest = range(RING, len(s.pieces) + LEAD)
        if rounds:
            state["c"] += chunks * (rounds - 1)
            state["n"] += pieces * (rounds - 1)
        plan.append((rounds, slots))

    for l in range(2):
        last = None if l == 0 else ("memv", (0, At(3)))
        k0 = Slot(w=f"mem{l}", chunk=At(0), pieces=K16, operand=f"amem{l}", prev=last)
        v0 = Slot(w=f"mem{l}", chunk=At(1), pieces=K16, operand=f"amem{l}", prev=("memk", (l, At(0))))
        if l == 0:
            k0.react, k0.gate = [("feed", 0)], ("h", 0, 0)
            v0.react = [("feed", 1)]
        else:
            k0.after, k0.react, k0.gate = [("vT", At(3))], [("feed", 2)], ("h", 1, None)
            v0.react = [("vcopy", (0, 3, At(3))), ("feed", 3)]
        add(None, [k0, v0])
        add(3, [
            Slot(w=f"mem{l}", chunk=At(2, 2), pieces=K16, operand=f"amem{l}", prev=("memv", (l, At(0, 1))),
                 after=[("vT", At(4 * l, 1))]),
            Slot(w=f"mem{l}", chunk=At(3, 2), pieces=K16, operand=f"amem{l}", prev=("memk", (l, At(1, 1))),
                 react=[("vcopy", (l, At(0, 1), At(4 * l, 1)))]),
        ])

    extra = {}
    for g in range(MEM_HEADS):
        extra.setdefault(g + 1, ([], []))[0].append(("memA", g))
        extra.setdefault(g + 2, ([], []))[0].append(("memB", g))
        extra.setdefault(g + 2, ([], []))[1].append(("memA", g))
        extra.setdefault(g + 3, ([], []))[0].append(("memC", g))
        extra.setdefault(g + 3, ([], []))[1].append(("memB", g))
        extra.setdefault(g + 4, ([], []))[1].append(("memC", g))
    rank = {"memC": 0, "memB": 1, "memA": 2}

    def ordered(steps):
        return sorted(steps, key=lambda s: rank[s[0]])

    def memory_steps(k):
        after, react = extra.get(k, ([], []))
        return ordered(after), ordered(react)[::-1]

    slots = []
    for g in range(MEM_HEADS):
        after, react = memory_steps(g)
        slots.append(Slot(w="in0", chunk=At(g), pieces=K16, operand="h", after=after, react=react,
                          prev=("memv", (1, At(3))) if g == 0 else ("qm", g - 1)))
    slots[0].after = [("vT", At(7))] + slots[0].after
    slots[0].gate, slots[0].react = ("h", 2, 1), [("feed", 4)]
    slots[1].react = [("vcopy", (1, 3, At(7)))] + slots[1].react
    for h in range(2):
        for j, kind in enumerate("qkv"):
            after, react = memory_steps(4 + 3 * h + j)
            prev = ("qm", 3) if (h, j) == (0, 0) else ("qkv", ("vqk"[j], (h if j else h - 1) % 2))
            slots.append(Slot(w="in0", chunk=At(4 + 3 * h + j), pieces=K16, operand="h", prev=prev,
                              after=after, react=react))
    for j, s in enumerate(slots[7:]):
        s.after = s.after + [("stick" + "ABC"[j], (At(0), 0))]
        if j:
            s.react = s.react + [("stick" + "AB"[j - 1], (At(0), 0))]
    add(None, slots)
    slots = []
    for h in range(2):
        p, q = h % 2, (h + 1) % 2
        before, this = (At(2 + h - 1, 2), q), None
        slots += [
            Slot(prev=("qkv", ("v", q)), after=[("stickA", before)], react=[("stickC", (At(h, 2), p))]),
            Slot(prev=("qkv", ("q", p)), after=[("stickB", before)], react=[("stickA", before)]),
            Slot(prev=("qkv", ("k", p)), after=[("stickC", before)], react=[("stickB", before)]),
        ]
    for j, s in enumerate(slots):
        s.w, s.chunk, s.pieces, s.operand = "in0", At(10 + j, 6), K16, "h"
    add(5, slots)

    def out_projection(l, first, second):
        first.w = second.w = f"out{l}"
        first.order = {0: [0, 1, 2, 3, 4, 5, 6, 7, 8, 9, 12, 13, 14, 15, 10, 11]}[0]
        first.gate = ("o", l)
        for k, s in enumerate((first, second)):
            s.chunk, s.pieces, s.operand = At(k), K16, "o"
        add(None, [first, second])
        add(7, [Slot(w=f"out{l}", chunk=At(2 + k, 2), pieces=K16, operand="o", prev=("y", (l, 1, At(1 + k, 2))))
                for k in range(2)])

    def ffn(l):
        gate0 = Slot(w=f"ffn{l}", chunk=At(0), pieces=K16, operand="h", prev=("y", (l, 1, At(DT - 1))),
                     before=[("post", 2 * l)], gate=("h", 3 + 2 * l, 2 + 2 * l),
                     react=[("post", 2 * l), ("feed", 5 + 2 * l)])
        up0 = Slot(w=f"ffn{l}", chunk=At(1), pieces=K16, operand="h", prev=("gate", (l, At(0))))
        add(None, [gate0, up0])
        add(FT - 1, [
            Slot(w=f"ffn{l}", chunk=At(2, 2), pieces=K16, operand="h", prev=("up", (l, At(0, 1)))),
            Slot(w=f"ffn{l}", chunk=At(3, 2), pieces=K16, operand="h", prev=("gate", (l, At(1, 1)))),
        ])
        add(None, [
            Slot(w=f"down{l}", chunk=At(0), pieces=K44, operand="mid", prev=("up", (l, At(FT - 1))),
                 gate=("mid", l)),
            Slot(w=f"down{l}", chunk=At(1), pieces=K44, operand="mid", prev=("y", (l, 3, At(0)))),
        ])
        add(7 - l, [Slot(w=f"down{l}", chunk=At(2 + k, 2), pieces=K44, operand="mid",
                         prev=("y", (l, 3, At(1 + k, 2)))) for k in range(2)])
        if l:
            last = [Slot(w=f"down{l}", chunk=At(DT - 2 + k), pieces=K44, operand="mid",
                         prev=("y", (l, 3, At(DT - 3 + k)))) for k in range(2)]
            add(None, last)
            last[1].rest = range(RING, len(K44))

    h11 = (At(11), 1)
    out_projection(
        0,
        Slot(prev=("qkv", ("v", 1)), react=[("stickC", (At(10), 0)), ("stickA", h11), ("stickB", h11), ("stickC", h11)],
             hooks={8: [("stickA", h11)], 10: [("stickB", h11)], 11: [("stickC", h11)]}),
        Slot(prev=("y", (0, 1, At(0)))))
    ffn(0)

    kinds = [("vc", 0), ("vc", 1), ("v", (0, 0)), ("v", (0, 1)), ("v", (1, 0)), ("v", (1, 1)),
             ("rope", "kc0"), ("rope", "kc1"), ("rope", "ks0"), ("rope", "ks1"), ("rope", "kw0"), ("rope", "kw1"),
             ("gates", 0)]
    kinds += [("qm", g) for g in range(MEM_HEADS)] + [("hid", k) for k in range(4)]
    kinds += [("rope", f"q{h % 2}") for h in range(HEADS)]
    slots = []
    cmp0, q0 = 17, 21
    for k in range(q0 + HEADS):
        s = Slot(prev=kinds[k - 1] if k else ("y", (0, 3, At(DT - 1))))
        if cmp0 <= k < q0:
            s.w, s.chunk, s.pieces, s.operand = "cmp", At(k - cmp0), K32, f"blk{(k - cmp0) // 2}"
        else:
            s.w, s.chunk, s.pieces, s.operand = "in1", At(k if k < cmp0 else k - 4), K16, "h"
        s.after, s.react = [], []
        slots.append(s)
    slots[0].before, slots[0].gate = [("post", 1)], ("h", 4, 3)
    slots[0].react = [("post", 1), ("feed", 6)]
    slots[1].react.append(("angles", 0))
    slots[4].react.append(("trig", 0))
    slots[5].react.append(("tables", 0))
    for j, (w, g) in enumerate([(0, 0), (0, 1), (1, 0), (1, 1)]):
        slots[3 + j].after.append(("vT", At(20 + j)))
        slots[4 + j].react.append(("vcopy1", (w, g, 20 + j)))
    slots[2].react.append(("windows", 1))
    slots[3].react.append(("blocks", (1, 1)))
    slots[8].react.append(("windows", 0))
    slots[10].react.append(("blocks", (0, 2)))
    slots[13].after.append(("gatesT", 24))
    slots[14].react.append(("gates", 24))
    for g in range(MEM_HEADS):
        slots[14 + g].after.append(("memA", 4 + g))
        slots[15 + g].after.append(("memB", 4 + g))
        slots[15 + g].react.append(("memA", 4 + g))
        slots[16 + g].after.append(("memC", 4 + g))
        slots[16 + g].react.append(("memB", 4 + g))
        slots[17 + g].react.append(("memC", 4 + g))
    for s in slots:
        mem = [x for x in s.after if x[0] in rank]
        s.after = [x for x in s.after if x[0] not in rank] + ordered(mem)
        mem = [x for x in s.react if x[0] in rank]
        s.react = [x for x in s.react if x[0] not in rank] + ordered(mem)[::-1]
    slots[19].after.append(("kcmp", 25))
    slots[20].react.append(("kcmp", 25))
    slots[21].after.append(("vcmp", 26))
    slots[22].react.append(("vcmp", 26))
    for k in range(HEADS):
        s = slots[q0 + k]
        s.after += [("nsa" + x, k - d) for x, d in (("C", 3), ("B", 2), ("A", 1)) if k >= d]
        s.react += [("nsa" + x, k - d) for x, d in (("A", 2), ("B", 3), ("E", 2), ("C", 4), ("S", 2)) if k >= d]
    add(None, slots)
    out_projection(
        1,
        Slot(prev=kinds[-1], before=[("nsaC", 9), ("nsaB", 10)],
             react=[("nsaA", 10), ("nsaB", 9), ("nsaE", 10), ("nsaC", 8), ("nsaS", 10), ("nsaB", 10), ("nsaC", 9),
                    ("nsaA", 11), ("nsaE", 11), ("nsaC", 10), ("nsaS", 11), ("nsaB", 11), ("nsaC", 11)],
             hooks={8: [("nsaC", 10), ("nsaA", 11)], 10: [("nsaB", 11), ("nsaC", 11)]}),
        Slot(prev=("y", (1, 1, At(0)))))
    ffn(1)
    return plan, state["c"], state["n"]


PLAN, CHUNKS, PIECES_ALL = schedule()


class Steps:

    def __init__(self, eng, sem):
        self.eng, self.sem, self.n, self.i, self.per = eng, sem, 0, None, 0

    def value(self):
        return self.n if self.i is None else self.i * self.per + self.n

    def done(self, ins, meanwhile=None):
        ins.then_inc(self.sem, 1)
        self.n += 1
        if meanwhile:
            meanwhile()
        self.eng.wait_ge(self.sem, self.value())

    @contextmanager
    def rounds(self, n, i, per):
        start, self.i, self.per = self.n, i, per
        yield
        assert self.n - start == per, (self.n - start, per)
        self.n, self.i = start + per * n, None


class Filler:

    def __init__(self, split, s, i):
        self.split, self.s, self.i, self.left = split, s, i, list(s.ahead)

    def __call__(self):
        if self.left:
            self.split(self.s, self.i, self.left.pop(0))

    def all(self):
        while self.left:
            self()


def tiles_in(s, j):
    return s.pieces[j] if j < len(s.pieces) else PIECE


def build(nc, A):
    with ExitStack() as ctx:
        def sb(name, shape, dt=F32, stack=ctx):
            return stack.enter_context(nc.sbuf_tensor(name, shape, dt))

        def sem(name):
            return ctx.enter_context(nc.semaphore(name))

        x = sb("x", [P, DT, T])
        with ExitStack() as over:
            sb("h_front", [P, DT, T], F32, over)
            y = sb("y", [P, DT, T], F32, over)
        h = sb("h", [P, DT, 2, T], F32R)
        raw = [sb(f"raw{k}", [P, PIECE * P]) for k in range(RING)]
        hi = [sb(f"hi{k}", [P, PIECE * P], F32R) for k in range(RING)]
        lo = [sb(f"lo{k}", [P, PIECE * P], F32R) for k in range(RING)]
        cross = sb("cross", [P, 2, T])
        cst = sb("cst", [P, C_COLS])
        msk = sb("msk", [P, M_COLS], BF16)
        gains = sb("gains", [P, 2, 5, DT])
        conv = sb("conv", [P, 2, FT, 4])
        acc = sb("acc", [P, T])
        sq1 = sb("sq1", [P, T])
        yt = sb("yt", [P, 2, T])
        root = sb("root", [P, T])
        rpost = sb("rpost", [P, T])
        rx = sb("rx", [P, T])
        vtmp, rmem = acc, sq1
        with ExitStack() as over:
            sq = sb("sq", [P, 4, T], F32, over)
        with ExitStack() as over:
            gp = sb("gp", [P, T + 8], F32, over)
            cv = sb("cv", [P, 3, T], F32, over)
            sg = sb("sg", [P, T], F32, over)
            up = sb("up", [P, T], F32, over)
            sgr = sb("sgr", [P, T], F32, over)
        sb("shared", [P, 7 * T + 8])
        def region(tensors):
            with ExitStack() as over:
                return [sb(n, s, dt, over) for n, s, dt in tensors]

        mid, = region([("mid", [P, FT, 2, T], F32R)])
        o, memT, km0, vm0, amem1 = region([
            ("o", [P, DT, 2, T], F32R), ("memT", [P, DT, T], F32), ("km0", [P, MEM_HEADS, T], F32),
            ("vm0", [P, 2, MEM_HEADS, P], F32), ("amem1", [P, DT, 2, T], F32R)])
        _, km1, vm1 = region([("o_a", [P, DT, 2, T], F32R), ("km1", [P, MEM_HEADS, T], F32),
                              ("vm1", [P, 2, MEM_HEADS, P], F32)])
        (_, _, _, _, qm_0, pm_0, ptm_0, q2, k2, vT2, vtok, ab, ex, ln, rl, sp, aw) = region([
            ("o_b", [P, DT, 2, T], F32R), ("memT_b", [P, DT, T], F32), ("km0_b", [P, MEM_HEADS, T], F32),
            ("vm0_b", [P, 2, MEM_HEADS, P], F32), ("qm_0", [P, MEM_HEADS, T], F32), ("pm_0", [P, 2, T], F32),
            ("ptm_0", [P, 2, T], F32), ("q2", [P, 2, T], F32), ("k2", [P, 2, T], F32), ("vT2", [P, 2, T], F32),
            ("vtok", [P, 2, P], F32), ("ab", [P, 384], F32), ("ex", [P, 384], F32), ("ln", [P, 384], F32),
            ("rl", [P, 384], F32), ("sp", [P, 384], F32), ("aw", [P, 384], F32)])
        with ExitStack() as over:
            (_, km1b, vm1b, cosT, sinT, ub, us, ra, rb, kT, vT, kc, vc, w2, pe, hid, ehid, hs, kcmp, vcmp,
             gt, eg, G, qr, qm_1, pm_1, ptm_1, vtmp1) = [sb(n, shape, F32R if n == "o_c" else F32, over) for n, shape in [
                 ("o_c", [P, DT, 2, T]), ("km1b", [P, MEM_HEADS, T]), ("vm1b", [P, 2, MEM_HEADS, P]),
                 ("cosT", [P, T]), ("sinT", [P, T]), ("ub", [P, T]), ("us", [P, T]), ("ra", [P, T]), ("rb", [P, T]),
                 ("kT", [P, 2, GROUPS, T]), ("vT", [P, 2, GROUPS, 2, P]), ("kc", [P, GROUPS, T]),
                 ("vc", [P, GROUPS, T]), ("w2", [P, 2, 2, P]), ("pe", [P, 2, CMP_LEN]), ("hid", [P, 2, 2 * NC]),
                 ("ehid", [P, 3, 2 * NC]), ("hs", [P, 2, 2, 2 * NC]), ("kcmp", [P, GROUPS, NC]),
                 ("vcmp", [P, GROUPS, P]), ("gt", [P, T]), ("eg", [P, 2, 36]), ("G", [P, HEADS, 3, 2]),
                 ("qr", [P, 2, T]), ("qm_1", [P, MEM_HEADS, T]), ("pm_1", [P, 2, T]), ("ptm_1", [P, 2, T]),
                 ("vtmp1", [P, T])]]
            blkf0, blkf1 = region([("blkf0", [P, CMP_LEN, 2 * NC], F32), ("blkf1", [P, CMP_LEN, 2 * NC], F32)])
            ps_s, ps_w, ps_c, pt_s, pt_w, pt_c = region([
                ("ps_s", [P, 384], F32), ("ps_w", [P, 384], F32), ("ps_c", [P, 2, 16], F32),
                ("pt_s", [P, 384], F32), ("pt_w", [P, 384], F32), ("pt_c", [P, 2, P], F32)])
        blk = region([("blk0", [P, CMP_LEN, 2, 2 * NC], F32R), ("blk1", [P, CMP_LEN, 2, 2 * NC], F32R)])
        sb("region", [P, FT, 2, T], F32R)
        mxs = sb("mxs", [P, 8])
        nb = sb("nb", [P, 8])
        sums = sb("sums", [P, 8])
        guard = sb("guard", [P, 8])
        rs = sb("rs", [P, 8])
        wgt = sb("wgt", [P, 8])
        km, vm = [km0, km1], [vm0, vm1]
        kmem, vmem = [km0, km1b], [vm0, vm1b]
        qms, pms, ptms = [qm_0, qm_1], [pm_0, pm_1], [ptm_0, ptm_1]
        amem = [o, amem1]

        def bank(name):
            return ctx.enter_context(nc.psum_tensor(name, [P, 512], F32))

        gb = [bank("gemm0"), bank("gemm1")]
        SA, SB, TA, TB, OB, XB = (bank(n) for n in ("SA", "SB", "TA", "TB", "OB", "XB"))

        landed = [sem(f"landed{k}") for k in range(RING)]
        hi_done, lo_done, piece_done = sem("hi_done"), sem("lo_done"), sem("piece_done")
        cross_done, evac_done = sem("cross_done"), sem("evac_done")
        s_gains = sem("s_gains")
        s_memq = [sem(f"s_mem{k}") for k in range(4)]
        s_x, s_small = sem("s_x"), sem("s_small")
        s_l1, s_spill = sem("s_l1"), sem("s_spill")
        s_out = sem("s_out")
        dve_step, act_step, pool_step = sem("dve_step"), sem("act_step"), sem("pool_step")
        sq_ready, sq_read = sem("sq_ready"), sem("sq_read")
        post_stat, root_ready, xn_ready = sem("post_stat"), sem("root_ready"), sem("xn_ready")
        hh_ready, h_done = sem("hh_ready"), sem("h_done")
        rpost_ready, rx_ready, yn_ready = sem("rpost_ready"), sem("rx_ready"), sem("yn_ready")
        sgr_ready = sem("sgr_ready")
        yt_ready, yt_read, acc_done = sem("yt_ready"), sem("yt_read"), sem("acc_done")
        x_written, x_read = sem("x_written"), sem("x_read")
        z_ready, ln_ready, sp_ready, c_ready, a_ready = (sem(n) for n in (
            "z_ready", "ln_ready", "sp_ready", "c_ready", "a_ready"))
        pv_ready, o_done, vtok_ready = sem("pv_ready"), sem("o_done"), sem("vtok_ready")
        ms_ready, mb_ready, me_ready, mp_ready, mt_ready, mpt_ready, mo_ready = (sem(n) for n in (
            "ms_ready", "mb_ready", "me_ready", "mp_ready", "mt_ready", "mpt_ready", "mo_ready"))
        conv_ready, silu_ready, mid_done = sem("conv_ready"), sem("silu_ready"), sem("mid_done")
        abs_ready, red_ready, trig_ready = sem("abs_ready"), sem("red_ready"), sem("trig_ready")
        rope_in, rope_done = sem("rope_in"), sem("rope_done")
        blkf_ready, blkh_ready, blk_done = sem("blkf_ready"), sem("blkh_ready"), sem("blk_done")
        hid_ready, hexp_ready, hs_ready = sem("hid_ready"), sem("hexp_ready"), sem("hs_ready")
        gt_ready, gexp_ready = sem("gt_ready"), sem("gexp_ready")
        cmp_ready = sem("cmp_ready")
        ns_ready, nb_ready, ne_ready, np_ready, nt_ready, npt_act, npt_dve = (sem(n) for n in (
            "ns_ready", "nb_ready", "ne_ready", "np_ready", "nt_ready", "npt_act", "npt_dve"))

        ones, ident = cst[:, C_ONES:C_ONES + P], cst[:, C_IDENT:C_IDENT + P]
        neg_l, neg_ones = cst[:, C_NEGL:C_NEGL + P], cst[:, C_NEGONES:C_NEGONES + P]

        def col(c):
            return cst[:, c:c + 1]

        identb, stick_mask = msk[:, M_IDENT:M_IDENT + P], msk[:, M_STICK:M_STICK + P]
        causal_mask = msk[:, M_CAUSAL:M_CAUSAL + P]

        def one(ap, k):
            return ap[:, k, :] if isinstance(k, int) else ap[:, bass.ds(k, 1), :].rearrange("p o t -> p (o t)")

        SMALL = 16 * 3
        ROOT_S, ROOT_P = (1, 2, 4, 6, 8), (3, 5, 7, 9)
        FEEDS = [
            ("mem", 0, 4, "amem0", range(DT), range(DT), None),
            ("mem", 1, 4, "amem1", range(8), (), None), ("mem", 1, 4, "amem1", range(8, DT), (), None),
            ("x", 0, 0, "h", range(8), (), None), ("x", 0, 0, "h", range(8, DT), range(DT), None),
            ("x", 0, 2, "h", range(DT), range(DT), 0), ("x", 1, 0, "h", range(DT), range(DT), 1),
            ("x", 1, 2, "h", range(DT), range(DT), 2)]
        FED = [sum(len(f[4]) for f in FEEDS[:k]) for k in range(len(FEEDS))]
        STATS = [sum(bool(f[5]) for f in FEEDS[:k]) for k in range(len(FEEDS))]
        PAIR_LEAD = 2
        dest = {"amem0": o, "amem1": amem1, "h": h, "o": o, "mid": mid, "blk0": blk[0], "blk1": blk[1]}
        ROPE_DEST = {"kc0": kc[:, 0, :], "kc1": kc[:, 1, :], "ks0": kT[:, 0, 0, :], "ks1": kT[:, 0, 1, :],
                     "kw0": kT[:, 1, 0, :], "kw1": kT[:, 1, 1, :], "q0": qr[:, 0, :], "q1": qr[:, 1, :]}
        L0_DOWN_END = None
        for rounds, slots in PLAN:
            for s in slots:
                if s.w == "down0" and rounds:
                    L0_DOWN_END = s.n.base + len(s.pieces) + s.n.step * (rounds - 1)
        NSLOT = sum((r or 1) * len(s) for r, s in PLAN)
        assert NSLOT == CHUNKS
        block = ctx.enter_context(nc.Block())

        @block.sync
        def _(sp):
            def load(s, i, j, off):
                k = s.n.slot(j)
                if s.n.base + j >= RING:
                    sp.wait_ge(lo_done, s.n(i, j - RING + 1))
                kt = s.pieces[j]
                c = s.chunk(i)
                w = A[s.w]
                src = (w[c] if isinstance(c, int) else w[bass.ds(c, 1)].rearrange("o p k n -> (o p) k n"))
                src = src[:, off:off + kt, :].rearrange("p k n -> p (k n)")
                sp.dma_start(raw[k][:, 0:kt * P], src).then_inc(landed[k], 16)

            def layer1_loads():
                sp.wait_ge(piece_done, L0_DOWN_END)
                sp.wait_ge(s_spill, 32)
                sp.dma_start(km1b[:], A["spill_k"]).then_inc(s_l1, 16)
                sp.dma_start(vm1b[:], A["spill_v"]).then_inc(s_l1, 16)
                sp.dma_start(w2[:], A["cmp_w2"]).then_inc(s_l1, 16)
                sp.dma_start(pe[:], A["cmp_pe"]).then_inc(s_l1, 16)
                sp.dma_start(ra[:].bitcast(I32), A["positions"]).then_inc(s_l1, 16)

            for rounds, slots in PLAN:
                def body(i):
                    for s in slots:
                        off = 0
                        for j in range(len(s.pieces)):
                            load(s, i, j, off)
                            off += s.pieces[j]
                        if s.w == "in1" and s.chunk(i) == 0:
                            layer1_loads()
                if rounds:
                    with sp.Fori(0, rounds) as i:
                        body(i)
                else:
                    body(None)
            for j in range(DT // 2):
                sp.wait_ge(xn_ready, (3 * DT) // 2 + j + 1)
                sp.dma_start(A["out"][:, 2 * j:2 * j + 2, :], x[:, 2 * j:2 * j + 2, :]).then_inc(s_out, 16)
            sp.wait_ge(s_out, 16 * DT // 2)

        @block.tensor
        def _(pe_):
            mm, tr = nc.tensor.matmul, nc.tensor.transpose

            def add(out, lhsT, rhs, first, last=True):
                return mm(out, lhsT, rhs, start=first, stop=last, skip_group_check=True)

            def stats(k, c):
                if (k, c) == (0, 0):
                    pe_.wait_ge(s_small, SMALL)
                pe_.wait_ge(sq_ready, DT * k + c + 1)
                mm(SB[:, T:2 * T], ones, sq[:, c % 4, :], start=c == 0, stop=c == DT - 1,
                   skip_group_check=True).then_inc(sq_read, 1)

            def post(k):
                pe_.wait_ge(acc_done, DT * (k + 1))
                mm(SB[:, 0:T], ones, acc[:], start=True, stop=True).then_inc(post_stat, 1)

            def transposes_of_v(s, i, u, src):
                pe_.wait_ge(evac_done, s.c(i))
                if u.base >= 1:
                    pe_.wait_ge(x_read, u(i))
                tr(XB[:, 0:P], src[:, 0:P], ident)
                tr(XB[:, P:2 * P], src[:, P:2 * P], ident).then_inc(x_written, 1)

            def stickA(s, i, a):
                hd, p = a
                transposes_of_v(s, i, At(8 + hd.base, hd.step), vT2[:, p, :])
                add(SA[:, 0:T], k2[:, p, 0:P], q2[:, p, :], True, False)
                add(SA[:, T:T + P], k2[:, p, P:T], q2[:, p, P:T], False, False)
                add(SA[:, 0:P], identb, stick_mask, False, False)
                add(SA[:, T:T + P], identb, stick_mask, False).then_inc(z_ready, 1)

            def stickB(s, i, a):
                hd, p = a
                pe_.wait_ge(sp_ready, hd(i, 1))
                add(SA[:, 0:T], neg_l, sp[:, 0:T], False, False)
                add(SA[:, P:T], neg_ones, sp[:, T:T + P], False, False)
                add(SA[:, T:T + P], neg_l, sp[:, T:T + P], False).then_inc(c_ready, 1)

            def stickC(s, i, a):
                hd, p = a
                pe_.wait_ge(a_ready, hd(i, 1))
                pe_.wait_ge(vtok_ready, hd(i, 1))
                pe_.wait_ge(o_done, hd(i, 0 if hd.base == 0 else MEM_HEADS)) if hd.base else None
                add(OB[:, 0:T], vtok[:, 0, :], aw[:, 0:T], True, False)
                add(OB[:, P:T], vtok[:, 1, :], aw[:, T:T + P], False).then_inc(pv_ready, 1)

            def memA(s, i, g):
                l, k = divmod(g, MEM_HEADS)
                pe_.wait_ge(evac_done, s.c(i))
                if l and k == 0:
                    pe_.wait_ge(s_l1, 16 * 5)
                for t in range(2):
                    m = add(SB[:, t * T:(t + 1) * T], qms[l][:, k, t * P:(t + 1) * P], kmem[l][:, k, :], t == 0)
                m.then_inc(ms_ready, 1)

            def memB(s, i, g):
                l = g // MEM_HEADS
                pe_.wait_ge(mp_ready, g + 1)
                for m_ in range(2):
                    for t in range(2):
                        m = tr(TA[:, m_ * T + t * P:m_ * T + (t + 1) * P], pms[l][:, t, m_ * P:(m_ + 1) * P], ident)
                m.then_inc(mt_ready, 1)

            def memC(s, i, g):
                l, k = divmod(g, MEM_HEADS)
                pe_.wait_ge(mpt_ready, g + 1)
                if k:
                    pe_.wait_ge(o_done, 16 * l + k)
                add(TB[:, 0:T], vmem[l][:, 0, k, :], ptms[l][:, 0, :], True, False)
                add(TB[:, 0:T], vmem[l][:, 1, k, :], ptms[l][:, 1, :], False).then_inc(mo_ready, 1)

            def gatesT(s, i, u):
                pe_.wait_ge(evac_done, s.c(i))
                pe_.wait_ge(x_read, u)
                for t in range(2):
                    m = tr(XB[:, t * P:(t + 1) * P], gt[:, t * P:(t + 1) * P], ident)
                m.then_inc(x_written, 1)

            def kcmp_mm(s, i, u):
                pe_.wait_ge(hs_ready, 2)
                pe_.wait_ge(x_read, u)
                for c in range(2):
                    m = mm(XB[:, 0:2 * NC], w2[:, 0, c, :], hs[:, 0, c, :], start=c == 0, stop=c == 1)
                m.then_inc(x_written, 1)

            def vcmp_mm(s, i, u):
                pe_.wait_ge(hs_ready, 4)
                pe_.wait_ge(x_read, u)
                for g in range(GROUPS):
                    for c in range(2):
                        m = add(XB[0:NC, g * P:(g + 1) * P], hs[:, 1, c, g * NC:(g + 1) * NC], w2[:, 1, c, :],
                                g == 0 and c == 0)
                m.then_inc(x_written, 1)

            def nsaA(s, i, hd):
                p, g = hd % 2, hd // HPG
                pe_.wait_ge(rope_done, 6 + hd + 1)
                pe_.wait_ge(cmp_ready, 1)
                qt = [qr[:, p, t * P:(t + 1) * P] for t in range(2)]
                for b, s_ in ((0, SA), (1, SB)):
                    add(s_[:, 0:P], qt[0], kT[:, b, g, 0:P], True, False)
                    add(s_[:, P:3 * P], qt[1], kT[:, b, g, :], False, False)
                    add(s_[:, 0:P], identb, causal_mask, False, False)
                    m = add(s_[:, 2 * P:3 * P], identb, causal_mask, False, b == 1)
                    if b == 0:
                        for t in range(2):
                            at = 3 * P + 16 * t
                            add(SA[:, at:at + NC], qt[t], kcmp[:, g, :], False, False)
                            add(SA[:, at:at + NC], identb, msk[:, M_CMP + 16 * t:M_CMP + 16 * t + NC], False, t == 1)
                m.then_inc(ns_ready, 1)

            def nsaB(s, i, hd):
                pe_.wait_ge(np_ready, hd + 1)
                for b, (src, dst) in enumerate(((ps_s, TA), (ps_w, TB))):
                    for k in range(3):
                        tr(dst[:, k * P:(k + 1) * P], src[:, k * P:(k + 1) * P], ident)
                    m = tr(XB[0:NC, b * P:(b + 1) * P], ps_c[:, b, 0:NC], ident)
                m.then_inc(nt_ready, 1)

            def nsaC(s, i, hd):
                g = hd // HPG
                pe_.wait_ge(npt_act, hd + 1)
                pe_.wait_ge(npt_dve, hd + 1)
                if hd == 0:
                    pe_.wait_ge(cmp_ready, 2)
                pe_.wait_ge(o_done, 16 + MEM_HEADS + hd)
                add(OB[:, 0:T], vcmp[0:NC, g, :], pt_c[0:NC, :, :].rearrange("p a b -> p (a b)"), True, False)
                for b, pt in ((0, pt_s), (1, pt_w)):
                    add(OB[:, 0:T], vT[:, b, g, 0, :], pt[:, 0:T], False, False)
                    m = add(OB[:, P:T], vT[:, b, g, 1, :], pt[:, T:T + P], False, b == 1)
                m.then_inc(pv_ready, 1)

            steps = {
                "post": lambda s, i, a: post(a),
                "vT": lambda s, i, a: transposes_of_v(s, i, a, vtmp if a.base < 8 else vtmp1),
                "stickA": stickA, "stickB": stickB, "stickC": stickC, "memA": memA, "memB": memB, "memC": memC,
                "gatesT": gatesT, "kcmp": kcmp_mm, "vcmp": vcmp_mm, "nsaA": nsaA, "nsaB": nsaB, "nsaC": nsaC}

            def gemm(s, i):
                if s.c.base >= 2:
                    pe_.wait_ge(evac_done, s.c(i, -1))
                act = dest[s.operand]
                cols = 2 * NC if s.w == "cmp" else T
                out = gb[s.c.base % 2]
                order = s.order or range(sum(s.pieces))
                k = 0
                starts = [sum(s.pieces[:j]) for j in range(len(s.pieces))]
                if s.w == "cmp" and s.chunk(i) % 2 == 0:
                    pe_.wait_ge(blk_done, 2)
                if s.gate and s.gate[0] == "mid":
                    pe_.wait_ge(mid_done, FT * s.gate[1] + FT - 1)
                for j, kts in enumerate(s.pieces):
                    pe_.wait_ge(lo_done, s.n(i, j + 1))
                    for _ in range(kts):
                        kt = order[k]
                        for step, a in s.hooks.get(kt, ()):
                            steps[step](s, i, a)
                        if s.gate:
                            if s.gate[0] == "h":
                                pe_.wait_ge(h_done, DT * s.gate[1] + kt + 1)
                            elif s.gate[0] == "o" and kt < HEADS:
                                pe_.wait_ge(o_done, 16 * s.gate[1] + MEM_HEADS + kt + 1)
                            elif s.gate[0] == "mid" and kt == FT - 1:
                                pe_.wait_ge(mid_done, FT * (s.gate[1] + 1))
                        slot = s.n.slot([m for m in range(len(starts)) if starts[m] <= kt][-1])
                        at = (kt - starts[[m for m in range(len(starts)) if starts[m] <= kt][-1]]) * P
                        mm(out[:, 0:2 * cols], hi[slot][:, at:at + P], act[:, kt, :, :].rearrange("p a t -> p (a t)"),
                           start=k == 0, stop=False, skip_group_check=True)
                        m = mm(out[:, cols:2 * cols], lo[slot][:, at:at + P], act[:, kt, 0, :],
                               start=False, stop=k == sum(s.pieces) - 1, skip_group_check=True)
                        k += 1
                        if s.gate and s.gate[0] == "h" and s.gate[2] is not None and k == sum(s.pieces):
                            m.then_inc(piece_done, 1)
                        if s.gate and s.gate[0] == "h" and s.gate[2] is not None:
                            stats(s.gate[2], kt)
                    if not (s.gate and s.gate[0] == "h" and s.gate[2] is not None and k == sum(s.pieces)):
                        m.then_inc(piece_done, 1)

            for rounds, slots in PLAN:
                def body(i):
                    for s in slots:
                        for step, a in s.before:
                            steps[step](s, i, a)
                        gemm(s, i)
                        for step, a in s.after:
                            steps[step](s, i, a)
                if rounds:
                    with pe_.Fori(0, rounds) as i:
                        body(i)
                else:
                    body(None)
            post(3)

        @block.scalar
        def _(act_):
            act = nc.scalar.activation
            me = Steps(act_, act_step)

            act_.dma_start(gains[:], A["gains"]).then_inc(s_gains, 16)
            for q in range(4):
                act_.dma_start(memT[:, 4 * q:4 * q + 4, :], A["memT"][:, 4 * q:4 * q + 4, :]).then_inc(s_memq[q], 16)
            act_.dma_start(cst[:], A["consts"]).then_inc(s_small, 16)
            act_.dma_start(msk[:], A["masks"]).then_inc(s_small, 16)
            act_.dma_start(conv[:], A["conv"]).then_inc(s_small, 16)
            act_.dma_start(x[:], A["xT"]).then_inc(s_x, 16)
            act_.wait_ge(s_gains, 16)

            def round_piece(s, i, j):
                k, kt = s.n.slot(j), tiles_in(s, j)
                act_.wait_ge(landed[k], s.n.landings(i, j))
                if s.n.base + j >= RING:
                    act_.wait_ge(piece_done, s.n(i, j - RING + 1))
                act(hi[k][:, 0:kt * P], raw[k][:, 0:kt * P], ACT.Copy).then_inc(hi_done, 1)

            def take_cross(s, i, last_piece=None):
                act_.wait_ge(piece_done, s.n(i) if s is not None else PIECES_ALL)
                b = (s.c.base - 1) % 2 if s is not None else (CHUNKS - 1) % 2
                c = 2 * NC if s is not None and s.prev[0] == "hid" else T
                act(cross[:, b, 0:c], gb[b][:, c:2 * c], ACT.Copy).then_inc(cross_done, 1)

            def square_root(src):
                act(root[:], src, ACT.Sqrt, bias=col(C_EPS), scale=1.0 / D).then_inc(root_ready, 1)

            def feed(f, fill):
                src, l, gain, dst, tiles, squares, after = FEEDS[f]
                t = memT if src == "mem" else x
                tiles, squares = list(tiles), list(squares)

                def arrived(c):
                    if src == "mem":
                        act_.wait_ge(s_memq[c // 4], 16)
                    elif after is None:
                        act_.wait_ge(s_x, 16)
                    else:
                        act_.wait_ge(xn_ready, (DT * after + c) // 2 + 1)
                for n in range(max(len(tiles), len(squares))):
                    if n < len(tiles):
                        c = tiles[n]
                        arrived(c)
                        act(dest[dst][:, c, 0, :], t[:, c, :], ACT.Copy, scale=gains[:, l, gain, c:c + 1])\
                            .then_inc(hh_ready, 1)
                    if n < len(squares):
                        c = squares[n]
                        seen = DT * STATS[f] + c
                        arrived(c)
                        if seen >= 4:
                            act_.wait_ge(sq_read, seen - 3)
                        act(sq[:, c % 4, :], t[:, c, :], ACT.Square).then_inc(sq_ready, 1)
                    if n % 4 == 3:
                        fill()
                if squares:
                    fill.all()
                    if STATS[f] == 0:
                        act_.wait_ge(s_small, SMALL)
                    act_.wait_ge(sq_read, DT * (STATS[f] + 1))
                    square_root(SB[:, T:2 * T])

            def post(k):
                act(guard[:, 7:8], col(C_EPS), ACT.Sqrt)
                act_.wait_ge(post_stat, k + 1)
                square_root(SB[:, 0:T])

            def stickA(i, a):
                hd, p = a
                act_.wait_ge(z_ready, hd(i, 1))
                me.done(act(ab[:], SA[:, 0:384], ACT.Abs, scale=SCALE))
                nc.scalar.sem_inc(abs_ready, 1)
                me.done(act(ex[:], ab[:], ACT.Exp, scale=-1.0))
                act(ln[:], ex[:], ACT.Ln, bias=1.0).then_inc(ln_ready, 1)

            def stickB(i, a):
                hd, p = a
                act_.wait_ge(c_ready, hd(i, 1))
                act(aw[:], SA[:, 0:384], ACT.Exp, scale=SCALE).then_inc(a_ready, 1)

            def memA(i, g):
                act_.wait_ge(mb_ready, g + 1)
                for t in range(2):
                    m = act(pms[g // MEM_HEADS][:, t, :], SB[:, t * T:(t + 1) * T], ACT.Exp, bias=nb[:, t:t + 1],
                            scale=SCALE, accum_out=sums[:, t:t + 1])
                    m.then_inc(me_ready, 1)

            def memB(i, g):
                act_.wait_ge(mt_ready, g + 1)
                act(ptms[g // MEM_HEADS][:].rearrange("p a t -> p (a t)"), TA[:, :], ACT.Copy).then_inc(mpt_ready, 1)

            def trig():
                act_.wait_ge(red_ready, 1)
                act(sinT[:], rb[:], ACT.Sin).then_inc(trig_ready, 1)
                me.done(act(us[:], rb[:], ACT.Abs))
                act(cosT[:], us[:], ACT.Sin, scale=-1.0, bias=col(C_HALFPI)).then_inc(trig_ready, 1)

            def blocks(a):
                k, n = a
                act_.wait_ge(blkf_ready, n)
                act(blk[k][:, :, 0, :], (blkf0, blkf1)[k][:], ACT.Copy).then_inc(blkh_ready, 1)

            def hidden(k):
                act_.wait_ge(hid_ready, k + 1)
                act(ehid[:, 0, :], hid[:, k % 2, :], ACT.Exp, scale=-1.0).then_inc(hexp_ready, 1)

            def gates():
                act_.wait_ge(x_written, 25)
                act(eg[:], XB[:, 0:T].rearrange("p (t c) -> p t c", t=2)[:, :, 0:36], ACT.Exp, scale=-1.0)\
                    .then_inc(gexp_ready, 1)

            def nsaE(i, hd):
                act_.wait_ge(nb_ready, hd + 1)
                spans = [(ps_c[:, 0, 0:NC], SA[:, 384:384 + NC]), (ps_c[:, 1, 0:NC], SA[:, 400:400 + NC]),
                         (ps_s[:, 0:P], SA[:, 0:P]), (ps_s[:, P:384], SA[:, P:384]),
                         (ps_w[:, 0:P], SB[:, 0:P]), (ps_w[:, P:384], SB[:, P:384])]
                for k, (dst, src) in enumerate(spans):
                    act(dst, src, ACT.Exp, bias=nb[:, k:k + 1], scale=SCALE, accum_out=sums[:, k:k + 1])\
                        .then_inc(ne_ready, 1)

            def nsaB(i, hd):
                act_.wait_ge(nt_ready, hd + 1)
                act(pt_s[:], TA[:, 0:384], ACT.Copy).then_inc(npt_act, 1)

            def silu(l, f, i):
                act_.wait_ge(conv_ready, FT * l + 1 + f if isinstance(f, int) else f + (FT * l + 1))
                act(sg[:], cv[:, 2, :], ACT.Silu).then_inc(silu_ready, 1)

            steps = {
                "post": lambda i, a: post(a), "stickA": stickA, "stickB": stickB, "memA": memA, "memB": memB,
                "trig": lambda i, a: trig(), "blocks": lambda i, a: blocks(a), "gates": lambda i, a: gates(),
                "nsaE": nsaE, "nsaB": nsaB}

            for rounds, slots in PLAN:
                def body(i):
                    for s in slots:
                        fill = Filler(round_piece, s, i)
                        feeds = any(step == "feed" for step, _ in s.react)
                        if s.prev:
                            take_cross(s, i)
                            if s.prev[0] == "up":
                                silu(s.prev[1][0], s.prev[1][1](i), i)
                        if not s.prev:
                            fill()
                        if not feeds:
                            fill.all()
                        if s.prev and s.prev[0] == "hid":
                            hidden(s.prev[1])
                        for step, a in s.react:
                            if step == "feed":
                                feed(a, fill)
                            elif step in steps:
                                steps[step](i, a)
                        fill.all()
                        for j in s.rest:
                            round_piece(s, i, j)
                if rounds:
                    per = 2 * sum(step == "stickA" for s in slots for step, _ in s.react)
                    with act_.Fori(0, rounds) as i, me.rounds(rounds, i, per):
                        body(i)
                else:
                    body(None)
            take_cross(None, None)
            post(3)

        @block.vector
        def _(dve):
            tt, ts, stt = nc.vector.tensor_tensor, nc.vector.tensor_scalar, nc.vector.scalar_tensor_tensor
            me = Steps(dve, dve_step)
            dve.wait_ge(s_gains, 16)

            def split_piece(s, i, j):
                k, kt = s.n.slot(j), tiles_in(s, j)
                dve.wait_ge(hi_done, s.n(i, j + 1))
                tt(lo[k][:, 0:kt * P], raw[k][:, 0:kt * P], hi[k][:, 0:kt * P].bitcast(F32), ALU.subtract)\
                    .then_inc(lo_done, 1)

            def split_out(dst, k, src):
                def part(n):
                    return dst[:, k, n, :] if isinstance(k, int) else \
                        dst[:, bass.ds(k, 1), n, :].rearrange("p o t -> p (o t)")
                me.done(ts(part(0), src, 1.0, None, ALU.mult))
                return tt(part(1), src, part(0).bitcast(F32), ALU.subtract)

            def take(s, i, fill):
                kind, a = s.prev if s is not None else ("y", (1, 3, At(DT - 1)))
                c = s.c(i) if s is not None else CHUNKS
                b = ((s.c.base if s is not None else CHUNKS) - 1) % 2
                dve.wait_ge(cross_done, c)
                main, cr = gb[b][:, 0:T], cross[:, b, :]

                def scaled(dst, r):
                    me.done(tt(cr, main, cr, ALU.add), fill)
                    tt(dst, cr, r[:], ALU.mult).then_inc(evac_done, 1)
                if kind == "memk":
                    scaled(one(km[a[0]], a[1](i)), rmem)
                elif kind == "memv":
                    scaled(vtmp[:], rmem)
                elif kind == "qm":
                    scaled(qms[0 if s.w == "in0" else 1][:, a, :], rx)
                elif kind == "qkv":
                    scaled({"q": q2, "k": k2, "v": vT2}[a[0]][:, a[1], :], rx)
                elif kind == "v":
                    j = GROUPS * a[0] + a[1]
                    if j:
                        dve.wait_ge(x_written, 20 + j)
                    scaled(vtmp1[:], rx)
                elif kind == "vc":
                    scaled(vc[:, a, :], rx)
                elif kind == "gates":
                    scaled(gt[:], rx)
                elif kind == "rope":
                    n = rope_seen[0]
                    rope_seen[0] += 1
                    if n >= 1:
                        dve.wait_ge(rope_done, n)
                    tt(ub[:], main, cr, ALU.add).then_inc(rope_in, 1)
                    half = P // 2
                    tt(us[0:half], gb[b][half:P, 0:T], cross[half:P, b, :], ALU.add).then_inc(rope_in, 1)
                    tt(us[half:P], gb[b][0:half, 0:T], cross[0:half, b, :], ALU.add).then_inc(evac_done, 1)
                elif kind == "hid":
                    me.done(tt(hid[:, a % 2, :], gb[b][:, 0:2 * NC], cross[:, b, 0:2 * NC], ALU.add), fill)
                    nc.vector.sem_inc(evac_done, 1)
                    nc.vector.sem_inc(hid_ready, 1)
                    fill.all()
                    dve.wait_ge(hexp_ready, a + 1)
                    me.done(ts(ehid[:, 1, :], ehid[:, 0, :], 1.0, None, ALU.add))
                    me.done(nc.vector.reciprocal(ehid[:, 2, :], ehid[:, 1, :]))
                    tt(hs[:, a // 2, a % 2, :], hid[:, a % 2, :], ehid[:, 2, :], ALU.mult).then_inc(hs_ready, 1)
                elif kind == "y":
                    l, gain, c = a
                    n = DT * (2 * l + (gain == 3))
                    cc = c(i)
                    p = c.base % 2
                    if n + c.base >= 1:
                        dve.wait_ge(yt_read, cc + n)
                    me.done(tt(yt[:, p, :], main, cr, ALU.add))
                    nc.vector.sem_inc(evac_done, 1)
                    nc.vector.sem_inc(yt_ready, 1)
                    me.done(ts(one(y, cc), yt[:, p, :], gains[:, l, gain, bass.ds(cc, 1)], None, ALU.mult))
                elif kind == "gate":
                    l, f = a[0], a[1](i)
                    if l == 0 and a[1].base == 0 and not a[1].step:
                        dve.wait_ge(s_spill, 32)
                    me.done(tt(cr, main, cr, ALU.add), fill)
                    me.done(tt(gp[:, 2:T + 2], cr, rx[:], ALU.mult), fill)
                    nc.vector.sem_inc(evac_done, 1)

                    def tap(k):
                        return conv[:, l, f, k:k + 1] if isinstance(f, int) else \
                            conv[:, l, bass.ds(f, 1), k:k + 1].rearrange("p o k -> p (o k)")
                    me.done(ts(cv[:, 0, :], gp[:, 0:T], tap(0), tap(3), ALU.mult, ALU.add))
                    me.done(stt(cv[:, 1, :], gp[:, 1:T + 1], tap(1), cv[:, 0, :], ALU.mult, ALU.add))
                    stt(cv[:, 2, :], gp[:, 2:T + 2], tap(2), cv[:, 1, :], ALU.mult, ALU.add).then_inc(conv_ready, 1)
                elif kind == "up":
                    l, f = a[0], a[1](i)
                    me.done(tt(up[:], main, cr, ALU.add), fill)
                    nc.vector.sem_inc(evac_done, 1)
                    fill.all()
                    dve.wait_ge(sgr_ready, f + (FT * l + 1))
                    me.done(tt(up[:], up[:], sgr[:], ALU.mult))
                    split_out(mid, f, up[:]).then_inc(mid_done, 1)

            rope_seen = [0]

            def feed(f, fill):
                src, l, gain, dst, tiles, squares, after = FEEDS[f]
                t, d = (memT if src == "mem" else x), dest[dst]
                if after is None and f in (0, 3):
                    for q in range(4):
                        dve.wait_ge(s_memq[q], 16) if src == "mem" else None
                    dve.wait_ge(s_x, 16) if src == "x" else None

                def low(n):
                    c = tiles[n]
                    dve.wait_ge(hh_ready, FED[f] + n + 1)
                    stt(d[:, c, 1, :], t[:, c, :], gains[:, l, gain, c:c + 1], d[:, c, 0, :].bitcast(F32),
                        ALU.mult, ALU.subtract).then_inc(h_done, 1)
                for n in range(0, len(tiles), 2):
                    if after is not None:
                        add_pair(after, n // 2)
                    if n >= 2 or after is None:
                        m = n - 2 if after is not None else n
                        low(m)
                        low(m + 1)
                    if n % 4 == 2:
                        fill()
                if after is not None:
                    low(len(tiles) - 2)
                    low(len(tiles) - 1)
                if squares:
                    fill.all()
                    dve.wait_ge(root_ready, ROOT_S[STATS[f]])
                    me.done(nc.vector.reciprocal((rmem if src == "mem" else rx)[:], root[:]))
                    nc.vector.sem_inc(rx_ready, 1)

            def pair(t, j):
                return t[:, 2 * j:2 * j + 2, :]

            r_pair = rpost[:].rearrange("p (o t) -> p o t", o=1).broadcast_to((P, 2, T))

            def post(k):
                dve.wait_ge(root_ready, ROOT_P[k])
                me.done(nc.vector.reciprocal(rpost[:], root[:]))
                nc.vector.sem_inc(rpost_ready, 1)
                for j in range(PAIR_LEAD):
                    m = tt(pair(y, j), pair(y, j), r_pair, ALU.mult)
                me.done(m)

            def add_pair(k, j):
                if j >= PAIR_LEAD:
                    dve.wait_ge(yn_ready, (DT // 2 - PAIR_LEAD) * k + j - PAIR_LEAD + 1)
                tt(pair(x, j), pair(x, j), pair(y, j), ALU.add).then_inc(xn_ready, 1)

            def vcopy(i, a):
                l, k, u = a
                k = k(i) if isinstance(k, At) else k
                dve.wait_ge(x_written, u(i, 1))
                dst = vm[l][:, :, k, :] if isinstance(k, int) else \
                    vm[l][:, :, bass.ds(k, 1), :].rearrange("p s o d -> p s (o d)")
                ts(dst, XB[:, 0:T].rearrange("p (s d) -> p s d", s=2), 1.0, None, ALU.mult).then_inc(x_read, 1)

            def vcopy1(i, a):
                w, g, u = a
                dve.wait_ge(x_written, u + 1)
                nc.vector.tensor_copy(vT[:, w, g, :, :], XB[:, 0:T].rearrange("p (s d) -> p s d", s=2))\
                    .then_inc(x_read, 1)

            def stickA(i, a):
                hd, p = a
                dve.wait_ge(x_written, hd(i, 9))
                me.done(nc.vector.tensor_copy(vtok[:], XB[:, 0:T].rearrange("p (s d) -> p s d", s=2)))
                nc.vector.sem_inc(x_read, 1)
                nc.vector.sem_inc(vtok_ready, 1)
                dve.wait_ge(abs_ready, hd(i, 1))
                me.done(ts(rl[:], SA[:, 0:384], 0.0, None, ALU.max))
                dve.wait_ge(ln_ready, hd(i, 1))
                stt(sp[:], ln[:], 1.0 / SCALE, rl[:], ALU.mult, ALU.add).then_inc(sp_ready, 1)

            def stickC(i, a):
                hd, p = a
                dve.wait_ge(pv_ready, hd(i, 1))
                split_out(o, hd(i), OB[:, 0:T]).then_inc(o_done, 1)

            def memA(i, g):
                l = g // MEM_HEADS
                dve.wait_ge(ms_ready, g + 1)
                me.done(nc.vector.reduce_max(mxs[:, 0:2], SB[:].rearrange("p (t m) -> p t m", t=2), AX_X))
                ts(nb[:, 0:2], mxs[:, 0:2], -SCALE, None, ALU.mult).then_inc(mb_ready, 1)
                dve.wait_ge(me_ready, 2 * g + 2)
                me.done(nc.vector.reciprocal(rs[:, 0:2], sums[:, 0:2]))
                for t in range(2):
                    m = ts(pms[l][:, t, :], pms[l][:, t, :], rs[:, t:t + 1], None, ALU.mult)
                    me.done(m)
                nc.vector.sem_inc(mp_ready, 1)

            def memC(i, g):
                dve.wait_ge(mo_ready, g + 1)
                split_out(o, HEADS + g % MEM_HEADS, TB[:, 0:T]).then_inc(o_done, 1)

            def blocks(a):
                k, n = a
                bf = (blkf0, blkf1)[k]
                dve.wait_ge(blkh_ready, n)
                tt(blk[k][:, :, 1, :], bf[:], blk[k][:, :, 0, :].bitcast(F32), ALU.subtract).then_inc(blk_done, 1)

            def gates():
                dve.wait_ge(gexp_ready, 1)
                nc.vector.sem_inc(x_read, 1)
                me.done(ts(eg[:], eg[:], 1.0, None, ALU.add))
                me.done(nc.vector.reciprocal(G[:].rearrange("p h b t -> p t (h b)"), eg[:]))

            def kcmp_copy():
                dve.wait_ge(x_written, 26)
                me.done(nc.vector.tensor_copy(kcmp[:].rearrange("p g c -> p (g c)"), XB[:, 0:2 * NC]))
                nc.vector.sem_inc(x_read, 1)
                nc.vector.sem_inc(cmp_ready, 1)

            def vcmp_copy():
                dve.wait_ge(x_written, 27)
                me.done(nc.vector.tensor_copy(vcmp[0:NC].rearrange("p g d -> p (g d)"), XB[0:NC, 0:T]))
                nc.vector.sem_inc(x_read, 1)
                nc.vector.sem_inc(cmp_ready, 1)

            def nsaA(i, hd):
                dve.wait_ge(ns_ready, hd + 1)
                rm = nc.vector.reduce_max
                rm(mxs[:, 0:2], SA[:, 384:416].rearrange("p (t c) -> p t c", t=2)[:, :, 0:NC], AX_X)
                rm(mxs[:, 2:3], SA[:, 0:P], AX_X)
                rm(mxs[:, 3:4], SA[:, P:384], AX_X)
                rm(mxs[:, 4:5], SB[:, 0:P], AX_X)
                me.done(rm(mxs[:, 5:6], SB[:, P:384], AX_X))
                ts(nb[:, 0:6], mxs[:, 0:6], GUARD, -SCALE, ALU.max, ALU.mult).then_inc(nb_ready, 1)

            def nsaS(i, hd):
                dve.wait_ge(ne_ready, 6 * hd + 6)
                me.done(ts(guard[:, 0:6], sums[:, 0:6], 1e-30, None, ALU.max))
                me.done(nc.vector.reciprocal(rs[:, 0:6], guard[:, 0:6]))
                me.done(tt(wgt[:, 0:6], rs[:, 0:6], G[:, hd, :, :].rearrange("p b t -> p (b t)"), ALU.mult))
                parts = [ps_c[:, 0, 0:NC], ps_c[:, 1, 0:NC], ps_s[:, 0:P], ps_s[:, P:384], ps_w[:, 0:P], ps_w[:, P:384]]
                for k, part in enumerate(parts):
                    m = ts(part, part, wgt[:, k:k + 1], None, ALU.mult)
                m.then_inc(np_ready, 1)

            def nsaB(i, hd):
                dve.wait_ge(nt_ready, hd + 1)
                nc.vector.tensor_copy(pt_w[:], TB[:, 0:384])
                nc.vector.tensor_copy(pt_c[0:NC].rearrange("p a b -> p (a b)"), XB[0:NC, 0:T]).then_inc(npt_dve, 1)

            def nsaC(i, hd):
                dve.wait_ge(pv_ready, HEADS + hd + 1)
                split_out(o, hd, OB[:, 0:T]).then_inc(o_done, 1)

            steps = {
                "post": lambda i, a: post(a), "vcopy": vcopy, "vcopy1": vcopy1, "stickA": stickA, "stickC": stickC,
                "memA": memA, "memC": memC, "blocks": lambda i, a: blocks(a),
                "gates": lambda i, a: gates(), "kcmp": lambda i, a: kcmp_copy(), "vcmp": lambda i, a: vcmp_copy(),
                "nsaA": nsaA, "nsaS": nsaS, "nsaB": nsaB, "nsaC": nsaC}
            PER_TAKE = {"y": 2, "gate": 4, "up": 3, "memk": 1, "memv": 1, "qkv": 1}
            PER_STEP = {"stickA": 2, "stickC": 1}

            for rounds, slots in PLAN:
                def body(i):
                    for s in slots:
                        fill = Filler(split_piece, s, i)
                        feeds = any(step == "feed" for step, _ in s.react)
                        if s.prev:
                            if s.prev[0] == "gate" and i is None:
                                me.done(nc.vector.memset(gp[:, 0:2], 0.0))
                            take(s, i, (lambda: None) if feeds else fill)
                        else:
                            fill()
                        if not feeds:
                            fill.all()
                        for step, a in s.react:
                            if step == "feed":
                                feed(a, fill)
                            elif step in steps:
                                steps[step](i, a)
                        fill.all()
                        for j in s.rest:
                            split_piece(s, i, j)
                if rounds:
                    per = sum(PER_TAKE.get(s.prev[0], 0) + sum(PER_STEP.get(step, 0) for step, _ in s.react)
                              for s in slots)
                    with dve.Fori(0, rounds) as i, me.rounds(rounds, i, per):
                        body(i)
                else:
                    body(None)
            take(None, None, None)
            post(3)
            for j in range(DT // 2):
                add_pair(3, j)

        @block.gpsimd
        def _(pool):
            tt = nc.gpsimd.tensor_tensor
            me = Steps(pool, pool_step)

            def squares(n, i, c):
                p = c.base % 2
                pool.wait_ge(yt_ready, c(i, n + 1))
                if c.base == 0:
                    me.done(tt(acc[:], yt[:, p, :], yt[:, p, :], ALU.mult))
                    nc.gpsimd.sem_inc(yt_read, 1)
                else:
                    me.done(tt(sq1[:], yt[:, p, :], yt[:, p, :], ALU.mult))
                    nc.gpsimd.sem_inc(yt_read, 1)
                    me.done(tt(acc[:], acc[:], sq1[:], ALU.add))
                nc.gpsimd.sem_inc(acc_done, 1)

            def scale_pairs(k):
                pool.wait_ge(rpost_ready, k + 1)
                for j in range(PAIR_LEAD, DT // 2):
                    two = y[:, 2 * j:2 * j + 2, :]
                    tt(two, two, rpost[:].rearrange("p (o t) -> p o t", o=1).broadcast_to((P, 2, T)), ALU.mult)\
                        .then_inc(yn_ready, 1)

            def silu_over_rms(l, f):
                pool.wait_ge(silu_ready, f + (FT * l + 1))
                tt(sgr[:], sg[:], rx[:], ALU.mult).then_inc(sgr_ready, 1)

            def angles():
                ts = nc.gpsimd.tensor_scalar
                pool.wait_ge(s_l1, 16 * 5)
                pool.wait_ge(s_small, SMALL)
                me.done(nc.gpsimd.tensor_copy(rb[:], ra[:].bitcast(I32)))
                me.done(ts(ub[:], rb[:], col(C_FREQ), None, ALU.mult))
                me.done(ts(us[:], ub[:], float(1 / (2 * np.pi)), None, ALU.mult))
                me.done(ts(ra[:], us[:], MAGIC, None, ALU.add))
                me.done(ts(us[:], ra[:], MAGIC, None, ALU.subtract))
                for part in TWO_PI_PARTS:
                    me.done(ts(ra[:], us[:], part, None, ALU.mult))
                    me.done(tt(rb[:], ub[:], ra[:], ALU.subtract))
                    me.done(nc.gpsimd.tensor_copy(ub[:], rb[:]))
                me.done(ts(rb[:], ub[:], 3.1415925, -3.1415925, ALU.min, ALU.max))
                nc.gpsimd.sem_inc(red_ready, 1)

            def tables():
                pool.wait_ge(trig_ready, 2)
                pool.wait_ge(rx_ready, 4)
                me.done(tt(cosT[:], cosT[:], rx[:], ALU.mult))
                me.done(tt(sinT[:], sinT[:], rx[:], ALU.mult))
                me.done(nc.gpsimd.tensor_scalar(sinT[:], sinT[:], col(C_SIGN), None, ALU.mult))

            def windows(k):
                u, bf = (kc, vc)[k], (blkf0, blkf1)[k]
                pool.wait_ge(s_l1, 16 * 5)
                if k == 0:
                    pool.wait_ge(rope_done, 2)
                for g in range(GROUPS):
                    v = u[:, g, :].rearrange("p (c b) -> p b c", b=CMP_STRIDE)
                    for a in range(2):
                        js = slice(a * CMP_STRIDE, (a + 1) * CMP_STRIDE)
                        me.done(tt(bf[:, js, g * NC:(g + 1) * NC], v[:, :, a:a + NC],
                                   pe[:, k, js].rearrange("p (j o) -> p j o", o=1).broadcast_to((P, CMP_STRIDE, NC)),
                                   ALU.add))
                nc.gpsimd.sem_inc(blkf_ready, 1)

            def rotate(k, dst):
                pool.wait_ge(rope_in, 2 * k + 2)
                me.done(tt(ra[:], ub[:], cosT[:], ALU.mult))
                me.done(tt(rb[:], us[:], sinT[:], ALU.mult))
                tt(dst, ra[:], rb[:], ALU.add).then_inc(rope_done, 1)

            ropes = 0
            for rounds, slots in PLAN:
                if slots[0].w == "in0" and not rounds:
                    pool.wait_ge(evac_done, 16)
                    pool.wait_ge(x_read, 8)
                    pool.dma_start(A["spill_k"], km1[:]).then_inc(s_spill, 16)
                    pool.dma_start(A["spill_v"], vm1[:]).then_inc(s_spill, 16)
                work = ("post", "angles", "tables", "windows")
                todo = [s for s in slots if s.prev and s.prev[0] in ("y", "rope", "up")
                        or any(step in work for step, _ in s.react)]
                if not todo:
                    continue

                def body(i):
                    nonlocal ropes
                    for s in todo:
                        if s.prev[0] == "y":
                            l, gain, c = s.prev[1]
                            squares(DT * (2 * l + (gain == 3)), i, c)
                        elif s.prev[0] == "up":
                            silu_over_rms(s.prev[1][0], s.prev[1][1](i))
                        elif s.prev[0] == "rope":
                            pool.wait_ge(evac_done, s.c(i))
                            rotate(ropes, ROPE_DEST[s.prev[1]])
                            ropes += 1
                        for step, a in s.react:
                            if step == "post":
                                scale_pairs(a)
                            elif step == "angles":
                                angles()
                            elif step == "tables":
                                tables()
                            elif step == "windows":
                                if a == 1:
                                    pool.wait_ge(evac_done, s.c(i))
                                windows(a)
                if rounds:
                    per = 2 * sum(s.prev[0] == "y" for s in todo)
                    with pool.Fori(0, rounds) as i, me.rounds(rounds, i, per):
                        body(i)
                else:
                    body(None)
            squares(3 * DT, None, At(DT - 1))
            scale_pairs(3)


def kernel(x, mem, positions, norm_g, w_in_sb, w_in_nsa, cmp_pe, cmp_w1, cmp_w2, w_mem_kv, w_o,
           w_ffn_gate, w_ffn_up, ffn_conv_w, ffn_conv_b, w_ffn_down):
    import ml_dtypes
    import concourse.bacc as bacc
    from concourse.bass_utils import run_bass_kernel_spmd as run

    def tiles(w):
        k, n = w.shape
        return w.reshape(k // P, P, n // P, P).transpose(2, 1, 0, 3)

    def feature_major(a):
        return np.ascontiguousarray(np.asarray(a)[0].T.reshape(DT, P, T).transpose(1, 0, 2))

    consts = np.zeros((P, C_COLS), np.float32)
    consts[:, C_ONES:C_ONES + P] = 1
    consts[:, C_IDENT:C_IDENT + P] = np.eye(P)
    consts[:, C_NEGL:C_NEGL + P] = -np.tril(np.ones((P, P)))
    consts[:, C_NEGONES:C_NEGONES + P] = -1
    freq = (10000.0 ** (-np.arange(0, P, 2) / P)).astype(np.float32)
    consts[:, C_FREQ] = np.concatenate([freq, freq])
    consts[:, C_SIGN] = np.repeat([-1.0, 1.0], P // 2)
    consts[:, C_EPS] = EPS
    consts[:, C_HALFPI] = np.pi / 2
    masks = np.zeros((P, M_COLS), np.float32)
    masks[:, M_IDENT:M_IDENT + P] = np.eye(P)
    masks[:, M_STICK:M_STICK + P] = NEG * np.tril(np.ones((P, P)))
    masks[:, M_CAUSAL:M_CAUSAL + P] = NEG * np.triu(np.ones((P, P)), 1)
    end = np.arange(NC) * CMP_STRIDE + CMP_LEN - 1
    for t in range(2):
        masks[:, M_CMP + 16 * t:M_CMP + 16 * t + NC] = NEG * (end[None, :] > (t * P + np.arange(P))[:, None])

    w_in_sb, w_in_nsa, w_mem_kv, w_o = (np.asarray(a) for a in (w_in_sb, w_in_nsa, w_mem_kv, w_o))
    w_ffn_gate, w_ffn_up, w_ffn_down = (np.asarray(a) for a in (w_ffn_gate, w_ffn_up, w_ffn_down))
    cmp_w1, cmp_w2, cmp_pe = (np.asarray(a) for a in (cmp_w1, cmp_w2, cmp_pe))
    sb = tiles(w_in_sb[0])
    order = [3 * HEADS + g for g in range(MEM_HEADS)] + [j * HEADS + hd for hd in range(HEADS) for j in range(3)]
    arrays = {"in0": sb[order]}
    q_cols, kv_cols = HEADS * P, GROUPS * P
    nsa = w_in_nsa[0]
    parts = {n: nsa[:, q_cols + j * kv_cols:q_cols + (j + 1) * kv_cols]
             for j, n in enumerate(("kc", "vc", "ks", "vs", "kw", "vw"))}
    g0 = q_cols + 6 * kv_cols
    gates = np.concatenate([nsa[:, g0:g0 + 3 * HEADS], np.zeros((D, P - 3 * HEADS), np.float32)], 1)
    arrays["in1"] = tiles(np.concatenate(
        [parts[n] for n in ("vc", "vs", "vw", "kc", "ks", "kw")] + [gates, nsa[:, g0 + 3 * HEADS:], nsa[:, :q_cols]], 1))
    for l in range(2):
        m = tiles(w_mem_kv[l])
        arrays[f"mem{l}"] = m[[j * MEM_HEADS + g for g in range(MEM_HEADS) for j in range(2)]]
        arrays[f"out{l}"] = tiles(w_o[l])
        arrays[f"ffn{l}"] = np.stack([tiles(w_ffn_gate[l]), tiles(w_ffn_up[l])], 1).reshape(2 * FT, P, DT, P)
        arrays[f"down{l}"] = tiles(w_ffn_down[l])
    arrays["cmp"] = np.concatenate([tiles(cmp_w1[0, k]) for k in range(2)])
    arrays["cmp_w2"] = cmp_w2[0].reshape(2, 2, P, P).transpose(2, 0, 1, 3)
    arrays["cmp_pe"] = cmp_pe[0].transpose(2, 0, 1)
    arrays["gains"] = np.asarray(norm_g).reshape(2, 5, DT, P).transpose(3, 0, 1, 2)
    arrays["conv"] = np.concatenate([np.asarray(ffn_conv_w), np.asarray(ffn_conv_b)[:, None]], 1)\
        .reshape(2, 4, FT, P).transpose(3, 0, 2, 1)
    arrays["positions"] = np.broadcast_to(np.asarray(positions), (P, T))
    arrays["consts"] = consts
    arrays["masks"] = masks.astype(ml_dtypes.bfloat16)
    arrays["xT"], arrays["memT"] = feature_major(x), feature_major(mem)

    nc = bacc.Bacc("TRN2", target_bir_lowering=False, num_devices=1)
    arrays = {n: np.ascontiguousarray(a) for n, a in arrays.items()}
    A = {n: nc.dram_tensor("in_" + n, a.shape, mybir.dt.from_np(a.dtype), kind="ExternalInput").ap()
         for n, a in arrays.items()}
    A["spill_k"] = nc.dram_tensor("spill_k", (P, MEM_HEADS, T), F32, kind="Internal").ap()
    A["spill_v"] = nc.dram_tensor("spill_v", (P, 2, MEM_HEADS, P), F32, kind="Internal").ap()
    A["out"] = nc.dram_tensor("out", (P, DT, T), F32, kind="ExternalOutput").ap()
    build(nc, A)
    got = run(nc, [{"in_" + n: a for n, a in arrays.items()}], core_ids=[0]).results[0]["out"]
    return np.ascontiguousarray(got.transpose(2, 1, 0)).reshape(1, T, D)
```

```python
from contextlib import ExitStack, contextmanager

import numpy as np

import concourse.bass as bass
from concourse import mybir

F32 = mybir.dt.float32
F32R = mybir.dt.float32r
BF16 = mybir.dt.bfloat16
I32 = mybir.dt.int32
ACT = mybir.ActivationFunctionType
ALU = mybir.AluOpType
AX_X = mybir.AxisListType.X

P = 128
T = 256
D = 2048
DT = D // P
DFF = 5632
FT = DFF // P
HEADS, MEM_HEADS, GROUPS = 12, 4, 2
HPG = HEADS // GROUPS
CMP_STRIDE, CMP_LEN = 16, 32
NC = T // CMP_STRIDE - 1
SCALE = P ** -0.5
EPS = 1e-6
NEG = -1e30
GUARD = -1e29
RING = 4
PIECE = 8
LEAD = 2
K16 = (8, 8)
K32 = (8, 8, 8, 8)
K44 = (8, 8, 7, 7, 7, 7)
MAGIC = 1.5 * 2.0 ** 23
TWO_PI_PARTS = (6.28125, 1.93500518798828125e-3, 3.01991598e-7)

C_ONES, C_IDENT, C_NEGL, C_NEGONES = 0, P, 2 * P, 3 * P
C_FREQ, C_SIGN, C_EPS, C_HALFPI = (4 * P + k for k in range(4))
C_COLS = 4 * P + 4
M_IDENT, M_STICK, M_CAUSAL, M_CMP = 0, P, 2 * P, 3 * P
M_COLS = 3 * P + 2 * CMP_STRIDE


class At:

    def __init__(self, base, step=0):
        self.base, self.step = base, step

    def __call__(self, i, k=0):
        return self.base + k if i is None or not self.step else i * self.step + (self.base + k)

    def slot(self, k=0):
        return (self.base + k) % RING

    def landings(self, i, k=0):
        first = 16 * ((self.base + k) // RING + 1)
        return first if i is None or not self.step else i * (16 * self.step // RING) + first


class Slot:

    def __init__(self, prev=None, w=None, chunk=None, pieces=None, operand=None, gate=None, order=None,
                 before=(), after=(), react=(), hooks=None, pair=None):
        self.w, self.chunk, self.pieces = w, chunk, pieces
        self.c = self.n = None
        self.operand = operand
        self.prev = prev
        self.gate = gate
        self.order = order
        self.before, self.after, self.react = before, after, react
        self.hooks = hooks or {}
        self.source = None
        self.pair = pair
        self.ahead = self.rest = None


def schedule():
    plan = []
    state = {"c": 0, "n": 0}

    def add(rounds, slots):
        chunks, pieces = len(slots), sum(len(s.pieces) for s in slots)
        if rounds:
            assert chunks % 2 == 0 and pieces % RING == 0
        for s in slots:
            s.c = At(state["c"], chunks if rounds else 0)
            s.n = At(state["n"], pieces if rounds else 0)
            state["c"] += 1
            state["n"] += len(s.pieces)
            s.ahead = range(LEAD if state["n"] > len(s.pieces) else 0, RING)
            s.rest = range(RING, len(s.pieces) + LEAD)
            if s.pair == "first":
                s.rest = range(RING, 2 * len(s.pieces) + LEAD)
            elif s.pair == "second":
                s.ahead = s.rest = ()
                fed = [a for step, a in slots[slots.index(s) - 1].react if step == "feed"]
                s.source = fed[0] if fed else None
        if rounds:
            state["c"] += chunks * (rounds - 1)
            state["n"] += pieces * (rounds - 1)
        plan.append((rounds, slots))

    for l in range(2):
        last = None if l == 0 else ("memv", (0, At(3)))
        k0 = Slot(w=f"mem{l}", chunk=At(0), pieces=K16, operand=f"amem{l}", prev=last)
        v0 = Slot(w=f"mem{l}", chunk=At(1), pieces=K16, operand=f"amem{l}", prev=("memk", (l, At(0))))
        if l == 0:
            k0.react, k0.gate = [("feed", 0)], ("h", 0, 0)
            v0.react = [("feed", 1)]
            k0.pair, v0.pair = "first", "second"
        else:
            k0.after, k0.react, k0.gate = [("vT", At(3))], [("feed", 2)], ("h", 1, None)
            v0.react = [("vcopy", (0, 3, At(3))), ("feed", 3)]
        add(None, [k0, v0])
        add(3, [
            Slot(w=f"mem{l}", chunk=At(2, 2), pieces=K16, operand=f"amem{l}", prev=("memv", (l, At(0, 1))),
                 after=[("vT", At(4 * l, 1))]),
            Slot(w=f"mem{l}", chunk=At(3, 2), pieces=K16, operand=f"amem{l}", prev=("memk", (l, At(1, 1))),
                 react=[("vcopy", (l, At(0, 1), At(4 * l, 1)))]),
        ])

    extra = {}
    for g in range(MEM_HEADS):
        extra.setdefault(g + 1, ([], []))[0].append(("memA", g))
        extra.setdefault(g + 2, ([], []))[0].append(("memB", g))
        extra.setdefault(g + 2, ([], []))[1].append(("memA", g))
        extra.setdefault(g + 3, ([], []))[0].append(("memC", g))
        extra.setdefault(g + 3, ([], []))[1].append(("memB", g))
        extra.setdefault(g + 4, ([], []))[1].append(("memC", g))
    rank = {"memC": 0, "memB": 1, "memA": 2}

    def ordered(steps):
        return sorted(steps, key=lambda s: rank[s[0]])

    def memory_steps(k):
        after, react = extra.get(k, ([], []))
        return ordered(after), ordered(react)[::-1]

    slots = []
    for g in range(MEM_HEADS):
        after, react = memory_steps(g)
        slots.append(Slot(w="in0", chunk=At(g), pieces=K16, operand="h", after=after, react=react,
                          prev=("memv", (1, At(3))) if g == 0 else ("qm", g - 1)))
    slots[0].after = [("vT", At(7))] + slots[0].after
    slots[0].gate, slots[0].react = ("h", 2, 1), [("feed", 4)]
    slots[1].react = [("vcopy", (1, 3, At(7)))] + slots[1].react
    for h in range(2):
        for j, kind in enumerate("qkv"):
            after, react = memory_steps(4 + 3 * h + j)
            prev = ("qm", 3) if (h, j) == (0, 0) else ("qkv", ("vqk"[j], (h if j else h - 1) % 2))
            slots.append(Slot(w="in0", chunk=At(4 + 3 * h + j), pieces=K16, operand="h", prev=prev,
                              after=after, react=react))
    for j, s in enumerate(slots[7:]):
        s.after = s.after + [("stick" + "ABC"[j], (At(0), 0))]
        if j:
            s.react = s.react + [("stick" + "AB"[j - 1], (At(0), 0))]
    add(None, slots)
    slots = []
    for h in range(2):
        p, q = h % 2, (h + 1) % 2
        before = (At(2 + h - 1, 2), q)
        slots += [
            Slot(prev=("qkv", ("v", q)), after=[("stickA", before)], react=[("stickC", (At(h, 2), p))]),
            Slot(prev=("qkv", ("q", p)), after=[("stickB", before)], react=[("stickA", before)]),
            Slot(prev=("qkv", ("k", p)), after=[("stickC", before)], react=[("stickB", before)]),
        ]
    for j, s in enumerate(slots):
        s.w, s.chunk, s.pieces, s.operand = "in0", At(10 + j, 6), K16, "h"
    add(5, slots)

    def out_projection(l, first, second):
        first.w = second.w = f"out{l}"
        first.order = [kt for kt in range(DT) if kt not in (HEADS - 2, HEADS - 1)] + [HEADS - 2, HEADS - 1]
        first.gate = ("o", l)
        first.pair, second.pair = "first", "second"
        for k, s in enumerate((first, second)):
            s.chunk, s.pieces, s.operand = At(k), K16, "o"
        add(None, [first, second])
        add(7, [Slot(w=f"out{l}", chunk=At(2 + k, 2), pieces=K16, operand="o", prev=("y", (l, 1, At(1 + k, 2))))
                for k in range(2)])

    def ffn(l):
        gate0 = Slot(w=f"ffn{l}", chunk=At(0), pieces=K16, operand="h", prev=("y", (l, 1, At(DT - 1))),
                     before=[("post", 2 * l)], gate=("h", 3 + 2 * l, 2 + 2 * l),
                     react=[("post", 2 * l), ("feed", 5 + 2 * l)], pair="first")
        up0 = Slot(w=f"ffn{l}", chunk=At(1), pieces=K16, operand="h", prev=("gate", (l, At(0))), pair="second")
        add(None, [gate0, up0])
        add(FT - 1, [
            Slot(w=f"ffn{l}", chunk=At(2, 2), pieces=K16, operand="h", prev=("up", (l, At(0, 1)))),
            Slot(w=f"ffn{l}", chunk=At(3, 2), pieces=K16, operand="h", prev=("gate", (l, At(1, 1)))),
        ])
        add(None, [
            Slot(w=f"down{l}", chunk=At(0), pieces=K44, operand="mid", prev=("up", (l, At(FT - 1))),
                 gate=("mid", l)),
            Slot(w=f"down{l}", chunk=At(1), pieces=K44, operand="mid", prev=("y", (l, 3, At(0)))),
        ])
        add(7 - l, [Slot(w=f"down{l}", chunk=At(2 + k, 2), pieces=K44, operand="mid",
                         prev=("y", (l, 3, At(1 + k, 2)))) for k in range(2)])
        if l:
            last = [Slot(w=f"down{l}", chunk=At(DT - 2 + k), pieces=K44, operand="mid",
                         prev=("y", (l, 3, At(DT - 3 + k)))) for k in range(2)]
            add(None, last)
            last[1].rest = range(RING, len(K44))

    h11 = (At(11), 1)
    out_projection(
        0,
        Slot(prev=("qkv", ("v", 1)), react=[("stickC", (At(10), 0)), ("stickA", h11), ("stickB", h11), ("stickC", h11)],
             hooks={(1, 5): [("stickA", h11)], (0, 15): [("stickB", h11)], (0, 11): [("stickC", h11)]}),
        Slot(prev=("y", (0, 1, At(0)))))
    ffn(0)

    kinds = [("vc", 0), ("vc", 1), ("v", (0, 0)), ("v", (0, 1)), ("v", (1, 0)), ("v", (1, 1)),
             ("rope", "kc0"), ("rope", "kc1"), ("rope", "ks0"), ("rope", "ks1"), ("rope", "kw0"), ("rope", "kw1"),
             ("gates", 0)]
    qm0 = len(kinds)
    kinds += [kind for g in range(MEM_HEADS) for kind in (("qm", g), ("hid", g))]
    q0 = len(kinds)
    kinds += [("rope", f"q{h % 2}") for h in range(HEADS)]
    slots = []
    for k in range(q0 + HEADS):
        s = Slot(prev=kinds[k - 1] if k else ("y", (0, 3, At(DT - 1))))
        if kinds[k][0] == "hid":
            s.w, s.chunk, s.pieces = "cmp", At(kinds[k][1]), K32
        else:
            s.w, s.chunk, s.pieces, s.operand = "in1", At(k - sum(x[0] == "hid" for x in kinds[:k])), K16, "h"
        s.after, s.react = [], []
        slots.append(s)
    slots[0].before, slots[0].gate = [("post", 1)], ("h", 4, 3)
    slots[0].react = [("post", 1), ("feed", 6)]
    slots[0].pair, slots[1].pair = "first", "second"
    slots[1].react.append(("angles", 0))
    slots[4].react.append(("trig", 0))
    slots[5].react.append(("tables", 0))
    for j, (w, g) in enumerate([(0, 0), (0, 1), (1, 0), (1, 1)]):
        slots[3 + j].after.append(("vT", At(20 + j)))
        slots[4 + j].react.append(("vcopy1", (w, g, 20 + j)))
    slots[2].react.append(("windows", 1))
    slots[3].react.append(("blocks", (1, 1)))
    slots[8].react.append(("windows", 0))
    slots[10].react.append(("blocks", (0, 2)))
    slots[13].after.append(("gatesT", 24))
    slots[14].react.append(("gates", 24))
    for g in range(MEM_HEADS):
        k = qm0 + 2 * g + 1
        slots[k].after.append(("memA", 4 + g))
        slots[k + 1].after.append(("memB", 4 + g))
        slots[k + 1].react.append(("memA", 4 + g))
        slots[k + 2].after.append(("memC", 4 + g))
        slots[k + 2].react.append(("memB", 4 + g))
        slots[k + 3].react.append(("memC", 4 + g))
    for s in slots:
        mem = [x for x in s.after if x[0] in rank]
        s.after = [x for x in s.after if x[0] not in rank] + ordered(mem)
        mem = [x for x in s.react if x[0] in rank]
        s.react = [x for x in s.react if x[0] not in rank] + ordered(mem)[::-1]
    for n, step in enumerate(("kcmp", "vcmp")):
        k = qm0 + 4 * n + 4
        slots[k].after.append(("hidT", n))
        slots[k + 1].react.append(("hidden", n))
        slots[k + 1].after.append((step, 25 + n))
        slots[k + 2].react.append((step, 25 + n))
    for k in range(HEADS):
        s = slots[q0 + k]
        s.after += [("nsa" + x, k - d) for x, d in (("C", 3), ("B", 2), ("A", 1)) if k >= d]
        s.react += [("nsa" + x, k - d) for x, d in (("A", 2), ("B", 3), ("E", 2), ("C", 4), ("S", 2)) if k >= d]
    add(None, slots)
    out_projection(
        1,
        Slot(prev=kinds[-1],
             react=[("nsaA", 10), ("nsaB", 9), ("nsaE", 10), ("nsaC", 8), ("nsaS", 10), ("nsaC", 9), ("nsaB", 10),
                    ("nsaA", 11), ("nsaE", 11), ("nsaC", 10), ("nsaS", 11), ("nsaB", 11), ("nsaC", 11)],
             hooks={(1, 2): [("nsaC", 9)], (1, 3): [("nsaB", 10)], (1, 5): [("nsaA", 11)], (0, 8): [("nsaC", 10)], (0, 15): [("nsaB", 11)],
                    (0, 11): [("nsaC", 11)]}),
        Slot(prev=("y", (1, 1, At(0)))))
    ffn(1)
    return plan, state["c"], state["n"]


PLAN, CHUNKS, PIECES_ALL = schedule()


class Steps:

    def __init__(self, eng, sem):
        self.eng, self.sem, self.n, self.i, self.per = eng, sem, 0, None, 0

    def value(self):
        return self.n if self.i is None else self.i * self.per + self.n

    def done(self, ins, meanwhile=None):
        ins.then_inc(self.sem, 1)
        self.n += 1
        if meanwhile:
            meanwhile()
        self.eng.wait_ge(self.sem, self.value())

    @contextmanager
    def rounds(self, n, i, per):
        start, self.i, self.per = self.n, i, per
        yield
        assert self.n - start == per, (self.n - start, per)
        self.n, self.i = start + per * n, None


class Filler:

    def __init__(self, split, s, i):
        self.split, self.s, self.i, self.left, self.late = split, s, i, list(s.ahead), list(s.rest)

    def __call__(self):
        if self.left:
            self.split(self.s, self.i, self.left.pop(0))

    def all(self):
        while self.left:
            self()

    def rest(self):
        self.all()
        while self.late:
            self.split(self.s, self.i, self.late.pop(0))


def ends_product(s):
    return bool(s.before) and s.before[0][0] == "post"


def tiles_in(s, j):
    return s.pieces[j] if j < len(s.pieces) else PIECE


def source(s, i, j):
    if s.pair:
        n = j + (len(s.pieces) if s.pair == "second" else 0)
        return s.chunk(i, n % 2 - (s.pair == "second")), sum(s.pieces[:n // 2]), s.pieces[n // 2]
    return s.chunk(i), sum(s.pieces[:j]), s.pieces[j]


def build(nc, A):
    with ExitStack() as ctx:
        def sb(name, shape, dt=F32, stack=ctx):
            return stack.enter_context(nc.sbuf_tensor(name, shape, dt))

        def sem(name):
            return ctx.enter_context(nc.semaphore(name))

        x = sb("x", [P, DT, T])
        with ExitStack() as over:
            sb("h_front", [P, DT, T], F32, over)
            y = sb("y", [P, DT, T], F32, over)
        h = sb("h", [P, DT, 2, T], F32R)
        raw = [sb(f"raw{k}", [P, PIECE * P]) for k in range(RING)]
        hi = [sb(f"hi{k}", [P, PIECE * P], F32R) for k in range(RING)]
        lo = [sb(f"lo{k}", [P, PIECE * P], F32R) for k in range(RING)]
        cross = sb("cross", [P, 2, T])
        cst = sb("cst", [P, C_COLS])
        msk = sb("msk", [P, M_COLS], BF16)
        gains = sb("gains", [P, 2, 5, DT])
        conv = sb("conv", [P, 2, FT, 4])
        acc = sb("acc", [P, T])
        sq1 = sb("sq1", [P, T])
        yt = sb("yt", [P, 2, T])
        root = sb("root", [P, T])
        rpost = sb("rpost", [P, T])
        rx = sb("rx", [P, T])
        vtmp, rmem = acc, sq1
        with ExitStack() as over:
            sq = sb("sq", [P, 4, T], F32, over)
        with ExitStack() as over:
            gp = sb("gp", [P, T + 8], F32, over)
            cv = sb("cv", [P, 3, T], F32, over)
            sg = sb("sg", [P, T], F32, over)
            up = sb("up", [P, T], F32, over)
            sgr = sb("sgr", [P, T], F32, over)
        sb("shared", [P, 7 * T + 8])
        def region(tensors):
            with ExitStack() as over:
                return [sb(n, s, dt, over) for n, s, dt in tensors]

        mid, = region([("mid", [P, FT, 2, T], F32R)])
        o, memT, km0, vm0, amem1 = region([
            ("o", [P, DT, 2, T], F32R), ("memT", [P, DT, T], F32), ("km0", [P, MEM_HEADS, T], F32),
            ("vm0", [P, 2, MEM_HEADS, P], F32), ("amem1", [P, DT, 2, T], F32R)])
        _, km1, vm1 = region([("o_a", [P, DT, 2, T], F32R), ("km1", [P, MEM_HEADS, T], F32),
                              ("vm1", [P, 2, MEM_HEADS, P], F32)])
        (_, _, _, _, qm_0, pm_0, ptm_0, q2, k2, vT2, vtok, ab, ex, ln, rl, sp, aw) = region([
            ("o_b", [P, DT, 2, T], F32R), ("memT_b", [P, DT, T], F32), ("km0_b", [P, MEM_HEADS, T], F32),
            ("vm0_b", [P, 2, MEM_HEADS, P], F32), ("qm_0", [P, MEM_HEADS, T], F32), ("pm_0", [P, 2, T], F32),
            ("ptm_0", [P, 2, T], F32), ("q2", [P, 2, T], F32), ("k2", [P, 2, T], F32), ("vT2", [P, 2, T], F32),
            ("vtok", [P, 2, P], F32), ("ab", [P, 384], F32), ("ex", [P, 384], F32), ("ln", [P, 384], F32),
            ("rl", [P, 384], F32), ("sp", [P, 384], F32), ("aw", [P, 384], F32)])
        with ExitStack() as over:
            (_, km1b, vm1b, cosT, sinT, ub, us, ra, rb, kT, vT, kc, vc, w2, pe, ehid, hs, kcmp, vcmp,
             gt, eg, G, qr, qm_1, pm_1, ptm_1, vtmp1) = [sb(n, shape, F32R if n == "o_c" else F32, over) for n, shape in [
                 ("o_c", [P, DT, 2, T]), ("km1b", [P, MEM_HEADS, T]), ("vm1b", [P, 2, MEM_HEADS, P]),
                 ("cosT", [P, T]), ("sinT", [P, T]), ("ub", [P, T]), ("us", [P, T]), ("ra", [P, T]), ("rb", [P, T]),
                 ("kT", [P, 2, GROUPS, T]), ("vT", [P, 2, GROUPS, 2, P]), ("kc", [P, GROUPS, T]),
                 ("vc", [P, GROUPS, T]), ("w2", [P, 2, 2, P]), ("pe", [P, 2, CMP_LEN]), ("ehid", [P, 3, 4 * NC]), ("hs", [P, 2, 2, 2 * NC]), ("kcmp", [P, GROUPS, NC]),
                 ("vcmp", [P, GROUPS, P]), ("gt", [P, T]), ("eg", [P, 2, 36]), ("G", [P, HEADS, 3, 2]),
                 ("qr", [P, 2, T]), ("qm_1", [P, MEM_HEADS, T]), ("pm_1", [P, 2, T]), ("ptm_1", [P, 2, T]),
                 ("vtmp1", [P, T])]]
            blkf0, blkf1 = region([("blkf0", [P, CMP_LEN, 2 * NC], F32), ("blkf1", [P, CMP_LEN, 2 * NC], F32)])
            ps_s, ps_w, ps_c, pt_s, pt_w, pt_c = region([
                ("ps_s", [P, 384], F32), ("ps_w", [P, 384], F32), ("ps_c", [P, 2, 16], F32),
                ("pt_s", [P, 384], F32), ("pt_w", [P, 384], F32), ("pt_c", [P, 2, P], F32)])
        blk = region([("blk0", [P, CMP_LEN, 2, 2 * NC], F32R), ("blk1", [P, CMP_LEN, 2, 2 * NC], F32R)])
        sb("region", [P, FT, 2, T], F32R)
        mxs = sb("mxs", [P, 8])
        nb = sb("nb", [P, 8])
        sums = sb("sums", [P, 8])
        guard = sb("guard", [P, 8])
        rs = sb("rs", [P, 8])
        wgt = sb("wgt", [P, 8])
        km, vm = [km0, km1], [vm0, vm1]
        kmem, vmem = [km0, km1b], [vm0, vm1b]
        qms, pms, ptms = [qm_0, qm_1], [pm_0, pm_1], [ptm_0, ptm_1]
        amem = [o, amem1]

        def bank(name):
            return ctx.enter_context(nc.psum_tensor(name, [P, 512], F32))

        gb = [bank("gemm0"), bank("gemm1")]
        SA, SB, TA, TB, OB, XB = (bank(n) for n in ("SA", "SB", "TA", "TB", "OB", "XB"))

        landed = [sem(f"landed{k}") for k in range(RING)]
        hi_done, lo_done, piece_done = sem("hi_done"), sem("lo_done"), sem("piece_done")
        cross_done, evac_done = sem("cross_done"), sem("evac_done")
        s_gains = sem("s_gains")
        s_memq = [sem(f"s_mem{k}") for k in range(4)]
        s_x, s_small = sem("s_x"), sem("s_small")
        s_l1, s_spill = sem("s_l1"), sem("s_spill")
        s_out = sem("s_out")
        dve_step, act_step, pool_step = sem("dve_step"), sem("act_step"), sem("pool_step")
        sq_ready, sq_read = sem("sq_ready"), sem("sq_read")
        post_stat, root_ready, xn_ready = sem("post_stat"), sem("root_ready"), sem("xn_ready")
        hh_ready, h_done = sem("hh_ready"), sem("h_done")
        rpost_ready, rx_ready, yn_ready = sem("rpost_ready"), sem("rx_ready"), sem("yn_ready")
        sgr_ready = sem("sgr_ready")
        yt_ready, yt_read, acc_done = sem("yt_ready"), sem("yt_read"), sem("acc_done")
        x_written, x_read = sem("x_written"), sem("x_read")
        z_ready, ln_ready, sp_ready, c_ready, a_ready = (sem(n) for n in (
            "z_ready", "ln_ready", "sp_ready", "c_ready", "a_ready"))
        pv_ready, o_done, vtok_ready = sem("pv_ready"), sem("o_done"), sem("vtok_ready")
        ms_ready, mb_ready, me_ready, mp_ready, mt_ready, mpt_ready, mo_ready = (sem(n) for n in (
            "ms_ready", "mb_ready", "me_ready", "mp_ready", "mt_ready", "mpt_ready", "mo_ready"))
        conv_ready, silu_ready, mid_done = sem("conv_ready"), sem("silu_ready"), sem("mid_done")
        abs_ready, red_ready, trig_ready = sem("abs_ready"), sem("red_ready"), sem("trig_ready")
        rope_in, rope_done = sem("rope_in"), sem("rope_done")
        blkf_ready, blkh_ready, blk_done = sem("blkf_ready"), sem("blkh_ready"), sem("blk_done")
        hid_ready, hexp_ready, hs_ready = sem("hid_ready"), sem("hexp_ready"), sem("hs_ready")
        gt_ready, gexp_ready = sem("gt_ready"), sem("gexp_ready")
        cmp_ready = sem("cmp_ready")
        ns_ready, nb_ready, ne_ready, np_ready, nt_ready, npt_act, npt_dve = (sem(n) for n in (
            "ns_ready", "nb_ready", "ne_ready", "np_ready", "nt_ready", "npt_act", "npt_dve"))

        ones, ident = cst[:, C_ONES:C_ONES + P], cst[:, C_IDENT:C_IDENT + P]
        neg_l, neg_ones = cst[:, C_NEGL:C_NEGL + P], cst[:, C_NEGONES:C_NEGONES + P]

        def col(c):
            return cst[:, c:c + 1]

        identb, stick_mask = msk[:, M_IDENT:M_IDENT + P], msk[:, M_STICK:M_STICK + P]
        causal_mask = msk[:, M_CAUSAL:M_CAUSAL + P]

        def one(ap, k):
            return ap[:, k, :] if isinstance(k, int) else ap[:, bass.ds(k, 1), :].rearrange("p o t -> p (o t)")

        SMALL = 16 * 3
        ROOT_S, ROOT_P = (1, 2, 4, 6, 8), (3, 5, 7, 9)
        FEEDS = [
            ("mem", 0, 4, "amem0", range(DT), range(DT), None),
            ("mem", 1, 4, "amem1", range(8), (), None), ("mem", 1, 4, "amem1", range(8, DT), (), None),
            ("x", 0, 0, "h", range(8), (), None), ("x", 0, 0, "h", range(8, DT), range(DT), None),
            ("x", 0, 2, "h", range(DT), range(DT), 0), ("x", 1, 0, "h", range(DT), range(DT), 1),
            ("x", 1, 2, "h", range(DT), range(DT), 2)]
        FED = [sum(len(f[4]) for f in FEEDS[:k]) for k in range(len(FEEDS))]
        STATS = [sum(bool(f[5]) for f in FEEDS[:k]) for k in range(len(FEEDS))]

        def lead(k):
            return 3 if k == 3 else 2
        dest = {"amem0": o, "amem1": amem1, "h": h, "o": o, "mid": mid}
        ROPE_DEST = {"kc0": kc[:, 0, :], "kc1": kc[:, 1, :], "ks0": kT[:, 0, 0, :], "ks1": kT[:, 0, 1, :],
                     "kw0": kT[:, 1, 0, :], "kw1": kT[:, 1, 1, :], "q0": qr[:, 0, :], "q1": qr[:, 1, :]}
        L0_DOWN_END = None
        for rounds, slots in PLAN:
            for s in slots:
                if s.w == "down0" and rounds:
                    L0_DOWN_END = s.n.base + len(s.pieces) + s.n.step * (rounds - 1)
        NSLOT = sum((r or 1) * len(s) for r, s in PLAN)
        assert NSLOT == CHUNKS
        block = ctx.enter_context(nc.Block())

        @block.sync
        def _(sp):
            def load(s, i, j):
                k = s.n.slot(j)
                if s.n.base + j >= RING:
                    sp.wait_ge(lo_done, s.n(i, j - RING + 1))
                c, off, kt = source(s, i, j)
                w = A[s.w]
                src = (w[c] if isinstance(c, int) else w[bass.ds(c, 1)].rearrange("o p k n -> (o p) k n"))
                src = src[:, off:off + kt, :].rearrange("p k n -> p (k n)")
                sp.dma_start(raw[k][:, 0:kt * P], src).then_inc(landed[k], 16)

            def layer1_loads():
                sp.wait_ge(piece_done, L0_DOWN_END)
                sp.wait_ge(s_spill, 32)
                sp.dma_start(km1b[:], A["spill_k"]).then_inc(s_l1, 16)
                sp.dma_start(vm1b[:], A["spill_v"]).then_inc(s_l1, 16)
                sp.dma_start(w2[:], A["cmp_w2"]).then_inc(s_l1, 16)
                sp.dma_start(pe[:], A["cmp_pe"]).then_inc(s_l1, 16)
                sp.dma_start(ra[:].bitcast(I32), A["positions"]).then_inc(s_l1, 16)

            def memory_quarter(q):
                sp.dma_start(memT[:, 4 * q:4 * q + 4, :], A["memT"][:, 4 * q:4 * q + 4, :]).then_inc(s_memq[q], 16)

            for rounds, slots in PLAN:
                def body(i):
                    for s in slots:
                        for j in range(len(s.pieces)):
                            load(s, i, j)
                            if s.n.base + j == 0:
                                memory_quarter(0)
                            elif s.n.base + j == 1:
                                for q in range(1, 4):
                                    memory_quarter(q)
                        if s.w == "in1" and s.chunk(i) == 1:
                            layer1_loads()
                if rounds:
                    with sp.Fori(0, rounds) as i:
                        body(i)
                else:
                    body(None)
            for j in range(DT // 2):
                sp.wait_ge(xn_ready, (3 * DT) // 2 + j + 1)
                sp.dma_start(A["out"][:, 2 * j:2 * j + 2, :], x[:, 2 * j:2 * j + 2, :]).then_inc(s_out, 16)
            sp.wait_ge(s_out, 16 * DT // 2)

        @block.tensor
        def _(pe_):
            mm, tr = nc.tensor.matmul, nc.tensor.transpose

            def add(out, lhsT, rhs, first, last=True):
                return mm(out, lhsT, rhs, start=first, stop=last, skip_group_check=True)

            def stats(k, c):
                if (k, c) == (0, 0):
                    pe_.wait_ge(s_small, SMALL)
                pe_.wait_ge(sq_ready, DT * k + c + 1)
                mm(SB[:, T:2 * T], ones, sq[:, c % 4, :], start=c == 0, stop=c == DT - 1,
                   skip_group_check=True).then_inc(sq_read, 1)

            def post(k):
                pe_.wait_ge(acc_done, (DT - 1) * (k + 1))
                mm(SB[:, 0:T], ones, acc[:], start=True, stop=False, skip_group_check=True)
                pe_.wait_ge(yt_read, DT * (k + 1))
                mm(SB[:, 0:T], ones, sq1[:], start=False, stop=True, skip_group_check=True).then_inc(post_stat, 1)

            def transposes_of_v(s, i, u, src):
                pe_.wait_ge(evac_done, s.c(i))
                if u.base >= 1:
                    pe_.wait_ge(x_read, u(i))
                tr(XB[:, 0:P], src[:, 0:P], ident)
                tr(XB[:, P:2 * P], src[:, P:2 * P], ident).then_inc(x_written, 1)

            def stickA(s, i, a):
                hd, p = a
                transposes_of_v(s, i, At(8 + hd.base, hd.step), vT2[:, p, :])
                add(SA[:, 0:T], k2[:, p, 0:P], q2[:, p, :], True, False)
                add(SA[:, T:T + P], k2[:, p, P:T], q2[:, p, P:T], False, False)
                add(SA[:, 0:P], identb, stick_mask, False, False)
                add(SA[:, T:T + P], identb, stick_mask, False).then_inc(z_ready, 1)

            def stickB(s, i, a):
                hd, p = a
                pe_.wait_ge(sp_ready, hd(i, 1))
                add(SA[:, 0:T], neg_l, sp[:, 0:T], False, False)
                add(SA[:, P:T], neg_ones, sp[:, T:T + P], False, False)
                add(SA[:, T:T + P], neg_l, sp[:, T:T + P], False).then_inc(c_ready, 1)

            def stickC(s, i, a):
                hd, p = a
                pe_.wait_ge(a_ready, hd(i, 1))
                pe_.wait_ge(vtok_ready, hd(i, 1))
                pe_.wait_ge(o_done, hd(i, 0 if hd.base == 0 else MEM_HEADS)) if hd.base else None
                add(OB[:, 0:T], vtok[:, 0, :], aw[:, 0:T], True, False)
                add(OB[:, P:T], vtok[:, 1, :], aw[:, T:T + P], False).then_inc(pv_ready, 1)

            def memA(s, i, g):
                l, k = divmod(g, MEM_HEADS)
                pe_.wait_ge(evac_done, s.c(i))
                if l and k == 0:
                    pe_.wait_ge(s_l1, 16 * 5)
                for t in range(2):
                    m = add(SB[:, t * T:(t + 1) * T], qms[l][:, k, t * P:(t + 1) * P], kmem[l][:, k, :], t == 0)
                m.then_inc(ms_ready, 1)

            def memB(s, i, g):
                l = g // MEM_HEADS
                pe_.wait_ge(mp_ready, g + 1)
                for m_ in range(2):
                    for t in range(2):
                        m = tr(TA[:, m_ * T + t * P:m_ * T + (t + 1) * P], pms[l][:, t, m_ * P:(m_ + 1) * P], ident)
                m.then_inc(mt_ready, 1)

            def memC(s, i, g):
                l, k = divmod(g, MEM_HEADS)
                pe_.wait_ge(mpt_ready, g + 1)
                if k:
                    pe_.wait_ge(o_done, 16 * l + k)
                add(TB[:, 0:T], vmem[l][:, 0, k, :], ptms[l][:, 0, :], True, False)
                add(TB[:, 0:T], vmem[l][:, 1, k, :], ptms[l][:, 1, :], False).then_inc(mo_ready, 1)

            def gatesT(s, i, u):
                pe_.wait_ge(evac_done, s.c(i))
                pe_.wait_ge(x_read, u)
                for t in range(2):
                    m = tr(XB[:, t * P:(t + 1) * P], gt[:, t * P:(t + 1) * P], ident)
                m.then_inc(x_written, 1)

            def hiddenT(s, i, k):
                pe_.wait_ge(evac_done, s.c(i))
                for half in range(2):
                    m = tr(SA[:, half * 2 * NC:(half + 1) * 2 * NC], vtmp1[0:2 * NC, half * P:(half + 1) * P],
                           ident[0:2 * NC, 0:2 * NC])
                m.then_inc(hid_ready, 1)

            def kcmp_mm(s, i, u):
                pe_.wait_ge(hs_ready, 1)
                pe_.wait_ge(x_read, u)
                for c in range(2):
                    m = mm(XB[:, 0:2 * NC], w2[:, 0, c, :], hs[:, 0, c, :], start=c == 0, stop=c == 1)
                m.then_inc(x_written, 1)

            def vcmp_mm(s, i, u):
                pe_.wait_ge(hs_ready, 2)
                pe_.wait_ge(x_read, u)
                for g in range(GROUPS):
                    for c in range(2):
                        m = add(XB[0:NC, g * P:(g + 1) * P], hs[:, 1, c, g * NC:(g + 1) * NC], w2[:, 1, c, :],
                                g == 0 and c == 0)
                m.then_inc(x_written, 1)

            def nsaA(s, i, hd):
                p, g = hd % 2, hd // HPG
                pe_.wait_ge(rope_done, 6 + hd + 1)
                pe_.wait_ge(cmp_ready, 1)
                qt = [qr[:, p, t * P:(t + 1) * P] for t in range(2)]
                for b, s_ in ((0, SA), (1, SB)):
                    add(s_[:, 0:P], qt[0], kT[:, b, g, 0:P], True, False)
                    add(s_[:, P:3 * P], qt[1], kT[:, b, g, :], False, False)
                    add(s_[:, 0:P], identb, causal_mask, False, False)
                    m = add(s_[:, 2 * P:3 * P], identb, causal_mask, False, b == 1)
                    if b == 0:
                        for t in range(2):
                            at = 3 * P + 16 * t
                            add(SA[:, at:at + NC], qt[t], kcmp[:, g, :], False, False)
                            add(SA[:, at:at + NC], identb, msk[:, M_CMP + 16 * t:M_CMP + 16 * t + NC], False, t == 1)
                m.then_inc(ns_ready, 1)

            def nsaB(s, i, hd):
                pe_.wait_ge(np_ready, hd + 1)
                for b, (src, dst) in enumerate(((ps_s, TA), (ps_w, TB))):
                    for k in range(3):
                        tr(dst[:, k * P:(k + 1) * P], src[:, k * P:(k + 1) * P], ident)
                    m = tr(XB[0:NC, b * P:(b + 1) * P], ps_c[:, b, 0:NC], ident)
                m.then_inc(nt_ready, 1)

            def nsaC(s, i, hd):
                g = hd // HPG
                pe_.wait_ge(npt_act, hd + 1)
                pe_.wait_ge(npt_dve, hd + 1)
                if hd == 0:
                    pe_.wait_ge(cmp_ready, 2)
                pe_.wait_ge(o_done, 16 + MEM_HEADS + hd)
                add(OB[:, 0:T], vcmp[0:NC, g, :], pt_c[0:NC, :, :].rearrange("p a b -> p (a b)"), True, False)
                for b, pt in ((0, pt_s), (1, pt_w)):
                    add(OB[:, 0:T], vT[:, b, g, 0, :], pt[:, 0:T], False, False)
                    m = add(OB[:, P:T], vT[:, b, g, 1, :], pt[:, T:T + P], False, b == 1)
                m.then_inc(pv_ready, 1)

            steps = {
                "post": lambda s, i, a: post(a),
                "vT": lambda s, i, a: transposes_of_v(s, i, a, vtmp if a.base < 8 else vtmp1),
                "stickA": stickA, "stickB": stickB, "stickC": stickC, "memA": memA, "memB": memB, "memC": memC,
                "gatesT": gatesT, "hidT": hiddenT, "kcmp": kcmp_mm, "vcmp": vcmp_mm, "nsaA": nsaA, "nsaB": nsaB, "nsaC": nsaC}

            def gemm(s, i):
                if s.c.base >= 2:
                    pe_.wait_ge(evac_done, s.c(i, -1))
                act = dest[s.operand]
                out = gb[s.c.base % 2]
                k = 0
                starts = [sum(s.pieces[:j]) for j in range(len(s.pieces))]
                if s.gate and s.gate[0] == "mid":
                    pe_.wait_ge(mid_done, FT * s.gate[1] + FT - 1)
                for j, kts in enumerate(s.pieces):
                    pe_.wait_ge(lo_done, s.n(i, j + 1))
                    for _ in range(kts):
                        kt = k
                        if s.gate:
                            if s.gate[0] == "h":
                                pe_.wait_ge(h_done, DT * s.gate[1] + kt + 1)
                            elif s.gate[0] == "mid" and kt == FT - 1:
                                pe_.wait_ge(mid_done, FT * (s.gate[1] + 1))
                        slot = s.n.slot([m for m in range(len(starts)) if starts[m] <= kt][-1])
                        at = (kt - starts[[m for m in range(len(starts)) if starts[m] <= kt][-1]]) * P
                        mm(out[:, 0:2 * T], hi[slot][:, at:at + P], act[:, kt, :, :].rearrange("p a t -> p (a t)"),
                           start=k == 0, stop=False, skip_group_check=True)
                        m = mm(out[:, T:2 * T], lo[slot][:, at:at + P], act[:, kt, 0, :],
                               start=False, stop=k == sum(s.pieces) - 1, skip_group_check=True)
                        k += 1
                        if s.gate and s.gate[0] == "h" and s.gate[2] is not None and k == sum(s.pieces):
                            m.then_inc(piece_done, 1)
                        if s.gate and s.gate[0] == "h" and s.gate[2] is not None:
                            stats(s.gate[2], kt)
                    if not (s.gate and s.gate[0] == "h" and s.gate[2] is not None and k == sum(s.pieces)):
                        m.then_inc(piece_done, 1)

            def compress(s, i):
                pe_.wait_ge(evac_done, s.c(i, -1))
                pe_.wait_ge(blk_done, 2)
                k, part = divmod(s.chunk(i), 2)
                out = gb[s.c.base % 2][0:2 * NC, 0:T]
                for j in range(len(s.pieces)):
                    pe_.wait_ge(lo_done, s.n(i, j + 1))
                    slot = s.n.slot(j)
                    for q in range(PIECE // 2):
                        kt, at = part * CMP_LEN // 2 + j * PIECE // 2 + q, slice(2 * q * P, 2 * (q + 1) * P)
                        first, last = (j, q) == (0, 0), (j, q) == (len(s.pieces) - 1, PIECE // 2 - 1)
                        mm(out, blk[k][:, kt, 0, :], hi[slot][:, at], start=first, stop=False)
                        mm(out, blk[k][:, kt, 0, :], lo[slot][:, at], start=False, stop=False)
                        m = mm(out, blk[k][:, kt, 1, :], hi[slot][:, at], start=False, stop=last)
                    m.then_inc(piece_done, 1)

            def gemm_pair(s, i, s2):
                act = dest[s.operand]
                order = s.order or list(range(DT))
                half = s.pieces[0]
                turns = [(b, n) for n in range(DT) for b in range(2)]
                if s.gate[0] == "o":
                    turns = [(b, n) for b in range(2) for n in range(half)] + turns[2 * half:]
                for b, n in turns:
                    chunk, kt, piece = (s, s2)[b], order[n], 2 * (n // half) + b
                    for step, a in s.hooks.get((b, kt), ()):
                        steps[step](s, i, a)
                    if b == 0:
                        if s.gate[0] == "h":
                            pe_.wait_ge(h_done, DT * s.gate[1] + kt + 1)
                        elif kt < HEADS:
                            pe_.wait_ge(o_done, 16 * s.gate[1] + MEM_HEADS + kt + 1)
                    if n % half == 0:
                        pe_.wait_ge(lo_done, s.n(i, piece + 1))
                    if n == 0 and chunk.c.base >= 2:
                        pe_.wait_ge(evac_done, chunk.c(i, -1))
                    slot, out, at = s.n.slot(piece), gb[chunk.c.base % 2], kt % half * P
                    mm(out[:, 0:2 * T], hi[slot][:, at:at + P], act[:, kt, :, :].rearrange("p a t -> p (a t)"),
                       start=n == 0, stop=False, skip_group_check=True)
                    m = mm(out[:, T:2 * T], lo[slot][:, at:at + P], act[:, kt, 0, :],
                           start=False, stop=n == DT - 1, skip_group_check=True)
                    if n % half == half - 1:
                        m.then_inc(piece_done, 1)
                    if b == 1 and s.gate[0] == "h":
                        stats(s.gate[2], kt)

            for rounds, slots in PLAN:
                def body(i):
                    for s in slots:
                        for step, a in s.before:
                            steps[step](s, i, a)
                        if s.pair:
                            if s.pair == "first":
                                gemm_pair(s, i, slots[slots.index(s) + 1])
                        elif s.w == "cmp":
                            compress(s, i)
                        else:
                            gemm(s, i)
                        for step, a in s.after:
                            steps[step](s, i, a)
                if rounds:
                    with pe_.Fori(0, rounds) as i:
                        body(i)
                else:
                    body(None)
            post(3)

        @block.scalar
        def _(act_):
            act = nc.scalar.activation
            me = Steps(act_, act_step)

            act_.dma_start(gains[:], A["gains"]).then_inc(s_gains, 16)
            act_.wait_ge(s_gains, 16)

            def round_piece(s, i, j):
                k, kt = s.n.slot(j), tiles_in(s, j)
                act_.wait_ge(landed[k], s.n.landings(i, j))
                if s.n.base + j >= RING:
                    act_.wait_ge(piece_done, s.n(i, j - RING + 1))
                act(hi[k][:, 0:kt * P], raw[k][:, 0:kt * P], ACT.Copy).then_inc(hi_done, 1)

            def take_cross(s, i, last_piece=None):
                n = PIECES_ALL if s is None else s.n(i, 1 if s.pair == "second" else 0)
                act_.wait_ge(piece_done, n)
                b = (s.c.base - 1) % 2 if s is not None else (CHUNKS - 1) % 2
                if s is not None and s.prev[0] == "hid":
                    act(cross[0:2 * NC, b, :], gb[b][0:2 * NC, 0:T], ACT.Copy).then_inc(cross_done, 1)
                else:
                    act(cross[:, b, :], gb[b][:, T:2 * T], ACT.Copy).then_inc(cross_done, 1)

            def square_root(src):
                act(root[:], src, ACT.Sqrt, bias=col(C_EPS), scale=1.0 / D).then_inc(root_ready, 1)

            def feed(f, fill):
                src, l, gain, dst, tiles, squares, after = FEEDS[f]
                t = memT if src == "mem" else x
                tiles, squares = list(tiles), list(squares)

                def arrived(c):
                    if src == "mem":
                        act_.wait_ge(s_memq[c // 4], 16)
                    elif after is None:
                        act_.wait_ge(s_x, 16 * 4)
                    else:
                        act_.wait_ge(xn_ready, (DT * after + c) // 2 + 1)
                for n in range(max(len(tiles), len(squares))):
                    if n < len(tiles):
                        c = tiles[n]
                        arrived(c)
                        act(dest[dst][:, c, 0, :], t[:, c, :], ACT.Copy, scale=gains[:, l, gain, c:c + 1])\
                            .then_inc(hh_ready, 1)
                    if n < len(squares):
                        c = squares[n]
                        seen = DT * STATS[f] + c
                        arrived(c)
                        if seen >= 4:
                            act_.wait_ge(sq_read, seen - 3)
                        act(sq[:, c % 4, :], t[:, c, :], ACT.Square).then_inc(sq_ready, 1)
                    if n % 4 == 3:
                        fill()
                if squares:
                    fill.rest()

            def root_of_source(f):
                if STATS[f] == 0:
                    act_.wait_ge(s_small, SMALL)
                act_.wait_ge(sq_read, DT * (STATS[f] + 1))
                square_root(SB[:, T:2 * T])

            def load_x(q):
                part = slice(0, 4) if q is None else bass.ds(q * 4 + 4, 4)
                act_.dma_start(x[:, part, :], A["xT"][:, part, :]).then_inc(s_x, 16)

            def last_square(k):
                act_.wait_ge(yt_ready, DT * (k + 1))
                act_.wait_ge(acc_done, (DT - 1) * (k + 1))
                act(sq1[:], yt[:, (DT - 1) % 2, :], ACT.Square).then_inc(yt_read, 1)
                act(guard[:, 7:8], col(C_EPS), ACT.Sqrt)

            def post(k):
                act_.wait_ge(post_stat, k + 1)
                square_root(SB[:, 0:T])

            def stickA(i, a):
                hd, p = a
                act_.wait_ge(z_ready, hd(i, 1))
                me.done(act(ab[:], SA[:, 0:384], ACT.Abs, scale=SCALE))
                nc.scalar.sem_inc(abs_ready, 1)
                me.done(act(ex[:], ab[:], ACT.Exp, scale=-1.0))
                act(ln[:], ex[:], ACT.Ln, bias=1.0).then_inc(ln_ready, 1)

            def stickB(i, a):
                hd, p = a
                act_.wait_ge(c_ready, hd(i, 1))
                act(aw[:], SA[:, 0:384], ACT.Exp, scale=SCALE).then_inc(a_ready, 1)

            def memA(i, g):
                act_.wait_ge(mb_ready, g + 1)
                for t in range(2):
                    m = act(pms[g // MEM_HEADS][:, t, :], SB[:, t * T:(t + 1) * T], ACT.Exp, bias=nb[:, t:t + 1],
                            scale=SCALE, accum_out=sums[:, t:t + 1])
                    m.then_inc(me_ready, 1)

            def memB(i, g):
                act_.wait_ge(mt_ready, g + 1)
                act(ptms[g // MEM_HEADS][:].rearrange("p a t -> p (a t)"), TA[:, :], ACT.Copy).then_inc(mpt_ready, 1)

            def trig():
                act_.wait_ge(red_ready, 1)
                act(sinT[:], rb[:], ACT.Sin).then_inc(trig_ready, 1)
                me.done(act(us[:], rb[:], ACT.Abs))
                act(cosT[:], us[:], ACT.Sin, scale=-1.0, bias=col(C_HALFPI)).then_inc(trig_ready, 1)

            def blocks(a):
                k, n = a
                act_.wait_ge(blkf_ready, n)
                act(blk[k][:, :, 0, :], (blkf0, blkf1)[k][:], ACT.Copy).then_inc(blkh_ready, 1)

            def hidden(k):
                act_.wait_ge(hid_ready, k + 1)
                act(ehid[:, 0, :], SA[:, 0:4 * NC], ACT.Exp, scale=-1.0).then_inc(hexp_ready, 1)

            def gates():
                act_.wait_ge(x_written, 25)
                act(eg[:], XB[:, 0:T].rearrange("p (t c) -> p t c", t=2)[:, :, 0:36], ACT.Exp, scale=-1.0)\
                    .then_inc(gexp_ready, 1)

            def nsaE(i, hd):
                act_.wait_ge(nb_ready, hd + 1)
                spans = [(ps_c[:, 0, 0:NC], SA[:, 384:384 + NC]), (ps_c[:, 1, 0:NC], SA[:, 400:400 + NC]),
                         (ps_s[:, 0:P], SA[:, 0:P]), (ps_s[:, P:384], SA[:, P:384]),
                         (ps_w[:, 0:P], SB[:, 0:P]), (ps_w[:, P:384], SB[:, P:384])]
                for k, (dst, src) in enumerate(spans):
                    act(dst, src, ACT.Exp, bias=nb[:, k:k + 1], scale=SCALE, accum_out=sums[:, k:k + 1])\
                        .then_inc(ne_ready, 1)

            def nsaB(i, hd):
                act_.wait_ge(nt_ready, hd + 1)
                act(pt_s[:], TA[:, 0:384], ACT.Copy).then_inc(npt_act, 1)

            def silu(l, f, i):
                act_.wait_ge(conv_ready, FT * l + 1 + f if isinstance(f, int) else f + (FT * l + 1))
                act(sg[:], cv[:, 2, :], ACT.Silu).then_inc(silu_ready, 1)

            steps = {
                "stickA": stickA, "stickB": stickB, "memA": memA, "memB": memB,
                "trig": lambda i, a: trig(), "blocks": lambda i, a: blocks(a), "gates": lambda i, a: gates(),
                "hidden": lambda i, k: hidden(k), "nsaE": nsaE, "nsaB": nsaB}

            for rounds, slots in PLAN:
                def body(i):
                    for s in slots:
                        fill = Filler(round_piece, s, i)
                        feeds = any(step == "feed" for step, _ in s.react)
                        if s.prev:
                            take_cross(s, i)
                            if ends_product(s):
                                last_square(s.before[0][1])
                            if s.prev[0] == "up":
                                silu(s.prev[1][0], s.prev[1][1](i), i)
                            if s.source is not None:
                                root_of_source(s.source)
                        if not s.prev:
                            fill()
                            fill()
                        if not feeds:
                            fill.all()
                        for step, a in s.react:
                            if step == "post":
                                fill()
                                post(a)
                                fill()
                            elif step == "feed":
                                feed(a, fill)
                                if FEEDS[a][5] and not s.pair:
                                    root_of_source(a)
                            elif step in steps:
                                steps[step](i, a)
                        fill.rest()
                        if s.c.base == 1:
                            load_x(None)
                        elif s.c.base == 2:
                            load_x(i)
                if rounds:
                    per = 2 * sum(step == "stickA" for s in slots for step, _ in s.react)
                    with act_.Fori(0, rounds) as i, me.rounds(rounds, i, per):
                        body(i)
                else:
                    body(None)
            take_cross(None, None)
            last_square(3)
            post(3)

        @block.vector
        def _(dve):
            tt, ts, stt = nc.vector.tensor_tensor, nc.vector.tensor_scalar, nc.vector.scalar_tensor_tensor
            me = Steps(dve, dve_step)
            dve.wait_ge(s_gains, 16)

            def split_piece(s, i, j):
                k, kt = s.n.slot(j), tiles_in(s, j)
                dve.wait_ge(hi_done, s.n(i, j + 1))
                tt(lo[k][:, 0:kt * P], raw[k][:, 0:kt * P], hi[k][:, 0:kt * P].bitcast(F32), ALU.subtract)\
                    .then_inc(lo_done, 1)

            def split_out(dst, k, src):
                def part(n):
                    return dst[:, k, n, :] if isinstance(k, int) else \
                        dst[:, bass.ds(k, 1), n, :].rearrange("p o t -> p (o t)")
                me.done(ts(part(0), src, 1.0, None, ALU.mult))
                return tt(part(1), src, part(0).bitcast(F32), ALU.subtract)

            def take(s, i, fill):
                kind, a = s.prev if s is not None else ("y", (1, 3, At(DT - 1)))
                c = s.c(i) if s is not None else CHUNKS
                b = ((s.c.base if s is not None else CHUNKS) - 1) % 2
                dve.wait_ge(cross_done, c)
                main, cr = gb[b][:, 0:T], cross[:, b, :]

                second = s is not None and s.pair == "second"

                def first_of_pair():
                    me.done(tt(yt[:, 0, :], main, cr, ALU.add))
                    nc.vector.sem_inc(evac_done, 1)
                    rms_of_source(s.source)

                def scaled(dst, r):
                    if second:
                        first_of_pair()
                        tt(dst, yt[:, 0, :], r[:], ALU.mult)
                    else:
                        me.done(tt(cr, main, cr, ALU.add), fill)
                        tt(dst, cr, r[:], ALU.mult).then_inc(evac_done, 1)
                if kind == "memk":
                    scaled(one(km[a[0]], a[1](i)), rmem)
                elif kind == "memv":
                    scaled(vtmp[:], rmem)
                elif kind == "qm":
                    scaled(qms[0 if s.w == "in0" else 1][:, a, :], rx)
                elif kind == "qkv":
                    scaled({"q": q2, "k": k2, "v": vT2}[a[0]][:, a[1], :], rx)
                elif kind == "v":
                    j = GROUPS * a[0] + a[1]
                    if j:
                        dve.wait_ge(x_written, 20 + j)
                    scaled(vtmp1[:], rx)
                elif kind == "vc":
                    scaled(vc[:, a, :], rx)
                elif kind == "gates":
                    scaled(gt[:], rx)
                elif kind == "rope":
                    n = rope_seen[0]
                    rope_seen[0] += 1
                    if n >= 1:
                        dve.wait_ge(rope_done, n)
                    tt(ub[:], main, cr, ALU.add).then_inc(rope_in, 1)
                    half = P // 2
                    tt(us[0:half], gb[b][half:P, 0:T], cross[half:P, b, :], ALU.add).then_inc(rope_in, 1)
                    tt(us[half:P], gb[b][0:half, 0:T], cross[0:half, b, :], ALU.add).then_inc(evac_done, 1)
                elif kind == "hid":
                    part, half = vtmp1[0:2 * NC, :], cross[0:2 * NC, b, :]
                    if a % 2 == 0:
                        m = nc.vector.tensor_copy(part, half)
                    else:
                        m = tt(part, part, half, ALU.add)
                    m.then_inc(evac_done, 1)
                elif kind == "y":
                    l, gain, c = a
                    n = DT * (2 * l + (gain == 3))
                    cc = c(i)
                    p = c.base % 2
                    if n + c.base >= 1:
                        dve.wait_ge(yt_read, cc + n)
                    me.done(tt(yt[:, p, :], main, cr, ALU.add))
                    nc.vector.sem_inc(evac_done, 1)
                    nc.vector.sem_inc(yt_ready, 1)
                    me.done(ts(one(y, cc), yt[:, p, :], gains[:, l, gain, bass.ds(cc, 1)], None, ALU.mult))
                elif kind == "gate":
                    l, f = a[0], a[1](i)
                    if l == 0 and a[1].base == 0 and not a[1].step:
                        dve.wait_ge(s_spill, 32)
                    if second:
                        first_of_pair()
                        nc.vector.memset(gp[:, 0:2], 0.0)
                        me.done(tt(gp[:, 2:T + 2], yt[:, 0, :], rx[:], ALU.mult))
                    else:
                        me.done(tt(cr, main, cr, ALU.add), fill)
                        me.done(tt(gp[:, 2:T + 2], cr, rx[:], ALU.mult), fill)
                        nc.vector.sem_inc(evac_done, 1)

                    def tap(k):
                        return conv[:, l, f, k:k + 1] if isinstance(f, int) else \
                            conv[:, l, bass.ds(f, 1), k:k + 1].rearrange("p o k -> p (o k)")
                    me.done(ts(cv[:, 0, :], gp[:, 0:T], tap(0), tap(3), ALU.mult, ALU.add))
                    me.done(stt(cv[:, 1, :], gp[:, 1:T + 1], tap(1), cv[:, 0, :], ALU.mult, ALU.add))
                    stt(cv[:, 2, :], gp[:, 2:T + 2], tap(2), cv[:, 1, :], ALU.mult, ALU.add).then_inc(conv_ready, 1)
                elif kind == "up":
                    l, f = a[0], a[1](i)
                    me.done(tt(up[:], main, cr, ALU.add), fill)
                    nc.vector.sem_inc(evac_done, 1)
                    fill.all()
                    dve.wait_ge(sgr_ready, f + (FT * l + 1))
                    me.done(tt(up[:], up[:], sgr[:], ALU.mult))
                    split_out(mid, f, up[:]).then_inc(mid_done, 1)

            rope_seen = [0]

            def feed(f, fill):
                src, l, gain, dst, tiles, squares, after = FEEDS[f]
                t, d = (memT if src == "mem" else x), dest[dst]
                def low(n):
                    c = tiles[n]
                    dve.wait_ge(hh_ready, FED[f] + n + 1)
                    stt(d[:, c, 1, :], t[:, c, :], gains[:, l, gain, c:c + 1], d[:, c, 0, :].bitcast(F32),
                        ALU.mult, ALU.subtract).then_inc(h_done, 1)
                for n in range(0, len(tiles), 2):
                    if after is not None:
                        add_pair(after, n // 2)
                    if n >= 2 or after is None:
                        m = n - 2 if after is not None else n
                        low(m)
                        low(m + 1)
                    if n % 4 == 2:
                        fill()
                if after is not None:
                    low(len(tiles) - 2)
                    low(len(tiles) - 1)
                if squares:
                    fill.rest()

            def rms_of_source(f):
                dve.wait_ge(root_ready, ROOT_S[STATS[f]])
                me.done(nc.vector.reciprocal((rmem if FEEDS[f][0] == "mem" else rx)[:], root[:]))
                nc.vector.sem_inc(rx_ready, 1)

            def pair(t, j):
                return t[:, 2 * j:2 * j + 2, :]

            r_pair = rpost[:].rearrange("p (o t) -> p o t", o=1).broadcast_to((P, 2, T))

            def post(k):
                dve.wait_ge(root_ready, ROOT_P[k])
                me.done(nc.vector.reciprocal(rpost[:], root[:]))
                nc.vector.sem_inc(rpost_ready, 1)
                for j in range(lead(k)):
                    m = tt(pair(y, j), pair(y, j), r_pair, ALU.mult)
                me.done(m)

            def add_pair(k, j):
                if j >= lead(k):
                    dve.wait_ge(yn_ready, (DT // 2 - lead(0)) * k + j - lead(k) + 1)
                tt(pair(x, j), pair(x, j), pair(y, j), ALU.add).then_inc(xn_ready, 1)

            def vcopy(i, a):
                l, k, u = a
                k = k(i) if isinstance(k, At) else k
                dve.wait_ge(x_written, u(i, 1))
                dst = vm[l][:, :, k, :] if isinstance(k, int) else \
                    vm[l][:, :, bass.ds(k, 1), :].rearrange("p s o d -> p s (o d)")
                ts(dst, XB[:, 0:T].rearrange("p (s d) -> p s d", s=2), 1.0, None, ALU.mult).then_inc(x_read, 1)

            def vcopy1(i, a):
                w, g, u = a
                dve.wait_ge(x_written, u + 1)
                nc.vector.tensor_copy(vT[:, w, g, :, :], XB[:, 0:T].rearrange("p (s d) -> p s d", s=2))\
                    .then_inc(x_read, 1)

            def stickA(i, a):
                hd, p = a
                dve.wait_ge(x_written, hd(i, 9))
                me.done(nc.vector.tensor_copy(vtok[:], XB[:, 0:T].rearrange("p (s d) -> p s d", s=2)))
                nc.vector.sem_inc(x_read, 1)
                nc.vector.sem_inc(vtok_ready, 1)
                dve.wait_ge(abs_ready, hd(i, 1))
                me.done(ts(rl[:], SA[:, 0:384], 0.0, None, ALU.max))
                dve.wait_ge(ln_ready, hd(i, 1))
                stt(sp[:], ln[:], 1.0 / SCALE, rl[:], ALU.mult, ALU.add).then_inc(sp_ready, 1)

            def stickC(i, a):
                hd, p = a
                dve.wait_ge(pv_ready, hd(i, 1))
                split_out(o, hd(i), OB[:, 0:T]).then_inc(o_done, 1)

            def memA(i, g):
                l = g // MEM_HEADS
                dve.wait_ge(ms_ready, g + 1)
                me.done(nc.vector.reduce_max(mxs[:, 0:2], SB[:].rearrange("p (t m) -> p t m", t=2), AX_X))
                ts(nb[:, 0:2], mxs[:, 0:2], -SCALE, None, ALU.mult).then_inc(mb_ready, 1)
                dve.wait_ge(me_ready, 2 * g + 2)
                me.done(nc.vector.reciprocal(rs[:, 0:2], sums[:, 0:2]))
                for t in range(2):
                    m = ts(pms[l][:, t, :], pms[l][:, t, :], rs[:, t:t + 1], None, ALU.mult)
                    me.done(m)
                nc.vector.sem_inc(mp_ready, 1)

            def memC(i, g):
                dve.wait_ge(mo_ready, g + 1)
                split_out(o, HEADS + g % MEM_HEADS, TB[:, 0:T]).then_inc(o_done, 1)

            def blocks(a):
                k, n = a
                bf = (blkf0, blkf1)[k]
                dve.wait_ge(blkh_ready, n)
                tt(blk[k][:, :, 1, :], bf[:], blk[k][:, :, 0, :].bitcast(F32), ALU.subtract).then_inc(blk_done, 1)

            def gates():
                dve.wait_ge(gexp_ready, 1)
                nc.vector.sem_inc(x_read, 1)
                me.done(ts(eg[:], eg[:], 1.0, None, ALU.add))
                me.done(nc.vector.reciprocal(G[:].rearrange("p h b t -> p t (h b)"), eg[:]))

            def hidden(k):
                dve.wait_ge(hexp_ready, k + 1)
                me.done(ts(ehid[:, 1, :], ehid[:, 0, :], 1.0, None, ALU.add))
                me.done(nc.vector.reciprocal(ehid[:, 2, :], ehid[:, 1, :]))
                tt(hs[:, k, :, :].rearrange("p a b -> p (a b)"), SA[:, 0:4 * NC], ehid[:, 2, :], ALU.mult)\
                    .then_inc(hs_ready, 1)

            def kcmp_copy():
                dve.wait_ge(x_written, 26)
                me.done(nc.vector.tensor_copy(kcmp[:].rearrange("p g c -> p (g c)"), XB[:, 0:2 * NC]))
                nc.vector.sem_inc(x_read, 1)
                nc.vector.sem_inc(cmp_ready, 1)

            def vcmp_copy():
                dve.wait_ge(x_written, 27)
                me.done(nc.vector.tensor_copy(vcmp[0:NC].rearrange("p g d -> p (g d)"), XB[0:NC, 0:T]))
                nc.vector.sem_inc(x_read, 1)
                nc.vector.sem_inc(cmp_ready, 1)

            def nsaA(i, hd):
                dve.wait_ge(ns_ready, hd + 1)
                rm = nc.vector.reduce_max
                rm(mxs[:, 0:2], SA[:, 384:416].rearrange("p (t c) -> p t c", t=2)[:, :, 0:NC], AX_X)
                rm(mxs[:, 2:3], SA[:, 0:P], AX_X)
                rm(mxs[:, 3:4], SA[:, P:384], AX_X)
                rm(mxs[:, 4:5], SB[:, 0:P], AX_X)
                me.done(rm(mxs[:, 5:6], SB[:, P:384], AX_X))
                ts(nb[:, 0:6], mxs[:, 0:6], GUARD, -SCALE, ALU.max, ALU.mult).then_inc(nb_ready, 1)

            def nsaS(i, hd):
                dve.wait_ge(ne_ready, 6 * hd + 6)
                me.done(ts(guard[:, 0:6], sums[:, 0:6], 1e-30, None, ALU.max))
                me.done(nc.vector.reciprocal(rs[:, 0:6], guard[:, 0:6]))
                me.done(tt(wgt[:, 0:6], rs[:, 0:6], G[:, hd, :, :].rearrange("p b t -> p (b t)"), ALU.mult))
                parts = [ps_c[:, 0, 0:NC], ps_c[:, 1, 0:NC], ps_s[:, 0:P], ps_s[:, P:384], ps_w[:, 0:P], ps_w[:, P:384]]
                for k, part in enumerate(parts):
                    m = ts(part, part, wgt[:, k:k + 1], None, ALU.mult)
                m.then_inc(np_ready, 1)

            def nsaB(i, hd):
                dve.wait_ge(nt_ready, hd + 1)
                nc.vector.tensor_copy(pt_w[:], TB[:, 0:384])
                nc.vector.tensor_copy(pt_c[0:NC].rearrange("p a b -> p (a b)"), XB[0:NC, 0:T]).then_inc(npt_dve, 1)

            def nsaC(i, hd):
                dve.wait_ge(pv_ready, HEADS + hd + 1)
                split_out(o, hd, OB[:, 0:T]).then_inc(o_done, 1)

            steps = {
                "post": lambda i, a: post(a), "vcopy": vcopy, "vcopy1": vcopy1, "stickA": stickA, "stickC": stickC,
                "memA": memA, "memC": memC, "blocks": lambda i, a: blocks(a),
                "gates": lambda i, a: gates(), "hidden": lambda i, k: hidden(k), "kcmp": lambda i, a: kcmp_copy(), "vcmp": lambda i, a: vcmp_copy(),
                "nsaA": nsaA, "nsaS": nsaS, "nsaB": nsaB, "nsaC": nsaC}
            PER_TAKE = {"y": 2, "gate": 4, "up": 3, "memk": 1, "memv": 1, "qkv": 1}
            PER_STEP = {"stickA": 2, "stickC": 1}

            for rounds, slots in PLAN:
                def body(i):
                    for s in slots:
                        fill = Filler(split_piece, s, i)
                        feeds = any(step == "feed" for step, _ in s.react)
                        if s.prev:
                            take(s, i, (lambda: None) if feeds else fill)
                            if ends_product(s):
                                fill()
                        else:
                            fill()
                            fill()
                        if not feeds:
                            fill.all()
                        for step, a in s.react:
                            if step == "feed":
                                feed(a, fill)
                                if FEEDS[a][5] and not s.pair:
                                    rms_of_source(a)
                            elif step in steps:
                                steps[step](i, a)
                        fill.rest()
                if rounds:
                    per = sum(PER_TAKE.get(s.prev[0], 0) + sum(PER_STEP.get(step, 0) for step, _ in s.react)
                              for s in slots)
                    with dve.Fori(0, rounds) as i, me.rounds(rounds, i, per):
                        body(i)
                else:
                    body(None)
            take(None, None, None)
            post(3)
            for j in range(DT // 2):
                add_pair(3, j)

        @block.gpsimd
        def _(pool):
            tt = nc.gpsimd.tensor_tensor
            me = Steps(pool, pool_step)

            pool.dma_start(cst[:], A["consts"]).then_inc(s_small, 16)
            pool.dma_start(msk[:], A["masks"]).then_inc(s_small, 16)
            pool.dma_start(conv[:], A["conv"]).then_inc(s_small, 16)

            def squares(n, i, c):
                p = c.base % 2
                pool.wait_ge(yt_ready, c(i, n + 1))
                if c.base == 0:
                    me.done(tt(acc[:], yt[:, p, :], yt[:, p, :], ALU.mult))
                    nc.gpsimd.sem_inc(yt_read, 1)
                else:
                    me.done(tt(sq1[:], yt[:, p, :], yt[:, p, :], ALU.mult))
                    nc.gpsimd.sem_inc(yt_read, 1)
                    me.done(tt(acc[:], acc[:], sq1[:], ALU.add))
                nc.gpsimd.sem_inc(acc_done, 1)

            def scale_pairs(k):
                pool.wait_ge(rpost_ready, k + 1)
                for j in range(lead(k), DT // 2):
                    two = y[:, 2 * j:2 * j + 2, :]
                    tt(two, two, rpost[:].rearrange("p (o t) -> p o t", o=1).broadcast_to((P, 2, T)), ALU.mult)\
                        .then_inc(yn_ready, 1)

            def silu_over_rms(l, f):
                pool.wait_ge(silu_ready, f + (FT * l + 1))
                tt(sgr[:], sg[:], rx[:], ALU.mult).then_inc(sgr_ready, 1)

            def angles():
                ts = nc.gpsimd.tensor_scalar
                pool.wait_ge(s_l1, 16 * 5)
                pool.wait_ge(s_small, SMALL)
                me.done(nc.gpsimd.tensor_copy(rb[:], ra[:].bitcast(I32)))
                me.done(ts(ub[:], rb[:], col(C_FREQ), None, ALU.mult))
                me.done(ts(us[:], ub[:], float(1 / (2 * np.pi)), None, ALU.mult))
                me.done(ts(ra[:], us[:], MAGIC, None, ALU.add))
                me.done(ts(us[:], ra[:], MAGIC, None, ALU.subtract))
                for part in TWO_PI_PARTS:
                    me.done(ts(ra[:], us[:], part, None, ALU.mult))
                    me.done(tt(rb[:], ub[:], ra[:], ALU.subtract))
                    me.done(nc.gpsimd.tensor_copy(ub[:], rb[:]))
                me.done(ts(rb[:], ub[:], 3.1415925, -3.1415925, ALU.min, ALU.max))
                nc.gpsimd.sem_inc(red_ready, 1)

            def tables():
                pool.wait_ge(trig_ready, 2)
                pool.wait_ge(rx_ready, 4)
                me.done(tt(cosT[:], cosT[:], rx[:], ALU.mult))
                me.done(tt(sinT[:], sinT[:], rx[:], ALU.mult))
                me.done(nc.gpsimd.tensor_scalar(sinT[:], sinT[:], col(C_SIGN), None, ALU.mult))

            def windows(k):
                u, bf = (kc, vc)[k], (blkf0, blkf1)[k]
                pool.wait_ge(s_l1, 16 * 5)
                if k == 0:
                    pool.wait_ge(rope_done, 2)
                for g in range(GROUPS):
                    v = u[:, g, :].rearrange("p (c b) -> p b c", b=CMP_STRIDE)
                    for a in range(2):
                        js = slice(a * CMP_STRIDE, (a + 1) * CMP_STRIDE)
                        me.done(tt(bf[:, js, g * NC:(g + 1) * NC], v[:, :, a:a + NC],
                                   pe[:, k, js].rearrange("p (j o) -> p j o", o=1).broadcast_to((P, CMP_STRIDE, NC)),
                                   ALU.add))
                nc.gpsimd.sem_inc(blkf_ready, 1)

            def rotate(k, dst):
                pool.wait_ge(rope_in, 2 * k + 2)
                me.done(tt(ra[:], ub[:], cosT[:], ALU.mult))
                me.done(tt(rb[:], us[:], sinT[:], ALU.mult))
                tt(dst, ra[:], rb[:], ALU.add).then_inc(rope_done, 1)

            ropes = 0
            for rounds, slots in PLAN:
                if slots[0].w == "in0" and not rounds:
                    pool.wait_ge(evac_done, 16)
                    pool.wait_ge(x_read, 8)
                    pool.dma_start(A["spill_k"], km1[:]).then_inc(s_spill, 16)
                    pool.dma_start(A["spill_v"], vm1[:]).then_inc(s_spill, 16)
                work = ("post", "angles", "tables", "windows")
                todo = [s for s in slots if s.prev and s.prev[0] in ("y", "rope", "up")
                        or any(step in work for step, _ in s.react)]
                if not todo:
                    continue

                def body(i):
                    nonlocal ropes
                    for s in todo:
                        if s.prev[0] == "y" and not ends_product(s):
                            l, gain, c = s.prev[1]
                            squares(DT * (2 * l + (gain == 3)), i, c)
                        elif s.prev[0] == "up":
                            silu_over_rms(s.prev[1][0], s.prev[1][1](i))
                        elif s.prev[0] == "rope":
                            pool.wait_ge(evac_done, s.c(i))
                            rotate(ropes, ROPE_DEST[s.prev[1]])
                            ropes += 1
                        for step, a in s.react:
                            if step == "post":
                                scale_pairs(a)
                            elif step == "angles":
                                angles()
                            elif step == "tables":
                                tables()
                            elif step == "windows":
                                if a == 1:
                                    pool.wait_ge(evac_done, s.c(i))
                                windows(a)
                if rounds:
                    per = 2 * sum(s.prev[0] == "y" for s in todo)
                    with pool.Fori(0, rounds) as i, me.rounds(rounds, i, per):
                        body(i)
                else:
                    body(None)
            scale_pairs(3)


def kernel(x, mem, positions, norm_g, w_in_sb, w_in_nsa, cmp_pe, cmp_w1, cmp_w2, w_mem_kv, w_o,
           w_ffn_gate, w_ffn_up, ffn_conv_w, ffn_conv_b, w_ffn_down):
    import ml_dtypes
    import concourse.bacc as bacc
    from concourse.bass_utils import run_bass_kernel_spmd as run

    def tiles(w):
        k, n = w.shape
        return w.reshape(k // P, P, n // P, P).transpose(2, 1, 0, 3)

    def feature_major(a):
        return np.ascontiguousarray(np.asarray(a)[0].T.reshape(DT, P, T).transpose(1, 0, 2))

    consts = np.zeros((P, C_COLS), np.float32)
    consts[:, C_ONES:C_ONES + P] = 1
    consts[:, C_IDENT:C_IDENT + P] = np.eye(P)
    consts[:, C_NEGL:C_NEGL + P] = -np.tril(np.ones((P, P)))
    consts[:, C_NEGONES:C_NEGONES + P] = -1
    freq = (10000.0 ** (-np.arange(0, P, 2) / P)).astype(np.float32)
    consts[:, C_FREQ] = np.concatenate([freq, freq])
    consts[:, C_SIGN] = np.repeat([-1.0, 1.0], P // 2)
    consts[:, C_EPS] = EPS
    consts[:, C_HALFPI] = np.pi / 2
    masks = np.zeros((P, M_COLS), np.float32)
    masks[:, M_IDENT:M_IDENT + P] = np.eye(P)
    masks[:, M_STICK:M_STICK + P] = NEG * np.tril(np.ones((P, P)))
    masks[:, M_CAUSAL:M_CAUSAL + P] = NEG * np.triu(np.ones((P, P)), 1)
    end = np.arange(NC) * CMP_STRIDE + CMP_LEN - 1
    for t in range(2):
        masks[:, M_CMP + 16 * t:M_CMP + 16 * t + NC] = NEG * (end[None, :] > (t * P + np.arange(P))[:, None])

    w_in_sb, w_in_nsa, w_mem_kv, w_o = (np.asarray(a) for a in (w_in_sb, w_in_nsa, w_mem_kv, w_o))
    w_ffn_gate, w_ffn_up, w_ffn_down = (np.asarray(a) for a in (w_ffn_gate, w_ffn_up, w_ffn_down))
    cmp_w1, cmp_w2, cmp_pe = (np.asarray(a) for a in (cmp_w1, cmp_w2, cmp_pe))
    sb = tiles(w_in_sb[0])
    order = [3 * HEADS + g for g in range(MEM_HEADS)] + [j * HEADS + hd for hd in range(HEADS) for j in range(3)]
    arrays = {"in0": sb[order]}
    q_cols, kv_cols = HEADS * P, GROUPS * P
    nsa = w_in_nsa[0]
    parts = {n: nsa[:, q_cols + j * kv_cols:q_cols + (j + 1) * kv_cols]
             for j, n in enumerate(("kc", "vc", "ks", "vs", "kw", "vw"))}
    g0 = q_cols + 6 * kv_cols
    gates = np.concatenate([nsa[:, g0:g0 + 3 * HEADS], np.zeros((D, P - 3 * HEADS), np.float32)], 1)
    arrays["in1"] = tiles(np.concatenate(
        [parts[n] for n in ("vc", "vs", "vw", "kc", "ks", "kw")] + [gates, nsa[:, g0 + 3 * HEADS:], nsa[:, :q_cols]], 1))
    for l in range(2):
        m = tiles(w_mem_kv[l])
        arrays[f"mem{l}"] = m[[j * MEM_HEADS + g for g in range(MEM_HEADS) for j in range(2)]]
        arrays[f"out{l}"] = tiles(w_o[l])
        arrays[f"ffn{l}"] = np.stack([tiles(w_ffn_gate[l]), tiles(w_ffn_up[l])], 1).reshape(2 * FT, P, DT, P)
        arrays[f"down{l}"] = tiles(w_ffn_down[l])
    arrays["cmp"] = cmp_w1[0].reshape(4, CMP_LEN // 2, P, 2 * P).transpose(0, 2, 1, 3).reshape(4, P, CMP_LEN, P)
    arrays["cmp_w2"] = cmp_w2[0].reshape(2, 2, P, P).transpose(2, 0, 1, 3)
    arrays["cmp_pe"] = cmp_pe[0].transpose(2, 0, 1)
    arrays["gains"] = np.asarray(norm_g).reshape(2, 5, DT, P).transpose(3, 0, 1, 2)
    arrays["conv"] = np.concatenate([np.asarray(ffn_conv_w), np.asarray(ffn_conv_b)[:, None]], 1)\
        .reshape(2, 4, FT, P).transpose(3, 0, 2, 1)
    arrays["positions"] = np.broadcast_to(np.asarray(positions), (P, T))
    arrays["consts"] = consts
    arrays["masks"] = masks.astype(ml_dtypes.bfloat16)
    arrays["xT"], arrays["memT"] = feature_major(x), feature_major(mem)

    nc = bacc.Bacc("TRN2", target_bir_lowering=False, num_devices=1)
    arrays = {n: np.ascontiguousarray(a) for n, a in arrays.items()}
    A = {n: nc.dram_tensor("in_" + n, a.shape, mybir.dt.from_np(a.dtype), kind="ExternalInput").ap()
         for n, a in arrays.items()}
    A["spill_k"] = nc.dram_tensor("spill_k", (P, MEM_HEADS, T), F32, kind="Internal").ap()
    A["spill_v"] = nc.dram_tensor("spill_v", (P, 2, MEM_HEADS, P), F32, kind="Internal").ap()
    A["out"] = nc.dram_tensor("out", (P, DT, T), F32, kind="ExternalOutput").ap()
    build(nc, A)
    got = run(nc, [{"in_" + n: a for n, a in arrays.items()}], core_ids=[0]).results[0]["out"]
    return np.ascontiguousarray(got.transpose(2, 1, 0)).reshape(1, T, D)
```
